# Optimizing a Trainium2 kernel written in Bass

```python
import math
import jax, jax.numpy as jnp
from jax import lax
import numpy as np

D_MODEL = 1024
BATCH = 1
SEQ = 256
DEPTH = 1

GRID_W = 64
HEAD_DIM = 64
N_Q_HEADS = 8
N_KV_HEADS = 2
Q_PER_KV = N_Q_HEADS // N_KV_HEADS
ATTN_WIDTH = N_Q_HEADS * HEAD_DIM
KV_WIDTH = N_KV_HEADS * HEAD_DIM
ROPE_THETA = 10000.0
Q_BLOCK = 128
HYENA_WIDTH = D_MODEL // 2
HYENA_ORDER = 2
SHORT_CONV = 3
FILTER_EMB = 33
FILTER_HIDDEN = 64
FAST_DECAY_PCT = 0.3
SLOW_DECAY_PCT = 1.5
DECAY_TARGET = 1e-2
N_BRANCHES = 2
IN_COLS = 3 * HYENA_WIDTH + ATTN_WIDTH + 2 * KV_WIDTH + N_BRANCHES * D_MODEL
N_EXPERTS = 32
TOP_K = 4
D_FF = D_MODEL
SWIGLU_LIMIT = 7.0
SWIGLU_ALPHA = 1.702
MOE_BLOCK = 256
EPS = 1e-6

kernel_name = "hybrid_hyena_gqa_axialrope_moe_encoder"

def rmsnorm(x, g):
    xf = x.astype(jnp.float32)
    y = xf * lax.rsqrt(jnp.mean(xf * xf, axis=-1, keepdims=True) + EPS)
    return (y * g.astype(jnp.float32)).astype(x.dtype)

def short_conv(z, w, b):
    L = z.shape[1]
    pad = SHORT_CONV // 2
    zp = jnp.pad(z, ((0, 0), (pad, pad), (0, 0)))
    out = b
    for k in range(SHORT_CONV):
        out = out + zp[:, k:k + L] * w[k]
    return out

def hyena_filters(L, fw1, fb1, ff1, fw2, fb2, ff2, fw3, fb3):
    f32 = jnp.float32
    t = jnp.linspace(0.0, 1.0, L, dtype=f32)[:, None]
    bands = (FILTER_EMB - 1) // 2
    w = 2.0 * math.pi * jnp.arange(L, dtype=f32)[:, None] / L
    fr = jnp.linspace(1e-4, bands - 1, bands, dtype=f32)[None, :]
    feats = jnp.concatenate([t, jnp.cos(w * fr), -jnp.sin(w * fr)], axis=-1)
    h = jnp.sin(ff1.astype(f32) * (feats @ fw1.astype(f32) + fb1.astype(f32)))
    h = jnp.sin(ff2.astype(f32) * (h @ fw2.astype(f32) + fb2.astype(f32)))
    h = h @ fw3.astype(f32) + fb3.astype(f32)
    h = h.reshape(L, HYENA_ORDER, 2, HYENA_WIDTH)
    max_decay = math.log(DECAY_TARGET) / FAST_DECAY_PCT
    min_decay = math.log(DECAY_TARGET) / SLOW_DECAY_PCT
    deltas = jnp.abs(jnp.linspace(min_decay, max_decay, HYENA_WIDTH, dtype=f32))
    h = h * jnp.exp(-t[:, :, None, None] * deltas)
    fwd, bwd = h[:, :, 0], h[:, :, 1]
    kern = jnp.concatenate([fwd, jnp.zeros((1, HYENA_ORDER, HYENA_WIDTH), f32), bwd[1:][::-1]], axis=0)
    return kern / jnp.sum(jnp.abs(kern), axis=0, keepdims=True)

def hyena_mixer(z, conv_w, conv_b, fw1, fb1, ff1, fw2, fb2, ff2, fw3, fb3, hyena_d):
    L = z.shape[1]
    zc = short_conv(z, conv_w, conv_b)
    v, x1, x2 = jnp.split(zc, 3, axis=-1)
    kern = hyena_filters(L, fw1, fb1, ff1, fw2, fb2, ff2, fw3, fb3)
    K = jnp.fft.rfft(kern, axis=0)
    y = v.astype(jnp.float32)
    for o, gate in enumerate((x1, x2)):
        Y = jnp.fft.rfft(y, n=2 * L, axis=1)
        conv = jnp.fft.irfft(Y * K[None, :, o, :], n=2 * L, axis=1)[:, :L]
        y = gate.astype(jnp.float32) * (conv + y * hyena_d[o].astype(jnp.float32))
    return y.astype(z.dtype)

def axial_rope_tables(L):
    rows = L // GRID_W
    row = jnp.repeat(jnp.arange(rows, dtype=jnp.float32), GRID_W)
    col = jnp.tile(jnp.arange(GRID_W, dtype=jnp.float32), rows)
    half = HEAD_DIM // 2
    freqs = ROPE_THETA ** (-jnp.arange(0, half, 2, dtype=jnp.float32) / half)
    ang = jnp.concatenate([row[:, None] * freqs, col[:, None] * freqs], axis=-1)
    return jnp.cos(ang), jnp.sin(ang)

def apply_rope(x, cos, sin):
    xr = x.reshape(x.shape[:-1] + (HEAD_DIM // 2, 2))
    x0, x1 = xr[..., 0], xr[..., 1]
    c, s = cos[None, :, None, :], sin[None, :, None, :]
    return jnp.stack([x0 * c - x1 * s, x0 * s + x1 * c], axis=-1).reshape(x.shape)

def head_rmsnorm(x, g):
    xf = x.astype(jnp.float32)
    return xf * lax.rsqrt(jnp.mean(xf * xf, axis=-1, keepdims=True) + EPS) * g.astype(jnp.float32)

def attention_mixer(q, k, v, q_norm_g, k_norm_g):
    B, L, _ = q.shape
    q = head_rmsnorm(q.reshape(B, L, N_Q_HEADS, HEAD_DIM), q_norm_g)
    k = head_rmsnorm(k.reshape(B, L, N_KV_HEADS, HEAD_DIM), k_norm_g)
    v = v.reshape(B, L, N_KV_HEADS, HEAD_DIM).astype(jnp.float32)
    cos, sin = axial_rope_tables(L)
    q = apply_rope(q, cos, sin) * (HEAD_DIM ** -0.5)
    k = apply_rope(k, cos, sin)
    nb = L // Q_BLOCK
    qb = q.reshape(B, nb, Q_BLOCK, N_KV_HEADS, Q_PER_KV, HEAD_DIM).transpose(1, 0, 2, 3, 4, 5)

    def attend(q_blk):
        s = jnp.einsum('bqkgd,bskd->bkgqs', q_blk, k)
        p = jax.nn.softmax(s, axis=-1)
        return jnp.einsum('bkgqs,bskd->bqkgd', p, v)

    o = lax.map(attend, qb)
    o = o.transpose(1, 0, 2, 3, 4, 5).reshape(B, L, ATTN_WIDTH)
    return o

def clamped_swiglu(h):
    x_glu, x_lin = h[..., ::2], h[..., 1::2]
    x_glu = jnp.minimum(x_glu, SWIGLU_LIMIT)
    x_lin = jnp.clip(x_lin, -SWIGLU_LIMIT, SWIGLU_LIMIT)
    return x_glu * jax.nn.sigmoid(SWIGLU_ALPHA * x_glu) * (x_lin + 1.0)

def moe(h, router_w, router_b, w1, b1, w2, b2):
    B, L, D = h.shape
    T = B * L
    xt = h.reshape(T, D)
    logits = (xt @ router_w + router_b).astype(jnp.float32)
    top_val, top_idx = lax.top_k(logits, TOP_K)
    gates = jax.nn.softmax(top_val, axis=-1)
    TK = T * TOP_K
    e_flat = top_idx.reshape(TK)
    tok_flat = jnp.arange(TK, dtype=jnp.int32) // TOP_K
    g_flat = gates.reshape(TK)
    order = jnp.argsort(e_flat)
    e_s, tok_s, g_s = e_flat[order], tok_flat[order], g_flat[order]
    counts = jnp.bincount(e_flat, length=N_EXPERTS)
    starts = jnp.cumsum(counts) - counts
    padded = ((counts + MOE_BLOCK - 1) // MOE_BLOCK) * MOE_BLOCK
    pad_ends = jnp.cumsum(padded)
    pad_starts = pad_ends - padded
    dest = pad_starts[e_s] + jnp.arange(TK, dtype=jnp.int32) - starts[e_s]
    n_blocks = (TK + N_EXPERTS * (MOE_BLOCK - 1) + MOE_BLOCK - 1) // MOE_BLOCK
    P = n_blocks * MOE_BLOCK
    src = jnp.zeros((P,), jnp.int32).at[dest].set(tok_s)
    gpad = jnp.zeros((P,), jnp.float32).at[dest].set(g_s)
    block_start = jnp.arange(n_blocks, dtype=jnp.int32) * MOE_BLOCK
    block_expert = jnp.minimum(jnp.sum(block_start[:, None] >= pad_ends[None, :], axis=1),
                               N_EXPERTS - 1).astype(jnp.int32)
    xg = xt[src].reshape(n_blocks, MOE_BLOCK, D)

    def expert_block(args):
        xb, e = args
        hb = clamped_swiglu(xb @ w1[e] + b1[e])
        return hb @ w2[e] + b2[e]

    y = lax.map(expert_block, (xg, block_expert)).reshape(P, D)
    y = y.astype(jnp.float32) * gpad[:, None]
    out = jax.ops.segment_sum(y, src, num_segments=T)
    return out.reshape(B, L, D).astype(h.dtype)

def setup_inputs(seed: int = 0) -> dict:
    key = jax.random.key(seed)
    ks = jax.random.split(key, 32)
    f32 = jnp.float32

    def nrm(k, shape, scale):
        return jax.random.normal(k, shape, f32) * scale

    Dp = DEPTH
    return {
        "x": jax.random.normal(ks[0], (BATCH, SEQ, D_MODEL), f32),
        "norm1_g": 1.0 + nrm(ks[1], (Dp, D_MODEL), 0.02),
        "w_in": nrm(ks[2], (Dp, D_MODEL, IN_COLS), D_MODEL ** -0.5),
        "conv_w": nrm(ks[3], (Dp, SHORT_CONV, 3 * HYENA_WIDTH), SHORT_CONV ** -0.5),
        "conv_b": nrm(ks[4], (Dp, 3 * HYENA_WIDTH), 0.02),
        "filt_w1": nrm(ks[5], (Dp, FILTER_EMB, FILTER_HIDDEN), FILTER_EMB ** -0.5),
        "filt_b1": nrm(ks[6], (Dp, FILTER_HIDDEN), 0.1),
        "filt_freq1": 1.0 + nrm(ks[7], (Dp, FILTER_HIDDEN), 0.05),
        "filt_w2": nrm(ks[8], (Dp, FILTER_HIDDEN, FILTER_HIDDEN), FILTER_HIDDEN ** -0.5),
        "filt_b2": nrm(ks[9], (Dp, FILTER_HIDDEN), 0.1),
        "filt_freq2": 1.0 + nrm(ks[10], (Dp, FILTER_HIDDEN), 0.05),
        "filt_w3": nrm(ks[11], (Dp, FILTER_HIDDEN, HYENA_ORDER * 2 * HYENA_WIDTH), FILTER_HIDDEN ** -0.5),
        "filt_b3": nrm(ks[12], (Dp, HYENA_ORDER * 2 * HYENA_WIDTH), 0.02),
        "hyena_d": nrm(ks[13], (Dp, HYENA_ORDER, HYENA_WIDTH), 0.5),
        "q_norm_g": 1.0 + nrm(ks[14], (Dp, HEAD_DIM), 0.02),
        "k_norm_g": 1.0 + nrm(ks[15], (Dp, HEAD_DIM), 0.02),
        "w_hyena_up": nrm(ks[16], (Dp, HYENA_WIDTH, D_MODEL), HYENA_WIDTH ** -0.5),
        "w_attn_up": nrm(ks[17], (Dp, ATTN_WIDTH, D_MODEL), ATTN_WIDTH ** -0.5),
        "w_out": nrm(ks[18], (Dp, D_MODEL, D_MODEL), D_MODEL ** -0.5),
        "norm2_g": 1.0 + nrm(ks[19], (Dp, D_MODEL), 0.02),
        "router_w": nrm(ks[20], (Dp, D_MODEL, N_EXPERTS), D_MODEL ** -0.5),
        "router_b": nrm(ks[21], (Dp, N_EXPERTS), 0.01),
        "expert_w1": nrm(ks[22], (Dp, N_EXPERTS, D_MODEL, 2 * D_FF), D_MODEL ** -0.5),
        "expert_b1": nrm(ks[23], (Dp, N_EXPERTS, 2 * D_FF), 0.02),
        "expert_w2": nrm(ks[24], (Dp, N_EXPERTS, D_FF, D_MODEL), D_FF ** -0.5),
        "expert_b2": nrm(ks[25], (Dp, N_EXPERTS, D_MODEL), 0.02),
    }

def reference(x, norm1_g, w_in, conv_w, conv_b, filt_w1, filt_b1, filt_freq1, filt_w2, filt_b2,
              filt_freq2, filt_w3, filt_b3, hyena_d, q_norm_g, k_norm_g, w_hyena_up, w_attn_up,
              w_out, norm2_g, router_w, router_b, expert_w1, expert_b1, expert_w2, expert_b2):
    o_q = 3 * HYENA_WIDTH
    o_k = o_q + ATTN_WIDTH
    o_v = o_k + KV_WIDTH
    o_g = o_v + KV_WIDTH
    for layer in range(DEPTH):
        u = rmsnorm(x, norm1_g[layer])
        proj = u @ w_in[layer]
        y_hy = hyena_mixer(proj[..., :o_q], conv_w[layer], conv_b[layer],
                           filt_w1[layer], filt_b1[layer], filt_freq1[layer],
                           filt_w2[layer], filt_b2[layer], filt_freq2[layer],
                           filt_w3[layer], filt_b3[layer], hyena_d[layer])
        y_at = attention_mixer(proj[..., o_q:o_k], proj[..., o_k:o_v], proj[..., o_v:o_g],
                               q_norm_g[layer], k_norm_g[layer]).astype(x.dtype)
        g_hy = jax.nn.sigmoid(proj[..., o_g:o_g + D_MODEL])
        g_at = jax.nn.sigmoid(proj[..., o_g + D_MODEL:])
        merged = g_hy * (y_hy @ w_hyena_up[layer]) + g_at * (y_at @ w_attn_up[layer])
        x = x + merged @ w_out[layer]
        hn = rmsnorm(x, norm2_g[layer])
        x = x + moe(hn, router_w[layer], router_b[layer], expert_w1[layer], expert_b1[layer],
                    expert_w2[layer], expert_b2[layer])
    return x


_drawn_inputs = setup_inputs


def setup_inputs(seed=0):
    import zlib

    import numpy as np

    out = dict(_drawn_inputs(seed))
    spreads = {}
    factors = {'conv_b': 3.158,
     'filt_freq1': 3.629,
     'filt_freq2': 12.937,
     'filt_b3': 13.785,
     'q_norm_g': 4.266,
     'k_norm_g': 4.262,
     'expert_b1': 5.161,
     'expert_b2': 5.931}
    for name, (base, spread) in spreads.items():
        noise = np.random.default_rng([zlib.crc32(name.encode()), seed]).standard_normal(out[name].shape)
        drawn = base * np.exp(spread * noise) if base else spread * noise
        out[name] = __import__('jax').numpy.asarray(drawn.astype(out[name].dtype))
    for name, factor in factors.items():
        out[name] = (out[name] * factor).astype(out[name].dtype)
    return out
```

```python
from contextlib import ExitStack

import numpy as np

import concourse.bass as bass
from concourse import mybir
from concourse.alu_op_type import AluOpType as ALU

ACT = mybir.ActivationFunctionType
AX = mybir.AxisListType
F32 = mybir.dt.float32
BF16 = mybir.dt.bfloat16
I32 = mybir.dt.int32
U32 = mybir.dt.uint32
ds = bass.ds

P = 128
T = 256
TT = T // P
D = 1024
KD = D // P
HW = 512
NH, NKV, HD = 8, 2, 64
QPK = NH // NKV
NE, TOPK = 32, 4
FF = 1024
EPS = 1e-6
LIMIT, ALPHA = 7.0, 1.702
FEMB, FHID = 33, 64
NDFT = 2 * T - 1
SLOTS = 64
SLOT = 2048
NSLOT = 16
CHUNKS = 12
GROUP = 4
TURNS = NE // GROUP
NLIST = 32
NWIN = T // SLOTS
PI = 3.14159274
PI_IN = 3.1415925
PI2_A, PI2_B, PI2_C = 6.28125, 1.9340515136718750e-03, 1.2556659146e-06

C_ID, C_TRI, C_IOTA, C_WK = 0, 128, 256, 512
C_COS, C_SIN, C_IOL, C_E, C_BASE, C_ID3, C_ONE, C_IOE = 514, 578, 642, 674, 675, 676, 708, 836
C_COLS = 868


def tables():
    c = np.zeros((P, C_COLS), np.float32)
    c[:, C_ID:C_ID + P] = np.eye(P)
    c[:, C_TRI:C_TRI + P] = np.triu(np.ones((P, P)), 1)
    c[:, C_IOTA:C_IOTA + T] = np.arange(T)
    bins = np.full(T, 2.0 / NDFT)
    bins[0] = 1.0 / NDFT
    c[:, C_WK:C_WK + 2] = bins.reshape(2, P).T
    half = HD // 2
    freqs = np.float32(10000.0) ** (-np.arange(0, half, 2, dtype=np.float32) / half)
    row = np.repeat(np.arange(T // 64, dtype=np.float32), 64)
    col = np.tile(np.arange(64, dtype=np.float32), T // 64)
    ang = np.concatenate([row[:, None] * freqs, col[:, None] * freqs], -1).astype(np.float32)
    c[:, C_COS:C_COS + 64] = np.cos(ang).reshape(2, P, 32).transpose(1, 0, 2).reshape(P, 64)
    c[:, C_SIN:C_SIN + 64] = np.sin(ang).reshape(2, P, 32).transpose(1, 0, 2).reshape(P, 64)
    c[:, C_IOL:C_IOL + NLIST] = np.arange(NLIST)
    j = np.arange((NWIN - 1) * NE)
    c[:j.size, C_E] = j % NE
    c[:j.size, C_BASE] = SLOTS * (1 + j // NE)
    c[:96, C_ID3:C_ID3 + 32] = np.tile(np.eye(32), (3, 1))
    c[:, C_ONE:C_ONE + P] = 1.0
    c[:, C_IOE:C_IOE + NE] = np.arange(NE)
    n = np.arange(T)
    w = 2 * np.pi * (np.outer(n, n) % NDFT) / NDFT
    dft = np.stack([np.cos(w), np.sin(w)]).astype(np.float32)
    dft = np.ascontiguousarray(dft.reshape(2, 2, P, T).transpose(2, 0, 1, 3)).reshape(P, 4 * T)
    f32 = np.float32
    t = np.linspace(0.0, 1.0, T, dtype=f32)[:, None]
    bands = (FEMB - 1) // 2
    wt = (f32(2.0 * np.pi) * np.arange(T, dtype=f32)[:, None] / f32(T)).astype(f32)
    fr = np.linspace(1e-4, bands - 1, bands, dtype=f32)[None, :]
    a = (wt * fr).astype(f32)
    feats = np.concatenate([t, np.cos(a), -np.sin(a)], -1).astype(f32)
    lo, hi = np.log(1e-2) / 1.5, np.log(1e-2) / 0.3
    deltas = np.abs(np.linspace(lo, hi, HW, dtype=f32))
    decay = np.exp(-t * deltas).astype(f32)
    decay = np.ascontiguousarray(decay.reshape(2, P, HW).transpose(1, 0, 2)).reshape(P, 2 * HW)
    return c, dft, np.ascontiguousarray(feats.T), decay


GROUPS = (
    ["vec", "f1"] + [f"uT{i}" for i in range(4)] + ["f2"]
    + [f"z{i}" for i in range(4)]
    + [f"h{t}{c}" for t in range(2) for c in range(4)]
    + ["q0", "q1", "kv0", "kv1"]
    + ["nrm0", "nrm1"] + [f"kf{o}{r}{k}" for o in range(2) for k in range(2) for r in range(2)]
    + [f"z{i}" for i in range(4, 8)]
    + ["tv0", "tv1"] + [f"fa{r}{k}" for k in range(2) for r in range(2)]
    + ["tx0", "tx1", "tq0", "tq1", "tk"]
    + [f"z{i}" for i in range(8, 12)]
    + ["ia0", "ia1"] + [f"sc{t}{j}" for t in range(2) for j in range(4)]
    + [f"gh{i}" for i in range(4)]
    + [f"fb{r}{k}" for k in range(2) for r in range(2)]
    + ["pt00", "pt01", "pt10", "pt11", "pv0", "pt20", "pt21", "pv1", "pt30", "pt31", "pv2", "pv3"]
    + [f"ga{i}" for i in range(4)]
    + [f"ib{i}" for i in range(4)]
    + [f"uh{i}" for i in range(4)] + [f"ua{i}" for i in range(4)]
    + ["wo00", "wo01", "wo10", "wo11"]
    + [f"th{i}" for i in range(4)] + ["lg", "lt", "rk", "lp", "ls", "gt"]
)
BANK = {g: n % 8 for n, g in enumerate(GROUPS)}
NTH = {g: n // 8 + 1 for n, g in enumerate(GROUPS)}

LOADS = ["v", "q", "kv", "x1", "x2", "gh0", "gh1", "ga0", "ga1", "hu", "au", "wo0", "wo1"]
LAST_USE = ["z3", "q1", "kv1", "z7", "z11", "gh1", "gh3", "ga1", "ga3", "uh3", "ua3", "wo11", "wo11"]
PAIR_SLOT = [14, 10, 12]


def hybrid_block(nc, x, norm1_g, w_in, conv_w, conv_b, filt_w1, filt_b1, filt_freq1, filt_w2,
                 filt_b2, filt_freq2, filt_w3, filt_b3, hyena_d, q_norm_g, k_norm_g, w_hyena_up,
                 w_attn_up, w_out, norm2_g, router_w, router_b, expert_w1, expert_b1, expert_w2,
                 expert_b2, c_tab, c_dft, c_feats, c_decay, out):
    with ExitStack() as ctx:
        def sb(name, shape, dt=F32):
            return ctx.enter_context(nc.sbuf_tensor(name, shape, dt))

        def sem(name):
            return ctx.enter_context(nc.semaphore(name))

        ps = ctx.enter_context(nc.psum_tensor("ps", [P, 8, 512], F32))

        ring = sb("ring", [P, NSLOT * SLOT])
        shared = sb("shared", [P, 14336])
        xh = sb("xh", [P, TT, D])
        tab = sb("tab", [P, C_COLS])
        dft = sb("dft", [P, 4 * T])
        b1p = sb("b1p", [P, 2 * FF], BF16)
        selB = sb("selB", [P, 2, SLOTS], BF16)
        sel = sb("sel", [P, TT, 2 * SLOTS], BF16)
        gate = sb("gate", [P, TT, NE])
        rankm = sb("rankm", [P, TT, NE + 4])
        logit = sb("logit", [P, TT, NE])
        stat = sb("stat", [P, 64])
        smax = sb("smax", [P, 56])
        mark = sb("mark", [P, 8])
        top8 = sb("top8", [P, TT, 8])
        idx8 = sb("idx8", [P, TT, 8], U32)
        idxf = sb("idxf", [P, TT, 8])
        olist = sb("olist", [1, 2 * NLIST + 8], I32)

        def ringw(slot, off, n, parts=P):
            return ring[0:parts, slot * SLOT + off:slot * SLOT + off + n]

        def sh(off, n, parts=P):
            return shared[0:parts, off:off + n]

        ident = tab[:, C_ID:C_ID + P]
        tri = tab[:, C_TRI:C_TRI + P]
        ones = tab[:, C_ONE:C_ONE + P]
        wk = [tab[:, C_WK + k:C_WK + k + 1] for k in range(2)]
        cs = [tab[:, C_COS + 32 * t:C_COS + 32 * t + 32] for t in range(2)]
        sn = [tab[:, C_SIN + 32 * t:C_SIN + 32 * t + 32] for t in range(2)]
        basis = [[dft[:, (2 * r + t) * T:(2 * r + t + 1) * T] for t in range(2)] for r in range(2)]

        decay = ringw(0, 0, 1024).rearrange("p (t n) -> p t n", t=2)
        dbc = ringw(0, 1024, 1024).rearrange("p (o n) -> p o n", o=2)
        fw3 = ringw(1, 0, 2048, FHID + 1)
        qz = ringw(1, 0, 2048).rearrange("p (h t) -> p h t", h=NH)
        zz = [ringw(2, 256 * i, 256) for i in range(8)] + [sh(12288 + 256 * i, 256) for i in range(4)]
        vT = ringw(3, 0, 1024).rearrange("p (t n) -> p t n", t=2)
        x1T = ringw(3, 1024, 1024).rearrange("p (t n) -> p t n", t=2)
        hk = ring[:, 4 * SLOT:6 * SLOT].rearrange("p (t o d n) -> p t o d n", t=2, o=2, d=2)
        probs = ring[:, 4 * SLOT:6 * SLOT].rearrange("p (t h s) -> p t h s", t=2, h=NH)
        g1b = ringw(4, 0, 1024)
        b1raw = ringw(3, 0, 2048, 96)
        b1mid = shared[0:96, 13312:14336].bitcast(BF16)
        u = ringw(6, 0, 2048).rearrange("p (t n) -> p t n", t=2)
        spec = ringw(6, 0, 2048).rearrange("p (r k n) -> p r k n", r=2, k=2)
        m7 = 7 * SLOT
        feats = ring[0:FEMB, m7:m7 + 256]
        h1 = ring[0:FHID, m7 + 256:m7 + 512]
        h2e = ring[0:FHID + 1, m7 + 512:m7 + 768]
        rope = ring[:, m7 + 768:m7 + 1280].rearrange("p (t a i) -> p t a i", t=2, a=8)
        kT = ring[:, m7 + 1280:m7 + 1536]
        vtok = ring[:, m7 + 1536:m7 + 1792].rearrange("p (t n) -> p t n", t=2)
        rows = ring[0:48, m7 + 1792:m7 + 1920]
        fvec = ring[0:FHID, m7 + 1968:m7 + 1972]
        vecT = ring[:, m7 + 1920:m7 + 1968]
        m8_ = 8 * SLOT
        qn = [ring[:, m8_ + 640 * t:m8_ + 640 * t + 640].rearrange("p (h c) -> p h c", c=HD) for t in range(2)]
        mm4 = [ring[:, m8_ + 1280 + 256 * i:m8_ + 1536 + 256 * i].rearrange("p (h i) -> p h i", i=32) for i in range(4)]
        qr = [ring[:, m8_ + 2304 + 512 * t:m8_ + 2816 + 512 * t] for t in range(2)]
        kr = [ring[:, m8_ + 3328 + 128 * t:m8_ + 3456 + 128 * t] for t in range(2)]
        ptb = [ring[:, m8_ + 512 * i:m8_ + 512 * i + 512].rearrange("p (s t) -> p s t", s=2) for i in range(4)]
        fw1 = ring[0:FEMB, m8_ + 3584:m8_ + 3584 + 64]
        fw2 = ring[0:FHID, m8_ + 3648:m8_ + 3648 + 64]
        qkg = ring[:, m8_ + 3712:m8_ + 3840]
        farg = ring[0:FHID, m8_ + 3840:m8_ + 4096]
        kf = sh(0, 4096).rearrange("p (o r k n) -> p o r k n", o=2, r=2, k=2)
        ghy = sh(4096, 2048).rearrange("p (m t) -> p m t", m=8)
        gat = sh(6144, 2048).rearrange("p (m t) -> p m t", m=8)
        mT = sh(8192, 2048).rearrange("p (m t) -> p m t", m=8)
        uT = sh(10240, 2048).rearrange("p (k t) -> p k t", k=8)
        x2z = zz[8:12]
        yat = sh(13312, 1024).rearrange("p (j t) -> p j t", j=4)
        sq = [sh(4096 + 640 * t, 640) for t in range(2)]
        fsum = sh(8192, 2048).rearrange("p (t o n) -> p t o n", t=2, o=2)
        absf = sh(0, 4096).rearrange("p (t o d n) -> p t o d n", t=2, o=2, d=2)
        habs = sh(6144, 1024).rearrange("p (o n) -> p o n", o=2)
        rinv = sh(7168, 1024).rearrange("p (o n) -> p o n", o=2)
        prod = sh(8192, 2048).rearrange("p (i n) -> p i n", i=4)
        frnd = sh(12288, 256, FHID)
        parts = shared[:, 0:3072].bitcast(BF16).rearrange("p (a t n) -> p a t n", a=3, t=2)
        b2pad = sh(3072, 1024)
        hn = sh(4096, 2048).rearrange("p (t n) -> p t n", t=2)
        hnT = sh(6144, 2048).rearrange("p (k t) -> p k t", k=8)
        glu = sh(6144, 512).rearrange("p (b n) -> p b n", b=2)
        lin = sh(6656, 512).rearrange("p (b n) -> p b n", b=2)
        sig = sh(7168, 512).rearrange("p (b n) -> p b n", b=2)
        hact = sh(7680, 512).rearrange("p (b n) -> p b n", b=2)
        xg = sh(8192, 2048).rearrange("p (b k s) -> p b k s", b=2, k=8)
        resid = sh(10240, 1024)
        yab = sh(10240, 1024).rearrange("p (w n) -> p w n", w=2)
        g2b = sh(11264, 1024)
        hT = sh(12288, 512).rearrange("p (f s) -> p f s", f=4)
        selG = sh(12800, 2 * 3 * SLOTS).rearrange("p (t s) -> p t s", t=2)
        gT = sh(13312, 512).rearrange("p (w t) -> p w t", w=4)
        gateT = dft[:, 0:256]
        rw = dft[:, 256:512].rearrange("p (k e) -> p k e", k=8)
        lgT = dft[0:NE, 512:768]
        mask3 = dft[:, 768:960].rearrange("p (t e) -> p t e", t=2)
        over = dft[:, 960:961]
        pos = dft[:, 961:962]
        onehot = dft[:, 962:962 + NLIST]
        rbias = dft[0:NE, 995:996]

        filled = [sem(f"bank_filled{b}") for b in range(8)]
        drained = [sem(f"bank_drained{b}") for b in range(8)]
        in_x = sem("in_x")
        in_tab = sem("in_tab")
        in_name = {n: sem("in_" + n) for n in
                   ("g1b", "rows", "feats", "fw1", "fw2", "fw3", "b3", "fvec", "decay", "dft", "dbc", "qkg", "b1", "rw", "rb", "g2b", "b2")}
        in_pair = [sem(f"in_pair{i}") for i in range(3)]
        dve_step = sem("dve_step")
        pool_step = sem("pool_step")
        x_ss = sem("x_sumsq")
        x_std = sem("x_std")
        x_var = sem("x_var")
        u_ready = sem("u_ready")
        f_arg = sem("filter_arg")
        f_out = sem("filter_sin")
        z_scaled = sem("z_scaled")
        abs_ready = sem("abs_ready")
        habs_ready = sem("habs_ready")
        hk_ready = sem("hk_ready")
        pm_ready = sem("filter_sums_ready")
        qk_sq = sem("qk_squared")
        qk_var = sem("qk_var")
        qk_std = sem("qk_std")
        qk_ready = sem("qk_rotated")
        qz_zero = sem("qz_zeroed")
        spec_ready = sem("spec_ready")
        mx_ready = sem("max_ready")
        p_exp = sem("probs_exp")
        p_ready = sem("probs_ready")
        b1_ready = sem("b1_parts_ready")
        h_ss = sem("h_sumsq")
        h_ready = sem("h_ready")
        h_var = sem("h_var")
        h_std = sem("h_std")
        hn_ready = sem("hn_ready")
        hi_ready, mid16_ready, lo_ready = sem("hi_ready"), sem("mid16_ready"), sem("lo_ready")
        res_ready = sem("residue_ready")
        r_exp = sem("router_exp")
        r_max = sem("router_max")
        gate_ready = sem("gate_ready")
        mask_ready = sem("mask_ready")
        rank_ready = sem("rank_ready")
        over_ready = sem("over_ready")
        pos_ready = sem("onehot_ready")
        list_ready = sem("list_ready")
        pads_ready = sem("pads_ready")
        ld = [sem(f"slot_loaded{s}") for s in range(NSLOT)]
        chunk_used = sem("chunk_used")
        t_full, t_free = sem("turn_full"), sem("turn_free")
        h_full, h_used = sem("hidden_full"), sem("hidden_used")
        y_full, y_used = sem("y_full"), sem("y_used")
        comb = sem("combined")
        selb_ready, sel_ready, selg_ready = sem("bias_select"), sem("gather_select"), sem("combine_select")
        glu_ready, sig_ready, lin_ready, mid_ready, hact_ready = (
            sem("glu_ready"), sem("sig_ready"), sem("lin_ready"), sem("glulin_ready"), sem("hact_ready"))
        out_ready, out_stored = sem("out_ready"), sem("out_stored")

        def wait_filled(eng, g):
            eng.wait_ge(filled[BANK[g]], NTH[g])

        def wait_drained(eng, g):
            eng.wait_ge(drained[BANK[g]], NTH[g])

        def drains(ins, g):
            ins.then_inc(drained[BANK[g]], 1)

        def pair_of(n):
            s = PAIR_SLOT[n % 3]
            return ring[:, s * SLOT:(s + 2) * SLOT], 16 * (n // 3 + 1)

        def chunk_src(e, part):
            if part < 8:
                src = expert_w1[0, ds(e, 1), P * part:P * part + P, :]
                return src.rearrange("o p n -> (o p) n")
            m = part - 8
            src = expert_w2[0, ds(e, 1), 2 * P * m:2 * P * (m + 1), :]
            return src.rearrange("o (k p) n -> p (o k) n", k=2)

        def slot_dst(slot, part):
            dst = ring[:, slot * SLOT:(slot + 1) * SLOT]
            return dst if part < 8 else dst.rearrange("p (k n) -> p k n", k=2)

        NCH = NE * CHUNKS
        block = ctx.enter_context(nc.Block())

        @block.sync
        def _(sp):
            sp.dma_start(xh[:], x[0].rearrange("(t p) d -> p t d", p=P)).then_inc(in_x, 16)
            sp.dma_start(g1b, norm1_g.partition_broadcast(P)).then_inc(in_name["g1b"], 16)
            cols = {"v": 0, "x1": HW, "x2": 2 * HW, "q": 3 * HW}
            c_kv = 3 * HW + NH * HD
            c_g = c_kv + 2 * NKV * HD
            for i in range(2):
                cols[f"gh{i}"] = c_g + 512 * i
                cols[f"ga{i}"] = c_g + D + 512 * i

            def load_pair(n):
                name = LOADS[n]
                dst, _ = pair_of(n)
                if n >= 3:
                    wait_filled(sp, LAST_USE[n - 3])
                done = in_pair[n % 3]
                if name == "kv":
                    sp.dma_start(dst[:, 0:2048].rearrange("p (k n) -> p k n", k=8),
                                 w_in[0, :, c_kv:c_kv + 256].rearrange("(k p) n -> p k n", p=P)).then_inc(done, 16)
                elif name in cols:
                    c = cols[name]
                    sp.dma_start(dst.rearrange("p (k n) -> p k n", k=8),
                                 w_in[0, :, c:c + 512].rearrange("(k p) n -> p k n", p=P)).then_inc(done, 16)
                elif name == "hu":
                    sp.dma_start(dst.rearrange("p (k n) -> p k n", k=4),
                                 w_hyena_up[0].rearrange("(k p) n -> p k n", p=P)).then_inc(done, 16)
                elif name == "au":
                    for g in range(NKV):
                        sp.dma_start(dst[HD * g:HD * g + HD, :].rearrange("p (j n) -> p j n", j=QPK),
                                     w_attn_up[0, g * QPK * HD:(g + 1) * QPK * HD, :]
                                     .rearrange("(j c) n -> c j n", c=HD)).then_inc(done, 16)
                else:
                    h = int(name[2])
                    sp.dma_start(dst.rearrange("p (k n) -> p k n", k=4),
                                 w_out[0, 512 * h:512 * h + 512, :].rearrange("(k p) n -> p k n", p=P)).then_inc(done, 16)

            def first(c):
                sp.dma_start(slot_dst(c, c % CHUNKS), chunk_src(c // CHUNKS, c % CHUNKS)).then_inc(ld[c], 16)

            def wait_used(e, before, part):
                if part == 7:
                    sp.wait_ge(h_full, e + 1)
                elif part == 11:
                    sp.wait_ge(y_full, e + 1)
                else:
                    sp.wait_ge(chunk_used, before + (part + 1 if part < 7 else part))

            for n in range(8):
                load_pair(n)
            wait_drained(sp, "z11")
            wait_drained(sp, "ia1")
            wait_filled(sp, "sc13")
            for c in (0, 1, 2):
                first(c)
            load_pair(8)
            wait_filled(sp, "fb11")
            first(3)
            load_pair(9)
            wait_filled(sp, "pv3")
            for c in (4, 5, 7, 8, 9):
                first(c)
            load_pair(10)
            wait_filled(sp, "ib3")
            first(6)
            sp.dma_start(rw, router_w[0].rearrange("(k p) e -> p k e", p=P)).then_inc(in_name["rw"], 16)
            sp.dma_start(rbias, router_b[0].unsqueeze(1)).then_inc(in_name["rb"], 16)
            sp.wait_ge(pads_ready, 2)
            sp.dma_start(b2pad[0:NE, :], expert_b2[0]).then_inc(in_name["b2"], 16)
            sp.dma_start(g2b, norm2_g.partition_broadcast(P)).then_inc(in_name["g2b"], 16)
            load_pair(11)
            load_pair(12)
            for c in (10, 11):
                wait_filled(sp, LAST_USE[10])
                first(c)
            for c in (12, 13, 14, 15):
                wait_filled(sp, "wo11")
                first(c)
            with sp.Fori(0, TURNS - 1) as it:
                for c in range(GROUP * CHUNKS):
                    n = c + NSLOT
                    wait_used(it * GROUP + c // CHUNKS, it * (GROUP * 10) + 10 * (c // CHUNKS), c % CHUNKS)
                    sp.dma_start(slot_dst(n % NSLOT, n % CHUNKS),
                                 chunk_src(it * GROUP + n // CHUNKS, n % CHUNKS)).then_inc(ld[n % NSLOT], 16)
            for n in range((TURNS - 1) * GROUP * CHUNKS + NSLOT, NCH):
                e, part = divmod(n - NSLOT, CHUNKS)
                wait_used(e, 10 * e, part)
                sp.dma_start(slot_dst(n % NSLOT, n % CHUNKS), chunk_src(n // CHUNKS, n % CHUNKS)).then_inc(ld[n % NSLOT], 16)
            sp.wait_ge(list_ready, 1)
            n_over = sp.value_load(olist[0:1, 2 * NLIST:2 * NLIST + 1], min_val=0, max_val=NLIST)
            with sp.If(n_over > 0):
                with sp.Fori(0, n_over) as i:
                    e = sp.value_load(olist[0:1, ds(i, 1)], min_val=0, max_val=NE - 1)
                    sp.wait_ge(y_full, i + NE)
                    for c in range(CHUNKS):
                        sp.dma_start(slot_dst(c, c), chunk_src(e, c)).then_inc(ld[c], 16)
            for t in range(TT):
                sp.wait_ge(out_ready, 2 * t + 2)
                sp.dma_start(out[0, P * t:P * t + P, :], xh[:, t, :]).then_inc(out_stored, 16)
            sp.wait_ge(out_stored, 16 * TT)

        @block.tensor
        def _(pe):
            def begin(g):
                if NTH[g] > 1:
                    pe.wait_ge(drained[BANK[g]], NTH[g] - 1)
                return ps[:, BANK[g], :]

            def end(mm, g):
                mm.then_inc(filled[BANK[g]], 1)

            def pair(name, k):
                n = LOADS.index(name)
                words, count = pair_of(n)
                extra = 16 if (n % 3 == 1 and n >= 10) else 0
                pe.wait_ge(in_pair[n % 3], count + extra)
                return words.rearrange("p (k n) -> p k n", k=k)

            pe.wait_ge(in_tab, 16)
            pe.wait_ge(in_name["rows"], 32)
            bk = begin("vec")
            end(pe.transpose(bk[:, 0:48], rows, ident[0:48, 0:48]), "vec")
            pe.wait_ge(in_name["feats"], 16)
            pe.wait_ge(in_name["fw1"], 16)
            bk = begin("f1")
            end(pe.matmul(bk[0:FHID, 0:T], fw1, feats, start=True, stop=True), "f1")
            pe.wait_ge(u_ready, 2)
            for i in range(4):
                bk = begin(f"uT{i}")
                for k in range(2):
                    for t in range(2):
                        mm = pe.transpose(bk[:, (2 * k + t) * P:(2 * k + t + 1) * P],
                                          u[:, t, (2 * i + k) * P:(2 * i + k + 1) * P], ident)
                end(mm, f"uT{i}")
            pe.wait_ge(in_name["fw2"], 16)
            pe.wait_ge(f_out, 1)
            bk = begin("f2")
            end(pe.matmul(bk[0:FHID, 0:T], fw2, h1, start=True, stop=True), "f2")

            def project_cols(load, tiles, groups, per_bank):
                w = pair(load, 8)
                for i in range(0, tiles, per_bank):
                    g = groups[i // per_bank]
                    bk = begin(g)
                    for s in range(per_bank):
                        for k in range(KD):
                            mm = pe.matmul(bk[:, s * T:(s + 1) * T], w[:, k, (i + s) * P:(i + s + 1) * P],
                                           uT[:, k, :], start=(k == 0), stop=(k == KD - 1))
                    end(mm, g)

            for i in range(4):
                wait_drained(pe, f"uT{i}")
            project_cols("v", 4, [f"z{i}" for i in range(4)], 1)

            pe.wait_ge(f_out, 2)
            pe.wait_ge(pads_ready, 1)
            pe.wait_ge(in_name["fw3"], 16)
            pe.wait_ge(in_name["b3"], 16)
            for t in range(2):
                for c in range(4):
                    g = f"h{t}{c}"
                    bk = begin(g)
                    end(pe.matmul(bk, h2e[:, t * P:(t + 1) * P], fw3[:, c * HW:(c + 1) * HW],
                                  start=True, stop=True), g)
            w = pair("q", 8)
            for t in range(2):
                bk = begin(f"q{t}")
                for k in range(KD):
                    mm = pe.matmul(bk, uT[:, k, t * P:(t + 1) * P], w[:, k, :], start=(k == 0), stop=(k == KD - 1))
                end(mm, f"q{t}")
            n = LOADS.index("kv")
            pe.wait_ge(in_pair[n % 3], pair_of(n)[1])
            w = pair_of(n)[0][:, 0:2048].rearrange("p (k n) -> p k n", k=8)
            for t in range(2):
                bk = begin(f"kv{t}")
                for k in range(KD):
                    mm = pe.matmul(bk[:, 0:256], uT[:, k, t * P:(t + 1) * P], w[:, k, :], start=(k == 0), stop=(k == KD - 1))
                end(mm, f"kv{t}")
            pe.wait_ge(habs_ready, 1)
            for o in range(2):
                bk = begin(f"nrm{o}")
                end(pe.matmul(bk, ones, habs[:, o, :], start=True, stop=True), f"nrm{o}")
            pe.wait_ge(pm_ready, 8)
            pe.wait_ge(in_name["dft"], 16)
            for o in range(2):
                for k in range(2):
                    for r in range(2):
                        g = f"kf{o}{r}{k}"
                        bk = begin(g)
                        for t in range(2):
                            src = fsum[:, t, o, :] if r == 0 else hk[:, t, o, 1, :]
                            mm = pe.matmul(bk, basis[r][t][:, k * P:(k + 1) * P], src, start=(t == 0), stop=(t == 1))
                        end(mm, g)
            project_cols("x1", 4, [f"z{i}" for i in range(4, 8)], 1)

            def turn_z(groups, first):
                for i in range(4):
                    wait_drained(pe, f"z{first + i}")
                for t in range(2):
                    bk = begin(groups[t])
                    for i in range(4):
                        mm = pe.transpose(bk[:, i * P:(i + 1) * P], zz[first + i][:, t * P:(t + 1) * P], ident)
                    end(mm, groups[t])

            def forward(prefix, y):
                for k in range(2):
                    for r in range(2):
                        g = f"{prefix}{r}{k}"
                        bk = begin(g)
                        for t in range(2):
                            mm = pe.matmul(bk, basis[r][t][:, k * P:(k + 1) * P], y[:, t, :], start=(t == 0), stop=(t == 1))
                        end(mm, g)

            turn_z(["tv0", "tv1"], 0)
            wait_drained(pe, "tv0")
            wait_drained(pe, "tv1")
            forward("fa", vT)
            turn_z(["tx0", "tx1"], 4)
            pe.wait_ge(qk_ready, 4)
            for t in range(2):
                bk = begin(f"tq{t}")
                for j in range(4):
                    mm = pe.transpose(bk[:, j * P:(j + 1) * P], qr[t][:, j * P:(j + 1) * P], ident)
                end(mm, f"tq{t}")
            bk = begin("tk")
            for t in range(2):
                mm = pe.transpose(bk[:, t * P:(t + 1) * P], kr[t], ident)
            end(mm, "tk")
            project_cols("x2", 4, [f"z{i}" for i in range(8, 12)], 1)
            pe.wait_ge(spec_ready, 4)
            for t in range(2):
                bk = begin(f"ia{t}")
                for n, (r, k) in enumerate([(r, k) for k in range(2) for r in range(2)]):
                    mm = pe.matmul(bk, basis[r][k][:, t * P:(t + 1) * P], spec[:, r, k, :], start=(n == 0), stop=(n == 3))
                end(mm, f"ia{t}")
            for t in range(2):
                wait_drained(pe, f"tq{t}")
            wait_drained(pe, "tk")
            for t in range(2):
                for j in range(4):
                    g = f"sc{t}{j}"
                    bk = begin(g)
                    for h in range(2):
                        mm = pe.matmul(bk[:, h * T:(h + 1) * T], qz[:, h * QPK + j, t * P:(t + 1) * P], kT,
                                       start=True, stop=True)
                    end(mm, g)
            for i in range(2):
                project_cols(f"gh{i}", 4, [f"gh{2 * i}", f"gh{2 * i + 1}"], 2)
            wait_drained(pe, "ia0")
            wait_drained(pe, "ia1")
            forward("fb", vT)

            def turn_probs(j, h):
                g = f"pt{j}{h}"
                pe.wait_ge(p_ready, 8)
                bk = begin(g)
                for s in range(2):
                    for t in range(2):
                        mm = pe.transpose(bk[:, s * T + t * P:s * T + (t + 1) * P],
                                          probs[:, t, h * QPK + j, s * P:(s + 1) * P], ident)
                end(mm, g)

            def attend(j):
                bk = begin(f"pv{j}")
                for h in range(2):
                    wait_drained(pe, f"pt{j}{h}")
                for s in range(2):
                    for h in range(2):
                        mm = pe.matmul(bk[h * HD:(h + 1) * HD, 0:T], vtok[:, s, h * HD:(h + 1) * HD],
                                       ptb[2 * (j % 2) + h][:, s, :], start=(s == 0), stop=(s == 1))
                end(mm, f"pv{j}")

            for h in range(2):
                turn_probs(0, h)
            for j in range(4):
                if j + 1 < 4:
                    for h in range(2):
                        turn_probs(j + 1, h)
                attend(j)
            for i in range(2):
                project_cols(f"ga{i}", 4, [f"ga{2 * i}", f"ga{2 * i + 1}"], 2)
            pe.wait_ge(spec_ready, 8)
            for i in range(4):
                bk = begin(f"ib{i}")
                for n, (r, k) in enumerate([(r, k) for k in range(2) for r in range(2)]):
                    mm = pe.matmul(bk[:, 0:T], spec[:, r, k, i * P:(i + 1) * P], basis[r][k], start=(n == 0), stop=(n == 3))
                end(mm, f"ib{i}")

            def up(load, groups, src):
                w = pair(load, 4)
                for i in range(4):
                    bk = begin(groups[i])
                    for s in range(2):
                        for k in range(4):
                            m = 2 * i + s
                            mm = pe.matmul(bk[:, s * T:(s + 1) * T], w[:, k, m * P:(m + 1) * P], src[k],
                                           start=(k == 0), stop=(k == 3))
                    end(mm, groups[i])

            for i in range(4):
                wait_drained(pe, f"ib{i}")
            up("hu", [f"uh{i}" for i in range(4)], x2z)
            for j in range(4):
                wait_drained(pe, f"pv{j}")
            up("au", [f"ua{i}" for i in range(4)], [yat[:, j, :] for j in range(4)])
            for i in range(4):
                wait_drained(pe, f"ua{i}")
            wa, wb = pair("wo0", 4), pair("wo1", 4)
            for t in range(2):
                for h in range(2):
                    g = f"wo{t}{h}"
                    bk = begin(g)
                    for k in range(KD):
                        w = wa if k < 4 else wb
                        mm = pe.matmul(bk, mT[:, k, t * P:(t + 1) * P], w[:, k % 4, h * 512:(h + 1) * 512],
                                       start=(k == 0), stop=(k == KD - 1))
                    end(mm, g)
            pe.wait_ge(hn_ready, 2)
            for i in range(4):
                bk = begin(f"th{i}")
                for k in range(2):
                    for t in range(2):
                        mm = pe.transpose(bk[:, (2 * k + t) * P:(2 * k + t + 1) * P],
                                          hn[:, t, (2 * i + k) * P:(2 * i + k + 1) * P], ident)
                end(mm, f"th{i}")
            for i in range(4):
                wait_drained(pe, f"th{i}")
            pe.wait_ge(in_name["rw"], 16)
            bk = begin("lg")
            for k in range(KD):
                mm = pe.matmul(bk[0:NE, 0:T], rw[:, k, :], hnT[:, k, :], start=(k == 0), stop=(k == KD - 1))
            end(mm, "lg")
            wait_drained(pe, "lg")
            bk = begin("lt")
            for t in range(2):
                mm = pe.transpose(bk[:, t * NE:(t + 1) * NE], lgT[:, t * P:(t + 1) * P], ident[0:NE, 0:NE])
            end(mm, "lt")
            pe.wait_ge(mask_ready, 2)
            bk = begin("rk")
            pe.matmul(bk[:, 0:NE], tri, mask3[:, 0, 0:NE], start=True, stop=True)
            pe.matmul(bk[:, NE:2 * NE], ones, mask3[:, 0, 0:NE], start=True, stop=False)
            pe.matmul(bk[:, NE:2 * NE], tri, mask3[:, 1, 0:NE], start=False, stop=True)
            pe.matmul(bk[0:96, 64:65], mask3[:, 0, :], ones[:, 0:1], start=True, stop=False)
            end(pe.matmul(bk[0:96, 64:65], mask3[:, 1, :], ones[:, 0:1], start=False, stop=True), "rk")
            pe.wait_ge(over_ready, 1)
            bk = begin("lp")
            end(pe.matmul(bk[0:96, 0:1], tri[0:96, 0:96], over[0:96, :], start=True, stop=True), "lp")
            pe.wait_ge(pos_ready, 1)
            bk = begin("ls")
            pe.matmul(bk[0:1, 0:NLIST], tab[0:96, C_E:C_E + 1], onehot[0:96, :], start=True, stop=True)
            pe.matmul(bk[0:1, NLIST:2 * NLIST], tab[0:96, C_BASE:C_BASE + 1], onehot[0:96, :], start=True, stop=True)
            end(pe.matmul(bk[0:1, 2 * NLIST:2 * NLIST + 1], over[0:96, :], ones[0:96, 0:1], start=True, stop=True), "ls")
            pe.wait_ge(gate_ready, 2)
            bk = begin("gt")
            for t in range(2):
                mm = pe.transpose(bk[0:NE, t * P:(t + 1) * P], gate[:, t, :], ident)
            end(mm, "gt")

            for b in range(8):
                last = [g for g in GROUPS if BANK[g] == b][-1]
                pe.wait_ge(drained[b], NTH[last])
            hid = ps[:, 4:6, :]
            ybk = ps[:, 6, :]
            tbk = ps[:, 7, :]
            acc = [[ps[:, 2 * t + w, :] for w in range(2)] for t in range(2)]
            pe.wait_ge(in_name["b2"], 16)
            for t in range(2):
                for w in range(2):
                    mm = pe.matmul(acc[t][w], gateT[:, t * P:(t + 1) * P], b2pad[:, w * 512:(w + 1) * 512],
                                   start=True, stop=False, skip_group_check=True)
            mm.then_inc(comb, 1)

            def gather(buf, half, use, ready):
                pe.wait_ge(sel_ready, ready)
                pe.wait_ge(t_free, use)
                for k in range(4):
                    kk = 4 * half + k
                    for t in range(2):
                        for a in range(3):
                            mm = pe.matmul(tbk[:, k * P:(k + 1) * P], parts[:, a, t, kk * P:(kk + 1) * P],
                                           sel[:, t, :], start=(t == 0 and a == 0), stop=(t == 1 and a == 2))
                mm.then_inc(t_full, 1)

            def hidden(pos, c0, nth, count, selected, gathered, cols):
                pe.wait_ge(selb_ready, selected)
                pe.wait_ge(h_used, count)
                pe.wait_ge(t_free, gathered)
                for b in range(2):
                    for h in range(2):
                        c = 2 * b + h
                        pe.matmul(hid[h * 64:(h + 1) * 64, b, :], selB[:, pos, :], b1p[:, c * 512:(c + 1) * 512],
                                  start=True, stop=False, skip_group_check=True)
                for k in range(8):
                    slot = (c0 + k) % NSLOT
                    pe.wait_ge(ld[slot], nth[k])
                    w = ring[:, slot * SLOT:(slot + 1) * SLOT]
                    for b in range(2):
                        for h in range(2):
                            c = 2 * b + h
                            mm = pe.matmul(hid[h * 64:(h + 1) * 64, b, :], cols[:, k, :], w[:, c * 512:(c + 1) * 512],
                                           start=False, stop=(k == 7), skip_group_check=True)
                    if k < 7:
                        mm.then_inc(chunk_used, 1)
                mm.then_inc(h_full, 1)

            def turn_hidden(use, count):
                pe.wait_ge(hact_ready, count)
                pe.wait_ge(t_free, use)
                for i in range(4):
                    mm = pe.transpose(tbk[:, i * P:(i + 1) * P], hact[:, i // 2, (i % 2) * P:(i % 2 + 1) * P], ident)
                mm.then_inc(t_full, 1)

            def second(odd, c0, nth, count, turned):
                pe.wait_ge(t_free, turned)
                pe.wait_ge(y_used, count)
                for m in range(4):
                    slot = (c0 + 8 + m) % NSLOT
                    pe.wait_ge(ld[slot], nth[8 + m])
                    w = ring[:, slot * SLOT:(slot + 1) * SLOT].rearrange("p (k n) -> p k n", k=2)
                    for kk in range(2):
                        f = 2 * m + kk
                        b, half, r = f // 4, (f // 2) % 2, f % 2
                        lhs = hT[:, 2 * b + r, half * 64:(half + 1) * 64]
                        for h in range(2):
                            wd = h ^ odd
                            mm = pe.matmul(ybk[h * 64:(h + 1) * 64, :], lhs, w[:, kk, wd * 512:(wd + 1) * 512],
                                           start=(f == 0), stop=(f == 7), skip_group_check=True)
                    if m < 3:
                        mm.then_inc(chunk_used, 1)
                    else:
                        mm.then_inc(y_full, 1)

            def turn_gates(use, count):
                pe.wait_ge(selg_ready, count)
                pe.wait_ge(t_free, use)
                for w in range(2):
                    for t in range(2):
                        mm = pe.transpose(tbk[:, (2 * w + t) * P:(2 * w + t + 1) * P],
                                          selG[:, t, w * SLOTS:(w + 2) * SLOTS], ident)
                mm.then_inc(t_full, 1)

            def combine(ready, turned):
                pe.wait_ge(y_used, ready)
                pe.wait_ge(t_free, turned)
                for w in range(2):
                    for t in range(2):
                        mm = pe.matmul(acc[t][w], gT[:, 2 * w + t, :], yab[:, w, :], start=False, stop=False,
                                       skip_group_check=True)
                mm.then_inc(comb, 1)

            pe.wait_ge(lo_ready, 2)
            pe.wait_ge(b1_ready, 1)
            gather(0, 0, 1, 1)
            gather(0, 1, 2, 1)
            with pe.Fori(0, TURNS) as it:
                use = it * 10 + 3
                for j in range(GROUP):
                    c0 = CHUNKS * j
                    nth = [it * 48 + 16 * ((c0 + k) // NSLOT + 1) for k in range(CHUNKS)]
                    e1 = it * GROUP + (j + 1)
                    hidden(j % 2, c0, nth, e1, e1, use, xg[:, j // 2, :, (j % 2) * SLOTS:(j % 2 + 1) * SLOTS])
                    if j == 0:
                        turn_gates(use, it * 2 + 1)
                        gather(1, 0, use + 1, it * 2 + 2)
                        use = use + 2
                    elif j == 1:
                        gather(1, 1, use, it * 2 + 2)
                        use = use + 1
                    elif j == 2:
                        combine(it * 4 + 3, it * 10 + 4)
                        turn_gates(use, it * 2 + 2)
                        use = use + 1
                    else:
                        gather(0, 0, use, it * 2 + 3)
                        gather(0, 1, use + 1, it * 2 + 3)
                        use = use + 2
                    turn_hidden(use, e1)
                    use = use + 1
                    second(j % 2, c0, nth, e1, use)
                combine(it * 4 + 5, it * 10 + 9)

            pe.wait_ge(list_ready, 1)
            n_over = pe.value_load(olist[0:1, 2 * NLIST:2 * NLIST + 1], min_val=0, max_val=NLIST)
            OU = 2 + 10 * TURNS + 1
            with pe.If(n_over > 0):
                with pe.Fori(0, n_over) as i:
                    use = i * 4 + OU
                    gather(0, 0, use, i + (2 * TURNS + 2))
                    gather(0, 1, use + 1, i + (2 * TURNS + 2))
                    nth = [i * 16 + 16 * (NCH // NSLOT + 1)] * CHUNKS
                    hidden(0, 0, nth, i + (NE + 1), i + (NE + 2), use + 2, xg[:, 0, :, 0:SLOTS])
                    turn_gates(use + 2, i + (2 * TURNS + 1))
                    turn_hidden(use + 3, i + (NE + 1))
                    second(0, 0, nth, i + (NE + 1), use + 4)
                    pe.wait_ge(y_used, i + (NE + 2))
                    for w in range(2):
                        for t in range(2):
                            mm = pe.matmul(acc[t][w], gT[w * 64:(w + 1) * 64, 2 * w + t, :],
                                           yab[w * 64:(w + 1) * 64, w, :], start=False, stop=False,
                                           skip_group_check=True)
                    mm.then_inc(comb, 1)


        @block.scalar
        def _(act):
            act.dma_start(tab[:], c_tab).then_inc(in_tab, 16)
            act.dma_start(rows[0:36, :], conv_w[0].rearrange("a (c p) -> (a c) p", p=P)).then_inc(in_name["rows"], 16)
            act.dma_start(rows[36:48, :], conv_b[0].rearrange("(c p) -> c p", p=P)).then_inc(in_name["rows"], 16)
            act.dma_start(feats, c_feats).then_inc(in_name["feats"], 16)
            act.dma_start(fw1, filt_w1[0]).then_inc(in_name["fw1"], 16)
            act.dma_start(fw2, filt_w2[0]).then_inc(in_name["fw2"], 16)
            for i, v in enumerate((filt_b1, filt_freq1, filt_b2, filt_freq2)):
                act.dma_start(fvec[:, i:i + 1], v[0].unsqueeze(1)).then_inc(in_name["fvec"], 16)
            act.dma_start(fw3[0:FHID, :], filt_w3[0]).then_inc(in_name["fw3"], 16)
            act.dma_start(fw3[FHID:FHID + 1, :], filt_b3).then_inc(in_name["b3"], 16)
            act.dma_start(decay.rearrange("p t n -> p (t n)"), c_decay).then_inc(in_name["decay"], 16)
            act.dma_start(dft[:], c_dft).then_inc(in_name["dft"], 16)
            for o in range(2):
                act.dma_start(dbc[:, o, :], hyena_d[0, o:o + 1, :].partition_broadcast(P)).then_inc(in_name["dbc"], 16)
            act.dma_start(qkg[:, 0:64], q_norm_g.partition_broadcast(P)).then_inc(in_name["qkg"], 16)
            act.dma_start(qkg[:, 64:128], k_norm_g.partition_broadcast(P)).then_inc(in_name["qkg"], 16)
            for g in range(3):
                act.dma_start(b1raw[32 * g:32 * g + 32, :], expert_b1[0]).then_inc(in_name["b1"], 16)

            act.wait_ge(in_x, 16)
            for t in range(2):
                act.activation(u[:, t, :], xh[:, t, :], ACT.Square, accum_out=stat[:, t:t + 1]).then_inc(x_ss, 1)
            act.wait_ge(x_var, 1)
            act.activation(stat[:, 4:6], stat[:, 2:4], ACT.Sqrt).then_inc(x_std, 1)
            act.wait_ge(f_arg, 1)
            act.activation(h1, farg, ACT.Sin).then_inc(f_out, 1)
            for i in range(4):
                wait_filled(act, f"uT{i}")
                drains(act.copy(uT[:, 2 * i:2 * i + 2, :].rearrange("p k t -> p (k t)"), ps[:, BANK[f"uT{i}"], :]), f"uT{i}")
            act.wait_ge(f_arg, 2)
            act.activation(h2e[0:FHID, :], farg, ACT.Sin).then_inc(f_out, 1)

            def scale_z(i):
                wait_drained(act, "vec")
                wait_filled(act, f"z{i}")
                act.activation(zz[i], ps[:, BANK[f"z{i}"], 0:T], ACT.Identity,
                               bias=vecT[:, 36 + i:37 + i], scale=vecT[:, 12 + i:13 + i]).then_inc(z_scaled, 1)

            for i in range(4):
                scale_z(i)
            act.wait_ge(hk_ready, 2)
            for t in range(2):
                for c in range(4):
                    wait_drained(act, f"h{t}{c}")
                act.activation(absf[:, t], hk[:, t], ACT.Abs).then_inc(abs_ready, 1)
            for t in range(2):
                wait_filled(act, f"q{t}")
                act.activation(sq[t][:, 0:512], ps[:, BANK[f"q{t}"], :], ACT.Square).then_inc(qk_sq, 1)
            for t in range(2):
                wait_filled(act, f"kv{t}")
                act.activation(sq[t][:, 512:640], ps[:, BANK[f"kv{t}"], 0:128], ACT.Square).then_inc(qk_sq, 1)
            act.wait_ge(qk_var, 1)
            act.activation(stat[:, 28:48], stat[:, 8:28], ACT.Sqrt).then_inc(qk_std, 1)
            for i in range(4, 8):
                scale_z(i)
            for g, dst in (("tv0", vT[:, 0, :]), ("tv1", vT[:, 1, :]), ("tx0", x1T[:, 0, :]), ("tx1", x1T[:, 1, :])):
                wait_filled(act, g)
                drains(act.copy(dst, ps[:, BANK[g], :]), g)
            act.wait_ge(qz_zero, 1)
            for t in range(2):
                g = f"tq{t}"
                wait_filled(act, g)
                src = ps[:, BANK[g], :].rearrange("p (j t) -> p j t", j=4)
                act.copy(qz[0:HD, 0:QPK, t * P:(t + 1) * P], src[0:HD])
                drains(act.copy(qz[HD:P, QPK:NH, t * P:(t + 1) * P], src[HD:P]), g)
            wait_filled(act, "tk")
            drains(act.copy(kT, ps[:, BANK["tk"], 0:T]), "tk")
            for i in range(8, 12):
                scale_z(i)
            for t in range(2):
                for j in range(4):
                    g, i = f"sc{t}{j}", 2 * (4 * t + j)
                    act.wait_ge(mx_ready, 4 * t + j + 1)
                    for h in range(2):
                        ins = act.activation(probs[:, t, h * QPK + j, :], ps[:, BANK[g], h * T:(h + 1) * T], ACT.Exp,
                                             bias=smax[:, i + h:i + h + 1], accum_out=smax[:, 16 + i + h:17 + i + h])
                    drains(ins, g)

            def open_gate(groups, dst):
                for i, g in enumerate(groups):
                    wait_filled(act, g)
                    drains(act.activation(dst[:, 2 * i:2 * i + 2, :].rearrange("p m t -> p (m t)"), ps[:, BANK[g], :], ACT.Sigmoid), g)

            open_gate([f"gh{i}" for i in range(4)], ghy)

            def take_probs(j):
                for h in range(2):
                    g = f"pt{j}{h}"
                    wait_filled(act, g)
                    drains(act.copy(ptb[2 * (j % 2) + h].rearrange("p s t -> p (s t)"), ps[:, BANK[g], :]), g)

            take_probs(0)
            take_probs(1)
            for j in range(4):
                wait_filled(act, f"pv{j}")
                drains(act.copy(yat[:, j, :], ps[:, BANK[f"pv{j}"], 0:T]), f"pv{j}")
                if j + 2 < 4:
                    take_probs(j + 2)
            open_gate([f"ga{i}" for i in range(4)], gat)
            for t in range(2):
                for w in range(2):
                    wait_drained(act, f"wo{t}{w}")
                    act.activation(sh(6144, 512), xh[:, t, w * 512:(w + 1) * 512], ACT.Square,
                                   accum_out=stat[:, 48 + 2 * t + w:49 + 2 * t + w]).then_inc(h_ss, 1)
                    act.wait_ge(h_ss, 2 * t + w + 1)
                act.wait_ge(h_var, t + 1)
                act.activation(stat[:, 54 + t:55 + t], stat[:, 52 + t:53 + t], ACT.Sqrt).then_inc(h_std, 1)
            for t in range(2):
                act.wait_ge(hn_ready, t + 1)
                act.copy(parts[:, 0, t, :], hn[:, t, :]).then_inc(hi_ready, 1)
            for i in range(4):
                g = f"th{i}"
                wait_filled(act, g)
                drains(act.copy(hnT[:, 2 * i:2 * i + 2, :].rearrange("p k t -> p (k t)"), ps[:, BANK[g], :]), g)
            for t in range(2):
                act.wait_ge(res_ready, t + 1)
                act.copy(parts[:, 1, t, :], resid).then_inc(mid16_ready, 1)
            act.wait_ge(r_max, 2)
            for t in range(2):
                act.activation(gate[:, t, :], logit[:, t, :], ACT.Exp, bias=smax[:, 48 + t:49 + t]).then_inc(r_exp, 1)

            def take_turn(dst, count):
                act.wait_ge(t_full, count)
                act.copy(dst, ps[:, 7, :]).then_inc(t_free, 1)

            def gathered(buf, half):
                return xg[:, buf, 4 * half:4 * half + 4, :].rearrange("p k s -> p (k s)")

            gT_all = gT.rearrange("p w t -> p (w t)")
            hT_all = hT.rearrange("p f s -> p (f s)")

            def sigmoid(count):
                act.wait_ge(glu_ready, count)
                act.activation(sig, glu, ACT.Sigmoid, scale=ALPHA).then_inc(sig_ready, 1)

            take_turn(gathered(0, 0), 1)
            take_turn(gathered(0, 1), 2)
            with act.Fori(0, TURNS) as it:
                n = 3
                for j, takes in enumerate(([gT_all, gathered(1, 0), hT_all], [gathered(1, 1), hT_all],
                                           [gT_all, hT_all], [gathered(0, 0), gathered(0, 1), hT_all])):
                    sigmoid(it * GROUP + (j + 1))
                    for dst in takes:
                        take_turn(dst, it * 10 + n)
                        n += 1
            act.wait_ge(list_ready, 1)
            n_over = act.value_load(olist[0:1, 2 * NLIST:2 * NLIST + 1], min_val=0, max_val=NLIST)
            with act.If(n_over > 0):
                with act.Fori(0, n_over) as i:
                    base = 2 + 10 * TURNS
                    take_turn(gathered(0, 0), i * 4 + (base + 1))
                    take_turn(gathered(0, 1), i * 4 + (base + 2))
                    sigmoid(i + (NE + 1))
                    take_turn(gT_all, i * 4 + (base + 3))
                    take_turn(hT_all, i * 4 + (base + 4))

        @block.vector
        def _(v):
            steps = [0]

            def link(ins):
                steps[0] += 1
                ins.then_inc(dve_step, 1)
                v.wait_ge(dve_step, steps[0])

            link(v.memset(h2e[FHID:FHID + 1, :], 1.0))
            link(v.memset(rankm[:], -1.0))
            v.memset(mark[:, 0:1], 0.0).then_inc(pads_ready, 1)

            def filter_arg(g, b, count):
                wait_filled(v, g)
                if count == 2:
                    v.wait_ge(f_out, 1)
                v.tensor_scalar(farg, ps[0:FHID, BANK[g], 0:T], fvec[:, b:b + 1], fvec[:, b + 1:b + 2], ALU.add, ALU.mult)\
                    .then_inc(drained[BANK[g]], 1)
                wait_drained(v, g)
                magic = 12582912.0
                link(v.tensor_scalar(frnd, farg, 0.15915494309, magic, ALU.mult, ALU.add))
                link(v.tensor_scalar(frnd, frnd, -magic, None, ALU.add))
                for part in (PI2_A, PI2_B, PI2_C):
                    link(v.scalar_tensor_tensor(farg, frnd, -part, farg, ALU.mult, ALU.add))
                v.tensor_scalar(farg, farg, PI_IN, -PI_IN, ALU.min, ALU.max).then_inc(f_arg, 1)

            wait_filled(v, "vec")
            drains(v.tensor_copy(vecT, ps[:, BANK["vec"], 0:48]), "vec")
            v.wait_ge(in_name["fvec"], 64)
            filter_arg("f1", 0, 1)
            v.wait_ge(x_ss, 2)
            v.tensor_scalar(stat[:, 2:4], stat[:, 0:2], 1.0 / D, EPS, ALU.mult, ALU.add).then_inc(x_var, 1)
            v.wait_ge(x_std, 1)
            link(v.reciprocal(stat[:, 6:8], stat[:, 4:6]))
            v.wait_ge(in_name["g1b"], 16)
            for t in range(2):
                v.scalar_tensor_tensor(u[:, t, :], xh[:, t, :], stat[:, 6 + t:7 + t], g1b, ALU.mult, ALU.mult).then_inc(u_ready, 1)
            v.wait_ge(u_ready, 2)
            filter_arg("f2", 2, 2)

            def outer_taps(i):
                v.wait_ge(z_scaled, i + 1)
                zp = ps[:, BANK[f"z{i}"], 0:T]
                link(v.scalar_tensor_tensor(zz[i][:, 1:T], zp[:, 0:T - 1], vecT[:, i:i + 1], zz[i][:, 1:T], ALU.mult, ALU.add))
                drains(v.scalar_tensor_tensor(zz[i][:, 0:T - 1], zp[:, 1:T], vecT[:, 24 + i:25 + i], zz[i][:, 0:T - 1],
                                              ALU.mult, ALU.add), f"z{i}")

            wait_drained(v, "vec")
            for i in range(4):
                outer_taps(i)
            v.wait_ge(in_name["decay"], 16)
            for t in range(2):
                for c in range(4):
                    g = f"h{t}{c}"
                    wait_filled(v, g)
                    drains(v.tensor_tensor(hk[:, t, c // 2, c % 2, :], ps[:, BANK[g], :], decay[:, t, :], ALU.mult), g)
                    if t == 0 and c % 2:
                        wait_drained(v, g)
                        v.memset(hk[0:1, 0, c // 2, 1, :], 0.0).then_inc(hk_ready, 1)
            v.wait_ge(abs_ready, 2)
            link(v.tensor_tensor(habs, absf[:, 0, :, 0, :], absf[:, 0, :, 1, :], ALU.add))
            link(v.tensor_tensor(habs, habs, absf[:, 1, :, 0, :], ALU.add))
            v.tensor_tensor(habs, habs, absf[:, 1, :, 1, :], ALU.add).then_inc(habs_ready, 1)
            v.wait_ge(in_name["qkg"], 32)
            v.wait_ge(in_tab, 16)
            for t in range(2):
                for a in range(2):
                    g = qkg[:, 64 * a:64 * a + 64].rearrange("p (i two) -> p two i", two=2)
                    scale = HD ** -0.5 if a == 0 else 1.0
                    for n, (eo, trig) in enumerate(((0, cs), (1, sn), (0, sn), (1, cs))):
                        ins = v.scalar_tensor_tensor(rope[:, t, 4 * a + n, :], g[:, eo, :], scale, trig[t], ALU.mult, ALU.mult)
            link(ins)
            v.wait_ge(qk_sq, 4)
            for t in range(2):
                link(v.tensor_reduce(stat[:, 8 + 10 * t:18 + 10 * t], sq[t].rearrange("p (h c) -> p h c", c=HD), AX.X, ALU.add))
            v.tensor_scalar(stat[:, 8:28], stat[:, 8:28], 1.0 / HD, EPS, ALU.mult, ALU.add).then_inc(qk_var, 1)
            v.wait_ge(qk_std, 1)
            link(v.reciprocal(stat[:, 8:28], stat[:, 28:48]))
            for t in range(2):
                rs = stat[:, 8 + 10 * t:18 + 10 * t].unsqueeze(2)
                drains(v.tensor_tensor(qn[t][:, 0:NH, :], ps[:, BANK[f"q{t}"], :].rearrange("p (h c) -> p h c", c=HD),
                                       rs[:, 0:NH, :].to_broadcast([P, NH, HD]), ALU.mult), f"q{t}")
                link(v.tensor_tensor(qn[t][:, NH:NH + NKV, :], ps[:, BANK[f"kv{t}"], 0:128].rearrange("p (h c) -> p h c", c=HD),
                                     rs[:, NH:NH + NKV, :].to_broadcast([P, NKV, HD]), ALU.mult))
                drains(v.tensor_copy(vtok[:, t, :], ps[:, BANK[f"kv{t}"], 128:256]), f"kv{t}")

            def rotate(src, heads, tables, dst):
                x0, x1 = src[:, :, 0::2], src[:, :, 1::2]
                m = [a[:, 0:heads, :] for a in mm4]
                for n, x in enumerate((x0, x1, x0, x1)):
                    ins = v.tensor_tensor(m[n], x, tables[:, n:n + 1, :].to_broadcast([P, heads, 32]), ALU.mult)
                link(ins)
                per = heads // NKV
                view = [a.rearrange("p (g j) i -> p g j i", g=NKV) for a in m]
                out_ = dst.rearrange("p (j g c) -> p g j c", g=NKV, j=per)
                link(v.tensor_tensor(out_[:, :, :, 0::2], view[0], view[1], ALU.subtract))
                v.tensor_tensor(out_[:, :, :, 1::2], view[2], view[3], ALU.add).then_inc(qk_ready, 1)
                done[0] += 1
                v.wait_ge(qk_ready, done[0])

            done = [0]
            for t in range(2):
                rotate(qn[t][:, 0:NH, :], NH, rope[:, t, 0:4, :], qr[t])
                rotate(qn[t][:, NH:NH + NKV, :], NKV, rope[:, t, 4:8, :], kr[t])
            for o in range(2):
                wait_filled(v, f"nrm{o}")
                drains(v.reciprocal(rinv[:, o, :], ps[:, BANK[f"nrm{o}"], :]), f"nrm{o}")
            v.wait_ge(in_name["dbc"], 32)
            for o in range(2):
                wait_drained(v, f"nrm{o}")
                for k in range(2):
                    for r in range(2):
                        g = f"kf{o}{r}{k}"
                        wait_filled(v, g)
                        drains(v.scalar_tensor_tensor(kf[:, o, r, k, :], ps[:, BANK[g], :], wk[k], rinv[:, o, :],
                                                      ALU.mult, ALU.mult), g)
                        if r == 0:
                            wait_drained(v, g)
                            link(v.scalar_tensor_tensor(kf[:, o, 0, k, :], dbc[:, o, :], wk[k], kf[:, o, 0, k, :],
                                                        ALU.mult, ALU.add))
            v.memset(qz, 0.0).then_inc(qz_zero, 1)
            for i in range(4, 8):
                outer_taps(i)

            def filter_product(prefix, o):
                for k in range(2):
                    yr, ys = (ps[:, BANK[f"{prefix}{r}{k}"], :] for r in range(2))
                    kr_, ks = kf[:, o, 0, k, :], kf[:, o, 1, k, :]
                    wait_filled(v, f"{prefix}0{k}")
                    v.tensor_tensor(prod[:, 0, :], yr, kr_, ALU.mult).then_inc(dve_step, 1)
                    steps[0] += 1
                    drains(v.tensor_tensor(prod[:, 2, :], yr, ks, ALU.mult), f"{prefix}0{k}")
                    wait_filled(v, f"{prefix}1{k}")
                    link(v.tensor_tensor(prod[:, 1, :], ys, ks, ALU.mult))
                    drains(v.tensor_tensor(prod[:, 3, :], ys, kr_, ALU.mult), f"{prefix}1{k}")
                    v.tensor_tensor(spec[:, 0, k, :], prod[:, 0, :], prod[:, 1, :], ALU.subtract).then_inc(spec_ready, 1)
                    wait_drained(v, f"{prefix}1{k}")
                    v.tensor_tensor(spec[:, 1, k, :], prod[:, 2, :], prod[:, 3, :], ALU.add).then_inc(spec_ready, 1)
                    v.wait_ge(spec_ready, 4 * o + 2 * k + 2)

            wait_drained(v, "kf111")
            filter_product("fa", 0)
            for i in range(8, 12):
                outer_taps(i)
            for t in range(2):
                wait_drained(v, f"tx{t}")
                wait_filled(v, f"ia{t}")
                drains(v.tensor_tensor(vT[:, t, :], ps[:, BANK[f"ia{t}"], :], x1T[:, t, :], ALU.mult), f"ia{t}")

            def normalise(n):
                t, j = n // 4, n % 4
                wait_drained(v, f"sc{t}{j}")
                link(v.reciprocal(smax[:, 32 + 2 * (n % 4):34 + 2 * (n % 4)], smax[:, 16 + 2 * n:18 + 2 * n]))
                pr = probs[:, t, j::QPK, :]
                rs = smax[:, 32 + 2 * (n % 4):34 + 2 * (n % 4)].unsqueeze(2).to_broadcast([P, 2, T])
                v.tensor_tensor(pr, pr, rs, ALU.mult).then_inc(p_ready, 1)
                v.wait_ge(p_ready, n + 1)

            for n in range(8):
                g = f"sc{n // 4}{n % 4}"
                wait_filled(v, g)
                v.tensor_reduce(smax[:, 2 * n:2 * n + 2], ps[:, BANK[g], :].rearrange("p (h s) -> p h s", h=2), AX.X,
                                ALU.max, negate=True).then_inc(mx_ready, 1)
                if n >= 1:
                    normalise(n - 1)
            normalise(7)
            filter_product("fb", 1)
            for i in range(4):
                g = f"ib{i}"
                wait_filled(v, g)
                drains(v.tensor_tensor(x2z[i], ps[:, BANK[g], 0:T], x2z[i], ALU.mult), g)
            v.memset(gateT, 0.0)
            v.memset(b2pad, 0.0).then_inc(pads_ready, 1)
            for i in range(4):
                g = f"uh{i}"
                wait_filled(v, g)
                wait_drained(v, f"gh{i}")
                drains(v.tensor_tensor(mT[:, 2 * i:2 * i + 2, :], ps[:, BANK[g], :].rearrange("p (m t) -> p m t", m=2),
                                       ghy[:, 2 * i:2 * i + 2, :], ALU.mult), g)
            for i in range(4):
                g = f"ua{i}"
                sl = slice(2 * i, 2 * i + 2)
                wait_filled(v, g)
                wait_drained(v, f"ga{i}")
                wait_drained(v, f"uh{i}")
                link(v.tensor_tensor(gat[:, sl, :], ps[:, BANK[g], :].rearrange("p (m t) -> p m t", m=2), gat[:, sl, :], ALU.mult))
                drains(v.tensor_tensor(mT[:, sl, :], mT[:, sl, :], gat[:, sl, :], ALU.add), g)
            for t in range(2):
                for w in range(2):
                    g = f"wo{t}{w}"
                    part = xh[:, t, w * 512:(w + 1) * 512]
                    wait_filled(v, g)
                    drains(v.tensor_tensor(part, ps[:, BANK[g], :], part, ALU.add), g)
                v.wait_ge(h_ss, 2 * t + 2)
                link(v.tensor_tensor(stat[:, 52 + t:53 + t], stat[:, 48 + 2 * t:49 + 2 * t], stat[:, 49 + 2 * t:50 + 2 * t], ALU.add))
                v.tensor_scalar(stat[:, 52 + t:53 + t], stat[:, 52 + t:53 + t], 1.0 / D, EPS, ALU.mult, ALU.add).then_inc(h_var, 1)
                v.wait_ge(h_std, t + 1)
                link(v.reciprocal(stat[:, 56 + t:57 + t], stat[:, 54 + t:55 + t]))
                v.wait_ge(in_name["g2b"], 16)
                v.scalar_tensor_tensor(hn[:, t, :], xh[:, t, :], stat[:, 56 + t:57 + t], g2b, ALU.mult, ALU.mult).then_inc(hn_ready, 1)
                v.wait_ge(hn_ready, t + 1)
            for t in range(2):
                v.wait_ge(hi_ready, t + 1)
                v.tensor_tensor(resid, hn[:, t, :], parts[:, 0, t, :], ALU.subtract).then_inc(res_ready, 1)
                v.wait_ge(mid16_ready, t + 1)
                v.tensor_tensor(parts[:, 2, t, :], resid, parts[:, 1, t, :], ALU.subtract).then_inc(lo_ready, 1)
                v.wait_ge(lo_ready, t + 1)
            wait_filled(v, "lg")
            v.wait_ge(in_name["rb"], 16)
            drains(v.tensor_scalar(lgT, ps[0:NE, BANK["lg"], 0:T], rbias, None, ALU.add), "lg")
            wait_filled(v, "lt")
            drains(v.tensor_copy(logit[:].rearrange("p t e -> p (t e)"), ps[:, BANK["lt"], 0:2 * NE]), "lt")
            wait_drained(v, "lt")
            ioe = tab[:, C_IOE:C_IOE + NE]
            for t in range(2):
                link(v.max(top8[:, t, :], logit[:, t, :]))
                v.tensor_scalar(smax[:, 48 + t:49 + t], top8[:, t, 0:1], -1.0, None, ALU.mult).then_inc(r_max, 1)
                link(v.max_index(idx8[:, t, :], top8[:, t, :], logit[:, t, :]))
                link(v.tensor_copy(idxf[:, t, :], idx8[:, t, :]))
                mk = mask3[:, t, 0:NE]
                link(v.tensor_scalar(mk, ioe, idxf[:, t, 0:1], None, ALU.is_equal))
                for r in range(1, TOPK):
                    link(v.scalar_tensor_tensor(mk, ioe, idxf[:, t, r:r + 1], mk, ALU.is_equal, ALU.add))
                v.tensor_copy(mask3[:, t, NE:2 * NE], mk)
                v.tensor_copy(mask3[:, t, 2 * NE:3 * NE], mk).then_inc(mask_ready, 1)
            v.wait_ge(mask_ready, 2)
            for t in range(2):
                v.wait_ge(r_exp, t + 1)
                link(v.tensor_tensor(gate[:, t, :], gate[:, t, :], mask3[:, t, 0:NE], ALU.mult))
                link(v.tensor_reduce(smax[:, 50 + t:51 + t], gate[:, t, :], AX.X, ALU.add))
                link(v.reciprocal(smax[:, 52 + t:53 + t], smax[:, 50 + t:51 + t]))
                v.tensor_scalar(gate[:, t, :], gate[:, t, :], smax[:, 52 + t:53 + t], None, ALU.mult).then_inc(gate_ready, 1)
            wait_filled(v, "rk")
            rk = ps[:, BANK["rk"], :]
            for t in range(2):
                link(v.scalar_tensor_tensor(rankm[:, t, 0:NE], rk[:, NE * t:NE * t + NE], 1.0, mask3[:, t, 0:NE], ALU.add, ALU.mult))
            v.tensor_scalar(rankm[:, :, 0:NE], rankm[:, :, 0:NE], -1.0, None, ALU.add).then_inc(rank_ready, 1)
            link(v.tensor_scalar(over[0:96, :], rk[0:96, 64:65], tab[0:96, C_BASE:C_BASE + 1], None, ALU.is_gt))
            drains(v.memset(mark[:, 0:1], 0.0), "rk")
            v.memset(mark[:, 1:2], 0.0).then_inc(over_ready, 1)
            wait_filled(v, "lp")
            link(v.tensor_copy(pos[0:96, :], ps[0:96, BANK["lp"], 0:1]))
            drains(v.memset(mark[:, 2:3], 0.0), "lp")
            v.tensor_scalar(onehot[0:96, :], tab[0:96, C_IOL:C_IOL + NLIST], pos[0:96, :], over[0:96, :], ALU.is_equal, ALU.mult)\
                .then_inc(pos_ready, 1)
            wait_filled(v, "ls")
            link(v.tensor_copy(olist[0:1, 0:2 * NLIST + 1], ps[0:1, BANK["ls"], 0:2 * NLIST + 1]))
            drains(v.memset(mark[:, 3:4], 0.0), "ls")
            v.memset(mark[:, 4:5], 0.0).then_inc(list_ready, 1)
            wait_filled(v, "gt")
            drains(v.tensor_copy(gateT[0:NE, :], ps[0:NE, BANK["gt"], 0:T]), "gt")

            iota = tab[:, C_IOTA:C_IOTA + T]
            iota0 = iota[:, 0:SLOTS]

            def select(e, block, first=iota0):
                for t in range(2):
                    ins = v.tensor_scalar(sel[:, t, block * SLOTS:(block + 1) * SLOTS], first, rankm[:, t, ds(e, 1)], None, ALU.is_equal)
                return ins

            def select_gates(e, block, first=iota0):
                for t in range(2):
                    ins = v.tensor_scalar(selG[:, t, block * SLOTS:(block + 1) * SLOTS], first, rankm[:, t, ds(e, 1)],
                                          gate[:, t, ds(e, 1)], ALU.is_equal, ALU.mult)
                return ins

            def select_bias(pos_, e):
                v.tensor_scalar(selB[:, pos_, :], ones[:, 0:SLOTS], tab[:, ds(e + C_ID3, 1)], None, ALU.mult).then_inc(selb_ready, 1)

            def swiglu(count):
                v.wait_ge(h_full, count)
                hid = ps[:, 4:6, :]
                v.tensor_scalar(glu, hid[:, :, 0::2], LIMIT, None, ALU.min).then_inc(glu_ready, 1)
                v.tensor_scalar(lin, hid[:, :, 1::2], LIMIT, -LIMIT, ALU.min, ALU.max).then_inc(h_used, 1)
                v.wait_ge(glu_ready, count)
                v.wait_ge(h_used, count + 1)
                v.scalar_tensor_tensor(lin, lin, 1.0, glu, ALU.add, ALU.mult).then_inc(mid_ready, 1)
                v.wait_ge(mid_ready, count)
                v.wait_ge(sig_ready, count)
                v.tensor_tensor(hact, lin, sig, ALU.mult).then_inc(hact_ready, 1)

            def take_y(odd, count, combined):
                v.wait_ge(comb, combined)
                v.wait_ge(y_full, count)
                v.tensor_copy(yab[0:64, odd, :], ps[0:64, 6, :])
                v.tensor_copy(yab[64:P, 1 - odd, :], ps[64:P, 6, :]).then_inc(y_used, 1)

            v.memset(mark[:, 0:1], 0.0).then_inc(t_free, 1)
            v.memset(mark[:, 1:2], 0.0).then_inc(h_used, 1)
            v.memset(mark[:, 2:3], 0.0).then_inc(y_used, 1)
            v.wait_ge(rank_ready, 1)
            v.wait_ge(gate_ready, 2)
            select(0, 0)
            select(1, 1).then_inc(sel_ready, 1)
            select_bias(0, 0)
            with v.Fori(0, TURNS) as it:
                e = it * GROUP
                v.wait_ge(t_full, it * 10 + 2)
                select(e + 2, 0)
                select(e + 3, 1).then_inc(sel_ready, 1)
                select_gates(e, 0)
                select_gates(e + 1, 1)
                select_gates(e, 2).then_inc(selg_ready, 1)
                for j in range(GROUP):
                    select_bias((j + 1) % 2, e + (j + 1))
                    swiglu(e + (j + 1))
                    take_y(j % 2, e + (j + 1), it * 2 + (j // 2 + 1))
                    if j == 1:
                        select(e + 4, 0)
                        select(e + 5, 1).then_inc(sel_ready, 1)
                        select_gates(e + 2, 0)
                        select_gates(e + 3, 1)
                        select_gates(e + 2, 2).then_inc(selg_ready, 1)
            n_over = v.value_load(olist[0:1, 2 * NLIST:2 * NLIST + 1], min_val=0, max_val=NLIST)
            with v.If(n_over > 0):
                with v.Fori(0, n_over) as i:
                    e = v.value_load(olist[0:1, ds(i, 1)], min_val=0, max_val=NE - 1)
                    base = v.value_load(olist[0:1, ds(i + NLIST, 1)], min_val=0, max_val=T - SLOTS)
                    v.wait_ge(comb, i + (NE // 2 + 1))
                    window = iota[:, ds(base, SLOTS)]
                    select(e, 0, window).then_inc(sel_ready, 1)
                    select_gates(e, 0, window)
                    select_gates(e, 2, window).then_inc(selg_ready, 1)
                    select_bias(0, e)
                    swiglu(i + (NE + 1))
                    take_y(0, i + (NE + 1), i + (NE // 2 + 1))
            v.wait_ge(comb, n_over + (NE // 2 + 1))
            for t in range(2):
                for w in range(2):
                    part = xh[:, t, w * 512:(w + 1) * 512]
                    v.tensor_tensor(part, ps[:, 2 * t + w, :], part, ALU.add).then_inc(out_ready, 1)

        @block.gpsimd
        def _(pool):
            def link(ins, n):
                ins.then_inc(pool_step, 1)
                pool.wait_ge(pool_step, n)

            pool.wait_ge(in_name["b1"], 48)
            link(pool.memset(b1p[96:P, :], 0.0), 1)
            link(pool.tensor_copy(b1p[0:96, :], b1raw), 2)
            link(pool.tensor_tensor(b1raw, b1raw, b1p[0:96, :], ALU.subtract), 3)
            link(pool.tensor_copy(b1mid, b1raw), 4)
            link(pool.tensor_tensor(b1raw, b1raw, b1mid, ALU.subtract), 5)
            link(pool.tensor_copy(b1p[32:64, :], b1mid[32:64, :]), 6)
            pool.tensor_copy(b1p[64:96, :], b1raw[64:96, :]).then_inc(b1_ready, 1)
            pool.wait_ge(b1_ready, 1)
            pool.wait_ge(abs_ready, 2)
            for o in range(2):
                for t in range(2):
                    f, b = hk[:, t, o, 0, :], hk[:, t, o, 1, :]
                    pool.tensor_tensor(fsum[:, t, o, :], f, b, ALU.add).then_inc(pm_ready, 1)
                    pool.wait_ge(pm_ready, 4 * o + 2 * t + 1)
                    pool.tensor_tensor(b, f, b, ALU.subtract).then_inc(pm_ready, 1)
                    pool.wait_ge(pm_ready, 4 * o + 2 * t + 2)


_INS = ["x", "norm1_g", "w_in", "conv_w", "conv_b", "filt_w1", "filt_b1", "filt_freq1", "filt_w2",
        "filt_b2", "filt_freq2", "filt_w3", "filt_b3", "hyena_d", "q_norm_g", "k_norm_g",
        "w_hyena_up", "w_attn_up", "w_out", "norm2_g", "router_w", "router_b", "expert_w1",
        "expert_b1", "expert_w2", "expert_b2"]


def kernel(**inputs):
    import numpy as _np
    import concourse.bacc as _bacc
    from concourse import mybir as _mybir
    from concourse.bass_utils import run_bass_kernel_spmd as _run

    nc = _bacc.Bacc("TRN2", target_bir_lowering=False, num_devices=1)
    arrays, args = {}, []
    named = [(n, inputs[n]) for n in _INS]
    named += list(zip(("c_tab", "c_dft", "c_feats", "c_decay"), tables()))
    for name, value in named:
        a = _np.ascontiguousarray(value)
        arrays[f"in_{name}"] = a
        args.append(nc.dram_tensor(f"in_{name}", a.shape, _mybir.dt.from_np(a.dtype), kind="ExternalInput").ap())
    out = nc.dram_tensor("out_0", (1, T, D), F32, kind="ExternalOutput").ap()
    hybrid_block(nc, *args, out)
    r = _run(nc, [arrays], core_ids=[0])
    return r.results[0]["out_0"]
```

```python
from contextlib import ExitStack

import numpy as np

import concourse.bass as bass
from concourse import mybir
from concourse.alu_op_type import AluOpType as ALU

ACT = mybir.ActivationFunctionType
AX = mybir.AxisListType
F32 = mybir.dt.float32
BF16 = mybir.dt.bfloat16
I32 = mybir.dt.int32
U32 = mybir.dt.uint32
ds = bass.ds

P = 128
T = 256
TT = T // P
D = 1024
KD = D // P
HW = 512
NH, NKV, HD = 8, 2, 64
QPK = NH // NKV
NE, TOPK = 32, 4
FF = 1024
EPS = 1e-6
LIMIT, ALPHA = 7.0, 1.702
FEMB, FHID = 33, 64
NDFT = 2 * T - 1
SLOTS = 64
SLOT = 2048
NSLOT = 16
CHUNKS = 12
GROUP = 4
TURNS = NE // GROUP
NLIST = 32
NWIN = T // SLOTS
PI = 3.14159274
PI_IN = 3.1415925
PI2_A, PI2_B, PI2_C = 6.28125, 1.9340515136718750e-03, 1.2556659146e-06

C_ID, C_TRI, C_IOTA, C_WK = 0, 128, 256, 512
C_COS, C_SIN, C_IOL, C_E, C_BASE, C_ID3, C_ONE, C_IOE = 514, 578, 642, 674, 675, 676, 708, 836
C_FEAT = 868
C_COLS = C_FEAT + T


def tables():
    c = np.zeros((P, C_COLS), np.float32)
    c[:, C_ID:C_ID + P] = np.eye(P)
    c[:, C_TRI:C_TRI + P] = np.triu(np.ones((P, P)), 1)
    c[:, C_IOTA:C_IOTA + T] = 1 + np.arange(T)
    bins = np.full(T, 2.0 / NDFT)
    bins[0] = 1.0 / NDFT
    c[:, C_WK:C_WK + 2] = bins.reshape(2, P).T
    half = HD // 2
    freqs = np.float32(10000.0) ** (-np.arange(0, half, 2, dtype=np.float32) / half)
    row = np.repeat(np.arange(T // 64, dtype=np.float32), 64)
    col = np.tile(np.arange(64, dtype=np.float32), T // 64)
    ang = np.concatenate([row[:, None] * freqs, col[:, None] * freqs], -1).astype(np.float32)
    c[:, C_COS:C_COS + 64] = np.cos(ang).reshape(2, P, 32).transpose(1, 0, 2).reshape(P, 64)
    c[:, C_SIN:C_SIN + 64] = np.sin(ang).reshape(2, P, 32).transpose(1, 0, 2).reshape(P, 64)
    c[:, C_IOL:C_IOL + NLIST] = np.arange(NLIST)
    j = np.arange((NWIN - 1) * NE)
    c[:j.size, C_E] = j % NE
    c[:j.size, C_BASE] = SLOTS * (1 + j // NE)
    c[:96, C_ID3:C_ID3 + 32] = np.tile(np.eye(32), (3, 1))
    c[:, C_ONE:C_ONE + P] = 1.0
    c[:, C_IOE:C_IOE + NE] = np.arange(NE)
    n = np.arange(T)
    w = 2 * np.pi * (np.outer(n, n) % NDFT) / NDFT
    dft = np.stack([np.cos(w), np.sin(w)]).astype(np.float32)
    dft = np.ascontiguousarray(dft.reshape(2, 2, P, T).transpose(2, 0, 1, 3)).reshape(P, 4 * T)
    f32 = np.float32
    t = np.linspace(0.0, 1.0, T, dtype=f32)[:, None]
    bands = (FEMB - 1) // 2
    wt = (f32(2.0 * np.pi) * np.arange(T, dtype=f32)[:, None] / f32(T)).astype(f32)
    fr = np.linspace(1e-4, bands - 1, bands, dtype=f32)[None, :]
    a = (wt * fr).astype(f32)
    feats = np.concatenate([t, np.cos(a), -np.sin(a)], -1).astype(f32)
    c[:FEMB, C_FEAT:C_FEAT + T] = feats.T
    lo, hi = np.log(1e-2) / 1.5, np.log(1e-2) / 0.3
    deltas = np.abs(np.linspace(lo, hi, HW, dtype=f32))
    decay = np.exp(-t * deltas).astype(f32)
    decay = np.ascontiguousarray(decay.reshape(2, P, HW).transpose(1, 0, 2)).reshape(P, 2 * HW)
    return c, dft, decay


GROUPS = (
    [f"uT{i}" for i in range(4)] + ["vec", "fv", "f1"] + ["z0", "f2", "z1", "z2", "z3"]
    + [f"h{t}{c}" for t in range(2) for c in range(4)]
    + ["q0", "q1", "kv0", "kv1"]
    + ["nrm0", "nrm1"] + [f"kf{o}{r}{k}" for o in range(2) for k in range(2) for r in range(2)]
    + [f"z{i}" for i in range(4, 8)]
    + ["tv0", "tv1"] + [f"fa{r}{k}" for k in range(2) for r in range(2)]
    + ["tx0", "tx1", "tq0", "tq1", "tk"]
    + [f"z{i}" for i in range(8, 12)]
    + ["ia0", "ia1"] + [f"sc{t}{j}" for t in range(2) for j in range(4)]
    + [f"gh{i}" for i in range(4)]
    + [f"fb{r}{k}" for k in range(2) for r in range(2)]
    + ["pt00", "pt01", "pt10", "pt11", "pv0", "pt20", "pt21", "pv1", "pt30", "pt31", "pv2", "pv3"]
    + [f"ga{i}" for i in range(4)]
    + [f"ib{i}" for i in range(4)]
    + [f"uh{i}" for i in range(4)] + [f"ua{i}" for i in range(4)]
)
BANK = {g: n % 8 for n, g in enumerate(GROUPS)}
BANK |= {"wo00": 0, "wo01": 1, "wo10": 2, "th00": 4, "th01": 5, "wo11": 3, "th10": 6, "th11": 7,
         "lg": 4, "lt": 5, "rk": 6, "lp": 5, "ls": 4}
ORDER = list(BANK)
NTH = {g: sum(BANK[x] == BANK[g] for x in ORDER[:n + 1]) for n, g in enumerate(ORDER)}

LOADS = ["v", "q", "kv", "x1", "x2", "gh0", "gh1", "ga0", "ga1", "hu", "au", "wo0", "wo1"]
LAST_USE = ["z3", "q1", "kv1", "z7", "z11", "gh1", "gh3", "ga1", "ga3", "uh3", "ua3", "wo11", "wo11"]
PAIR_SLOT = [14, 10, 12]


def hybrid_block(nc, x, norm1_g, w_in, conv_w, conv_b, filt_w1, filt_b1, filt_freq1, filt_w2,
                 filt_b2, filt_freq2, filt_w3, filt_b3, hyena_d, q_norm_g, k_norm_g, w_hyena_up,
                 w_attn_up, w_out, norm2_g, router_w, router_b, expert_w1, expert_b1, expert_w2,
                 expert_b2, c_tab, c_dft, c_decay, out):
    with ExitStack() as ctx:
        def sb(name, shape, dt=F32):
            return ctx.enter_context(nc.sbuf_tensor(name, shape, dt))

        def sem(name):
            return ctx.enter_context(nc.semaphore(name))

        ps = ctx.enter_context(nc.psum_tensor("ps", [P, 8, 512], F32))

        ring = sb("ring", [P, NSLOT * SLOT])
        shared = sb("shared", [P, 14336])
        xh = sb("xh", [P, TT, D])
        tab = sb("tab", [P, C_FEAT])
        dft = sb("dft", [P, 4 * T])
        b1p = sb("b1p", [P, 2 * FF], BF16)
        selB = sb("selB", [P, 2, SLOTS], BF16)
        sel = sb("sel", [P, TT, 2 * SLOTS], BF16)
        gate = sb("gate", [P, TT, NE])
        rankm = sb("rankm", [P, TT, NE + 4])
        logit = sb("logit", [P, TT, NE])
        stat = sb("stat", [P, 64])
        smax = sb("smax", [P, 56])
        c16 = sb("c16", [P, 2 * P + 2], BF16)
        zlhs = sb("zlhs", [P, P], BF16)
        mask3 = sb("mask3", [P, TT, 3 * NE], BF16)
        over = sb("over", [P, 1], BF16)
        overf = sb("overf", [P, 1])
        pos = sb("pos", [P, 1])
        onehot = sb("onehot", [P, NLIST], BF16)
        rbias = sb("rbias", [NE, 1])
        mark = sb("mark", [P, 8])
        top8 = sb("top8", [P, TT, 8])
        idx8 = sb("idx8", [P, TT, 8], U32)
        idxf = sb("idxf", [P, TT, 8])
        olist = sb("olist", [1, 2 * NLIST + 8], I32)

        def ringw(slot, off, n, parts=P):
            return ring[0:parts, slot * SLOT + off:slot * SLOT + off + n]

        def sh(off, n, parts=P):
            return shared[0:parts, off:off + n]

        tri16, ones16, eb16 = c16[:, 0:P], c16[:, P:2 * P], c16[:, 2 * P:2 * P + 2]
        ident = tab[:, C_ID:C_ID + P]
        tri = tab[:, C_TRI:C_TRI + P]
        ones = tab[:, C_ONE:C_ONE + P]
        wk = [tab[:, C_WK + k:C_WK + k + 1] for k in range(2)]
        cs = [tab[:, C_COS + 32 * t:C_COS + 32 * t + 32] for t in range(2)]
        sn = [tab[:, C_SIN + 32 * t:C_SIN + 32 * t + 32] for t in range(2)]
        basis = [[dft[:, (2 * r + t) * T:(2 * r + t + 1) * T] for t in range(2)] for r in range(2)]

        decay = ringw(0, 0, 1024).rearrange("p (t n) -> p t n", t=2)
        dbc = ringw(0, 1024, 1024).rearrange("p (o n) -> p o n", o=2)
        fw3 = ringw(1, 0, 2048, FHID + 1)
        qz = ringw(1, 0, 2048).rearrange("p (h t) -> p h t", h=NH)
        zz = [ringw(2, 256 * i, 256) for i in range(8)] + [sh(12288 + 256 * i, 256) for i in range(4)]
        vT = ringw(3, 0, 1024).rearrange("p (t n) -> p t n", t=2)
        x1T = ringw(3, 1024, 1024).rearrange("p (t n) -> p t n", t=2)
        hk = ring[:, 4 * SLOT:6 * SLOT].rearrange("p (t o d n) -> p t o d n", t=2, o=2, d=2)
        probs = ring[:, 4 * SLOT:6 * SLOT].rearrange("p (t h s) -> p t h s", t=2, h=NH)
        g1b = ringw(4, 0, 1024)
        b1raw = ringw(3, 0, 2048, 96)
        u = ringw(6, 0, 2048).rearrange("p (t n) -> p t n", t=2)
        spec = ringw(6, 0, 2048).rearrange("p (r k n) -> p r k n", r=2, k=2)
        m7 = 7 * SLOT
        feats = ring[0:FEMB, m7:m7 + 256]
        h1 = ring[0:FHID, m7 + 256:m7 + 512]
        h2e = ring[0:FHID + 1, m7 + 512:m7 + 768]
        rope = ring[:, m7 + 768:m7 + 1280].rearrange("p (t a i) -> p t a i", t=2, a=8)
        kT = ring[:, m7 + 1280:m7 + 1536]
        vtok = ring[:, m7 + 1536:m7 + 1792].rearrange("p (t n) -> p t n", t=2)
        rows = ring[0:48, m7 + 1792:m7 + 1920]
        frow = ring[0:4, m7 + 1280:m7 + 1280 + FHID]
        fvec = ring[0:FHID, m7 + 1968:m7 + 1972]
        vecT = ring[:, m7 + 1920:m7 + 1968]
        m8_ = 8 * SLOT
        qn = [ring[:, m8_ + 640 * t:m8_ + 640 * t + 640].rearrange("p (h c) -> p h c", c=HD) for t in range(2)]
        mm4 = [ring[:, m8_ + 1280 + 256 * i:m8_ + 1536 + 256 * i].rearrange("p (h i) -> p h i", i=32) for i in range(4)]
        qr = [ring[:, m8_ + 2304 + 512 * t:m8_ + 2816 + 512 * t] for t in range(2)]
        kr = [ring[:, m8_ + 3328 + 128 * t:m8_ + 3456 + 128 * t] for t in range(2)]
        ptb = [ring[:, m8_ + 512 * i:m8_ + 512 * i + 512].rearrange("p (s t) -> p s t", s=2) for i in range(4)]
        fw1 = ring[0:FEMB, m8_ + 3584:m8_ + 3584 + 64]
        fw2 = ring[0:FHID, m8_ + 3648:m8_ + 3648 + 64]
        qkg = ring[:, m8_ + 3712:m8_ + 3840]
        farg = ring[0:FHID, m8_ + 3840:m8_ + 4096]
        kf = sh(0, 4096).rearrange("p (o r k n) -> p o r k n", o=2, r=2, k=2)
        ghy = sh(4096, 2048).rearrange("p (m t) -> p m t", m=8)
        gat = sh(6144, 2048).rearrange("p (m t) -> p m t", m=8)
        mT = sh(8192, 2048).rearrange("p (m t) -> p m t", m=8)
        uT = sh(10240, 2048).rearrange("p (k t) -> p k t", k=8)
        x2z = zz[8:12]
        yat = sh(13312, 1024).rearrange("p (j t) -> p j t", j=4)
        sq = [sh(4096 + 640 * t, 640) for t in range(2)]
        fsum = sh(8192, 2048).rearrange("p (t o n) -> p t o n", t=2, o=2)
        absf = sh(0, 4096).rearrange("p (t o d n) -> p t o d n", t=2, o=2, d=2)
        habs = sh(6144, 1024).rearrange("p (o n) -> p o n", o=2)
        rinv = sh(7168, 1024).rearrange("p (o n) -> p o n", o=2)
        prod = sh(8192, 2048).rearrange("p (i n) -> p i n", i=4)
        frnd = sh(12288, 256, FHID)
        parts = shared[:, 0:3072].bitcast(BF16).rearrange("p (a t n) -> p a t n", a=3, t=2)
        b2raw = sh(3072, 1024, 96)
        hn = sh(4096, 2048).rearrange("p (t n) -> p t n", t=2)
        junk = sh(12288, 512)
        hot = sh(12288, 256).rearrange("p (t r e) -> p t r e", t=2, r=TOPK)
        maskf = sh(12544, 64).rearrange("p (t e) -> p t e", t=2)
        hnT = sh(6144, 2048).rearrange("p (k t) -> p k t", k=8)
        glu = sh(6144, 512).rearrange("p (b n) -> p b n", b=2)
        lin = sh(6656, 512).rearrange("p (b n) -> p b n", b=2)
        sig = sh(7168, 512).rearrange("p (b n) -> p b n", b=2)
        hact = sh(7680, 512).rearrange("p (b n) -> p b n", b=2)
        xg = sh(8192, 2048).rearrange("p (b k s) -> p b k s", b=2, k=8)
        resid = [sh(10240, 1024), sh(8192, 1024)]
        yab = sh(10240, 1024).rearrange("p (w n) -> p w n", w=2)
        g2b = sh(11264, 1024)
        hT = sh(12288, 512).rearrange("p (f s) -> p f s", f=4)
        selG = sh(12800, 2 * 3 * SLOTS).rearrange("p (t s) -> p t s", t=2)
        gT = sh(13312, 512).rearrange("p (w t) -> p w t", w=4)
        b2p = dft[:, 0:512].bitcast(BF16)
        rw = dft[:, 512:768].rearrange("p (k e) -> p k e", k=8)
        lgT = dft[0:NE, 768:1024]
        filled = [sem(f"bank_filled{b}") for b in range(8)]
        drained = [sem(f"bank_drained{b}") for b in range(8)]
        in_x = [sem(f"in_x{t}") for t in range(TT)]
        in_tab = sem("in_tab")
        in_name = {n: sem("in_" + n) for n in
                   ("g1b", "feats", "rows", "fw1", "fw2", "fw3", "b3", "fvec", "decay", "dft", "dbc", "qkg", "b1", "rw", "rb", "g2b", "b2")}
        in_pair = [sem(f"in_pair{i}") for i in range(3)]
        dve_step = sem("dve_step")
        pool_step = sem("pool_step")
        x_ss = sem("x_sumsq")
        x_std = sem("x_std")
        x_var = sem("x_var")
        u_ready = sem("u_ready")
        f_arg = sem("filter_arg")
        f_out = sem("filter_sin")
        z_scaled = sem("z_scaled")
        abs_ready = sem("abs_ready")
        habs_ready = sem("habs_ready")
        hk_ready = sem("hk_ready")
        pm_ready = sem("filter_sums_ready")
        qk_sq = sem("qk_squared")
        qk_var = sem("qk_var")
        qk_std = sem("qk_std")
        qk_ready = sem("qk_rotated")
        qz_zero = sem("qz_zeroed")
        spec_ready = sem("spec_ready")
        mx_ready = sem("max_ready")
        p_exp = sem("probs_exp")
        p_ready = sem("probs_ready")
        b1_ready, b2_ready = sem("b1_parts_ready"), sem("b2_parts_ready")
        h_ss = sem("h_sumsq")
        h_var = sem("h_var")
        h_std = sem("h_std")
        hn_ready = sem("hn_ready")
        hi_ready, mid16_ready = sem("hi_ready"), sem("mid16_ready")
        lo_ready = [sem(f"lo_ready{t}") for t in range(2)]
        res_ready = [sem(f"residue_ready{t}") for t in range(2)]
        r_exp = sem("router_exp")
        r_max = sem("router_max")
        gate_ready = sem("gate_ready")
        mask_ready = sem("mask_ready")
        over_ready = sem("over_ready")
        pos_ready = sem("onehot_ready")
        list_ready = sem("list_ready")
        pads_ready = sem("pads_ready")
        ld = [sem(f"slot_loaded{s}") for s in range(NSLOT)]
        chunk_used = sem("chunk_used")
        t_full, t_free = sem("turn_full"), sem("turn_free")
        h_full, h_used = sem("hidden_full"), sem("hidden_used")
        y_full, y_used = sem("y_full"), sem("y_used")
        comb = sem("combined")
        added = sem("bank_combined")
        selb_ready, sel_ready, selg_ready = sem("bias_select"), sem("gather_select"), sem("combine_select")
        glu_ready, sig_ready, mid_ready, hact_ready = (
            sem("glu_ready"), sem("sig_ready"), sem("glulin_ready"), sem("hact_ready"))
        out_ready, out_stored = sem("out_ready"), sem("out_stored")

        def wait_filled(eng, g):
            eng.wait_ge(filled[BANK[g]], NTH[g])

        def wait_drained(eng, g):
            eng.wait_ge(drained[BANK[g]], NTH[g])

        def drains(ins, g):
            ins.then_inc(drained[BANK[g]], 1)

        def pair_of(n):
            s = PAIR_SLOT[n % 3]
            return ring[:, s * SLOT:(s + 2) * SLOT], 16 * (n // 3 + 1)

        def chunk_src(e, part):
            if part < 8:
                src = expert_w1[0, ds(e, 1), P * part:P * part + P, :]
                return src.rearrange("o p n -> (o p) n")
            m = part - 8
            src = expert_w2[0, ds(e, 1), 2 * P * m:2 * P * (m + 1), :]
            return src.rearrange("o (k p) n -> p (o k) n", k=2)

        def slot_dst(slot, part):
            dst = ring[:, slot * SLOT:(slot + 1) * SLOT]
            return dst if part < 8 else dst.rearrange("p (k n) -> p k n", k=2)

        def take_parts(eng, t):
            eng.wait_ge(hi_ready, t + 1)
            eng.tensor_tensor(resid[t], hn[:, t, :], parts[:, 0, t, :], ALU.subtract).then_inc(res_ready[t], 1)
            eng.wait_ge(mid16_ready, t + 1)
            eng.tensor_tensor(parts[:, 2, t, :], resid[t], parts[:, 1, t, :], ALU.subtract).then_inc(lo_ready[t], 1)
            eng.wait_ge(lo_ready[t], 1)

        NCH = NE * CHUNKS
        block = ctx.enter_context(nc.Block())

        @block.sync
        def _(sp):
            for t in range(TT):
                sp.dma_start(xh[:, t, :], x[0, P * t:P * t + P, :]).then_inc(in_x[t], 16)
            sp.dma_start(g1b, norm1_g.partition_broadcast(P)).then_inc(in_name["g1b"], 16)
            sp.dma_start(tab[:], c_tab[:, 0:C_FEAT]).then_inc(in_tab, 16)
            sp.dma_start(rows[0:36, :], conv_w[0].rearrange("a (c p) -> (a c) p", p=P)).then_inc(in_name["rows"], 16)
            sp.dma_start(rows[36:48, :], conv_b[0].rearrange("(c p) -> c p", p=P)).then_inc(in_name["rows"], 16)
            for i, v in enumerate((filt_b1, filt_freq1, filt_b2, filt_freq2)):
                sp.dma_start(frow[i:i + 1, :], v).then_inc(in_name["fvec"], 16)
            sp.dma_start(feats, c_tab[0:FEMB, C_FEAT:C_COLS]).then_inc(in_name["feats"], 16)
            sp.dma_start(fw1, filt_w1[0]).then_inc(in_name["fw1"], 16)
            sp.dma_start(fw2, filt_w2[0]).then_inc(in_name["fw2"], 16)
            cols = {"v": 0, "x1": HW, "x2": 2 * HW, "q": 3 * HW}
            c_kv = 3 * HW + NH * HD
            c_g = c_kv + 2 * NKV * HD
            for i in range(2):
                cols[f"gh{i}"] = c_g + 512 * i
                cols[f"ga{i}"] = c_g + D + 512 * i

            def load_pair(n):
                name = LOADS[n]
                dst, _ = pair_of(n)
                if n >= 3:
                    wait_filled(sp, LAST_USE[n - 3])
                done = in_pair[n % 3]
                if name == "kv":
                    sp.dma_start(dst[:, 0:2048].rearrange("p (k n) -> p k n", k=8),
                                 w_in[0, :, c_kv:c_kv + 256].rearrange("(k p) n -> p k n", p=P)).then_inc(done, 16)
                elif name in cols:
                    c = cols[name]
                    sp.dma_start(dst.rearrange("p (k n) -> p k n", k=8),
                                 w_in[0, :, c:c + 512].rearrange("(k p) n -> p k n", p=P)).then_inc(done, 16)
                elif name == "hu":
                    sp.dma_start(dst.rearrange("p (k n) -> p k n", k=4),
                                 w_hyena_up[0].rearrange("(k p) n -> p k n", p=P)).then_inc(done, 16)
                elif name == "au":
                    for g in range(NKV):
                        sp.dma_start(dst[HD * g:HD * g + HD, :].rearrange("p (j n) -> p j n", j=QPK),
                                     w_attn_up[0, g * QPK * HD:(g + 1) * QPK * HD, :]
                                     .rearrange("(j c) n -> c j n", c=HD)).then_inc(done, 16)
                else:
                    h = int(name[2])
                    sp.dma_start(dst.rearrange("p (k n) -> p k n", k=4),
                                 w_out[0, 512 * h:512 * h + 512, :].rearrange("(k p) n -> p k n", p=P)).then_inc(done, 16)

            def first(c):
                sp.dma_start(slot_dst(c, c % CHUNKS), chunk_src(c // CHUNKS, c % CHUNKS)).then_inc(ld[c], 16)

            def wait_used(e, before, part):
                if part == 7:
                    sp.wait_ge(h_full, e + 1)
                elif part == 11:
                    sp.wait_ge(y_full, e + 1)
                else:
                    sp.wait_ge(chunk_used, before + (part + 1 if part < 7 else part))

            for n in range(8):
                load_pair(n)
            wait_drained(sp, "z11")
            wait_drained(sp, "ia1")
            wait_filled(sp, "sc13")
            for c in (0, 1, 2):
                first(c)
            load_pair(8)
            wait_filled(sp, "fb11")
            first(3)
            load_pair(9)
            wait_filled(sp, "pv3")
            for c in (4, 5, 7, 8, 9):
                first(c)
            load_pair(10)
            wait_filled(sp, "ib3")
            first(6)
            sp.dma_start(rw, router_w[0].rearrange("(k p) e -> p k e", p=P)).then_inc(in_name["rw"], 16)
            sp.dma_start(rbias[:], router_b[0].unsqueeze(1)).then_inc(in_name["rb"], 16)
            sp.wait_ge(spec_ready, 8)
            for i in range(3):
                sp.dma_start(b2raw[32 * i:32 * i + 32, :], expert_b2[0]).then_inc(in_name["b2"], 16)
            sp.dma_start(g2b, norm2_g.partition_broadcast(P)).then_inc(in_name["g2b"], 16)
            load_pair(11)
            load_pair(12)
            for c in (10, 11):
                wait_filled(sp, LAST_USE[10])
                first(c)
            for c in (12, 13, 14, 15):
                wait_filled(sp, "wo11")
                first(c)
            with sp.Fori(0, TURNS - 1) as it:
                for c in range(GROUP * CHUNKS):
                    n = c + NSLOT
                    wait_used(it * GROUP + c // CHUNKS, it * (GROUP * 10) + 10 * (c // CHUNKS), c % CHUNKS)
                    sp.dma_start(slot_dst(n % NSLOT, n % CHUNKS),
                                 chunk_src(it * GROUP + n // CHUNKS, n % CHUNKS)).then_inc(ld[n % NSLOT], 16)
            for n in range((TURNS - 1) * GROUP * CHUNKS + NSLOT, NCH):
                e, part = divmod(n - NSLOT, CHUNKS)
                wait_used(e, 10 * e, part)
                sp.dma_start(slot_dst(n % NSLOT, n % CHUNKS), chunk_src(n // CHUNKS, n % CHUNKS)).then_inc(ld[n % NSLOT], 16)
            sp.wait_ge(list_ready, 1)
            n_over = sp.value_load(olist[0:1, 2 * NLIST:2 * NLIST + 1], min_val=0, max_val=NLIST)
            with sp.If(n_over > 0):
                with sp.Fori(0, n_over) as i:
                    e = sp.value_load(olist[0:1, ds(i, 1)], min_val=0, max_val=NE - 1)
                    sp.wait_ge(y_full, i + NE)
                    for c in range(CHUNKS):
                        sp.dma_start(slot_dst(c, c), chunk_src(e, c)).then_inc(ld[c], 16)
            for t in range(TT):
                for w in range(2):
                    half = slice(w * 512, (w + 1) * 512)
                    sp.wait_ge(out_ready, 2 * t + w + 1)
                    sp.dma_start(out[0, P * t:P * t + P, half], xh[:, t, half]).then_inc(out_stored, 16)
            sp.wait_ge(out_stored, 32 * TT)

        @block.tensor
        def _(pe):
            def begin(g):
                if NTH[g] > 1:
                    pe.wait_ge(drained[BANK[g]], NTH[g] - 1)
                return ps[:, BANK[g], :]

            def end(mm, g):
                mm.then_inc(filled[BANK[g]], 1)

            def pair(name, k):
                n = LOADS.index(name)
                words, count = pair_of(n)
                extra = 16 if (n % 3 == 1 and n >= 10) else 0
                pe.wait_ge(in_pair[n % 3], count + extra)
                return words.rearrange("p (k n) -> p k n", k=k)

            pe.wait_ge(in_tab, 16)
            pe.wait_ge(u_ready, 2)
            for i in range(4):
                bk = begin(f"uT{i}")
                for k in range(2):
                    for t in range(2):
                        mm = pe.transpose(bk[:, (2 * k + t) * P:(2 * k + t + 1) * P],
                                          u[:, t, (2 * i + k) * P:(2 * i + k + 1) * P], ident)
                end(mm, f"uT{i}")
            pe.wait_ge(in_name["rows"], 32)
            bk = begin("vec")
            end(pe.transpose(bk[:, 0:48], rows, ident[0:48, 0:48]), "vec")
            pe.wait_ge(in_name["fvec"], 64)
            bk = begin("fv")
            end(pe.transpose(bk[0:FHID, 0:4], frow, ident[0:4, 0:4]), "fv")
            pe.wait_ge(in_name["feats"], 16)
            pe.wait_ge(in_name["fw1"], 16)
            bk = begin("f1")
            end(pe.matmul(bk[0:FHID, 0:T], fw1, feats, start=True, stop=True), "f1")

            def project_cols(load, tiles, groups, per_bank, first=0):
                w = pair(load, 8)
                for i in range(first, tiles, per_bank):
                    g = groups[i // per_bank]
                    bk = begin(g)
                    for s in range(per_bank):
                        for k in range(KD):
                            mm = pe.matmul(bk[:, s * T:(s + 1) * T], w[:, k, (i + s) * P:(i + s + 1) * P],
                                           uT[:, k, :], start=(k == 0), stop=(k == KD - 1))
                    end(mm, g)

            for i in range(4):
                wait_drained(pe, f"uT{i}")
            project_cols("v", 1, ["z0"], 1)
            pe.wait_ge(in_name["fw2"], 16)
            pe.wait_ge(f_out, 1)
            bk = begin("f2")
            end(pe.matmul(bk[0:FHID, 0:T], fw2, h1, start=True, stop=True), "f2")
            project_cols("v", 4, [None, "z1", "z2", "z3"], 1, 1)

            pe.wait_ge(f_out, 2)
            pe.wait_ge(pads_ready, 1)
            pe.wait_ge(in_name["fw3"], 16)
            pe.wait_ge(in_name["b3"], 16)
            for t in range(2):
                for c in range(4):
                    g = f"h{t}{c}"
                    bk = begin(g)
                    end(pe.matmul(bk, h2e[:, t * P:(t + 1) * P], fw3[:, c * HW:(c + 1) * HW],
                                  start=True, stop=True), g)
            w = pair("q", 8)
            for t in range(2):
                bk = begin(f"q{t}")
                for k in range(KD):
                    mm = pe.matmul(bk, uT[:, k, t * P:(t + 1) * P], w[:, k, :], start=(k == 0), stop=(k == KD - 1))
                end(mm, f"q{t}")
            n = LOADS.index("kv")
            pe.wait_ge(in_pair[n % 3], pair_of(n)[1])
            w = pair_of(n)[0][:, 0:2048].rearrange("p (k n) -> p k n", k=8)
            for t in range(2):
                bk = begin(f"kv{t}")
                for k in range(KD):
                    mm = pe.matmul(bk[:, 0:256], uT[:, k, t * P:(t + 1) * P], w[:, k, :], start=(k == 0), stop=(k == KD - 1))
                end(mm, f"kv{t}")
            pe.wait_ge(habs_ready, 1)
            for o in range(2):
                bk = begin(f"nrm{o}")
                end(pe.matmul(bk, ones, habs[:, o, :], start=True, stop=True), f"nrm{o}")
            pe.wait_ge(pm_ready, 8)
            pe.wait_ge(in_name["dft"], 16)
            for o in range(2):
                for k in range(2):
                    for r in range(2):
                        g = f"kf{o}{r}{k}"
                        bk = begin(g)
                        for t in range(2):
                            src = fsum[:, t, o, :] if r == 0 else hk[:, t, o, 1, :]
                            mm = pe.matmul(bk, basis[r][t][:, k * P:(k + 1) * P], src, start=(t == 0), stop=(t == 1))
                        end(mm, g)
            project_cols("x1", 4, [f"z{i}" for i in range(4, 8)], 1)

            def turn_z(groups, first):
                for i in range(4):
                    wait_drained(pe, f"z{first + i}")
                for t in range(2):
                    bk = begin(groups[t])
                    for i in range(4):
                        mm = pe.transpose(bk[:, i * P:(i + 1) * P], zz[first + i][:, t * P:(t + 1) * P], ident)
                    end(mm, groups[t])

            def forward(prefix, y):
                for k in range(2):
                    for r in range(2):
                        g = f"{prefix}{r}{k}"
                        bk = begin(g)
                        for t in range(2):
                            mm = pe.matmul(bk, basis[r][t][:, k * P:(k + 1) * P], y[:, t, :], start=(t == 0), stop=(t == 1))
                        end(mm, g)

            turn_z(["tv0", "tv1"], 0)
            wait_drained(pe, "tv0")
            wait_drained(pe, "tv1")
            forward("fa", vT)
            turn_z(["tx0", "tx1"], 4)
            pe.wait_ge(qk_ready, 4)
            for t in range(2):
                bk = begin(f"tq{t}")
                for j in range(4):
                    mm = pe.transpose(bk[:, j * P:(j + 1) * P], qr[t][:, j * P:(j + 1) * P], ident)
                end(mm, f"tq{t}")
            bk = begin("tk")
            for t in range(2):
                mm = pe.transpose(bk[:, t * P:(t + 1) * P], kr[t], ident)
            end(mm, "tk")
            project_cols("x2", 4, [f"z{i}" for i in range(8, 12)], 1)
            pe.wait_ge(spec_ready, 4)
            for t in range(2):
                bk = begin(f"ia{t}")
                for n, (r, k) in enumerate([(r, k) for k in range(2) for r in range(2)]):
                    mm = pe.matmul(bk, basis[r][k][:, t * P:(t + 1) * P], spec[:, r, k, :], start=(n == 0), stop=(n == 3))
                end(mm, f"ia{t}")
            for t in range(2):
                wait_drained(pe, f"tq{t}")
            wait_drained(pe, "tk")
            for t in range(2):
                for j in range(4):
                    g = f"sc{t}{j}"
                    bk = begin(g)
                    for h in range(2):
                        mm = pe.matmul(bk[:, h * T:(h + 1) * T], qz[:, h * QPK + j, t * P:(t + 1) * P], kT,
                                       start=True, stop=True)
                    end(mm, g)
            for i in range(2):
                project_cols(f"gh{i}", 4, [f"gh{2 * i}", f"gh{2 * i + 1}"], 2)
            wait_drained(pe, "ia0")
            wait_drained(pe, "ia1")
            forward("fb", vT)

            def turn_probs(j, h):
                g = f"pt{j}{h}"
                pe.wait_ge(p_ready, 8)
                bk = begin(g)
                for s in range(2):
                    for t in range(2):
                        mm = pe.transpose(bk[:, s * T + t * P:s * T + (t + 1) * P],
                                          probs[:, t, h * QPK + j, s * P:(s + 1) * P], ident)
                end(mm, g)

            def attend(j):
                bk = begin(f"pv{j}")
                for h in range(2):
                    wait_drained(pe, f"pt{j}{h}")
                for s in range(2):
                    for h in range(2):
                        mm = pe.matmul(bk[h * HD:(h + 1) * HD, 0:T], vtok[:, s, h * HD:(h + 1) * HD],
                                       ptb[2 * (j % 2) + h][:, s, :], start=(s == 0), stop=(s == 1))
                end(mm, f"pv{j}")

            for h in range(2):
                turn_probs(0, h)
            for j in range(4):
                if j + 1 < 4:
                    for h in range(2):
                        turn_probs(j + 1, h)
                attend(j)
            for i in range(2):
                project_cols(f"ga{i}", 4, [f"ga{2 * i}", f"ga{2 * i + 1}"], 2)
            pe.wait_ge(spec_ready, 8)
            for i in range(4):
                bk = begin(f"ib{i}")
                for n, (r, k) in enumerate([(r, k) for k in range(2) for r in range(2)]):
                    mm = pe.matmul(bk[:, 0:T], spec[:, r, k, i * P:(i + 1) * P], basis[r][k], start=(n == 0), stop=(n == 3))
                end(mm, f"ib{i}")

            def up(load, groups, src, made):
                w = pair(load, 4)
                for i in range(4):
                    bk = begin(groups[i])
                    for s in range(2):
                        for k in range(4):
                            m = 2 * i + s
                            if m == 0:
                                wait_drained(pe, f"{made}{k}")
                            mm = pe.matmul(bk[:, s * T:(s + 1) * T], w[:, k, m * P:(m + 1) * P], src[k],
                                           start=(k == 0), stop=(k == 3))
                    end(mm, groups[i])

            up("hu", [f"uh{i}" for i in range(4)], x2z, "ib")
            up("au", [f"ua{i}" for i in range(4)], [yat[:, j, :] for j in range(4)], "pv")
            wa, wb = pair("wo0", 4), pair("wo1", 4)

            def project_out(t, h):
                g = f"wo{t}{h}"
                bk = begin(g)
                for k in range(KD):
                    if k % 2 == 0 and (t, h) == (0, 0):
                        wait_drained(pe, f"ua{k // 2}")
                    w = wa if k < 4 else wb
                    mm = pe.matmul(bk, mT[:, k, t * P:(t + 1) * P], w[:, k % 4, h * 512:(h + 1) * 512],
                                   start=(k == 0), stop=(k == KD - 1))
                end(mm, g)

            def turn_hn(t):
                pe.wait_ge(hn_ready, t + 1)
                for i in range(2):
                    g = f"th{t}{i}"
                    bk = begin(g)
                    for k in range(4):
                        kk = 4 * i + k
                        mm = pe.transpose(bk[:, k * P:(k + 1) * P], hn[:, t, kk * P:(kk + 1) * P], ident)
                    end(mm, g)

            project_out(0, 0)
            project_out(0, 1)
            project_out(1, 0)
            turn_hn(0)
            project_out(1, 1)
            turn_hn(1)
            for t in range(2):
                for i in range(2):
                    wait_drained(pe, f"th{t}{i}")
            pe.wait_ge(in_name["rw"], 16)
            bk = begin("lg")
            for k in range(KD):
                mm = pe.matmul(bk[0:NE, 0:T], rw[:, k, :], hnT[:, k, :], start=(k == 0), stop=(k == KD - 1))
            end(mm, "lg")
            for g in ("wo00", "wo01", "wo10", "wo11"):
                wait_drained(pe, g)
            pe.wait_ge(b1_ready, 1)
            pe.wait_ge(pads_ready, 1)
            for b in range(4):
                mm = pe.matmul(ps[:, b, :], zlhs[:], b1p[:, 0:512], start=True, stop=False, skip_group_check=True)
            mm.then_inc(comb, 1)
            wait_drained(pe, "lg")
            bk = begin("lt")
            for t in range(2):
                mm = pe.transpose(bk[:, t * NE:(t + 1) * NE], lgT[:, t * P:(t + 1) * P], ident[0:NE, 0:NE])
            end(mm, "lt")
            pe.wait_ge(mask_ready, 1)
            bk = begin("rk")
            pe.matmul(bk[:, 0:NE], tri16, mask3[:, 0, 0:NE], start=True, stop=True)
            pe.matmul(bk[:, NE:2 * NE], ones16, mask3[:, 0, 0:NE], start=True, stop=False)
            pe.matmul(bk[:, NE:2 * NE], tri16, mask3[:, 1, 0:NE], start=False, stop=True)
            pe.matmul(bk[0:96, 64:65], mask3[:, 0, :], ones16[:, 0:1], start=True, stop=False)
            end(pe.matmul(bk[0:96, 64:65], mask3[:, 1, :], ones16[:, 0:1], start=False, stop=True), "rk")
            hid = ps[:, 4:6, :]
            ybk = ps[:, 6, :]
            tbk = ps[:, 7, :]
            acc = [[ps[:, 2 * t + w, :] for w in range(2)] for t in range(2)]
            def gather(buf, half, use, ready):
                pe.wait_ge(sel_ready, ready)
                pe.wait_ge(t_free, use)
                for k in range(4):
                    kk = 4 * half + k
                    for t in range(2):
                        for a in range(3):
                            mm = pe.matmul(tbk[:, k * P:(k + 1) * P], parts[:, a, t, kk * P:(kk + 1) * P],
                                           sel[:, t, :], start=(t == 0 and a == 0), stop=(t == 1 and a == 2))
                mm.then_inc(t_full, 1)

            def hidden(pos, c0, nth, count, selected, gathered, cols):
                pe.wait_ge(selb_ready, selected)
                pe.wait_ge(h_used, count)
                for b in range(2):
                    for h in range(2):
                        c = 2 * b + h
                        pe.matmul(hid[h * 64:(h + 1) * 64, b, :], selB[:, pos, :], b1p[:, c * 512:(c + 1) * 512],
                                  start=True, stop=False, skip_group_check=True)
                pe.wait_ge(t_free, gathered)
                for k in range(8):
                    slot = (c0 + k) % NSLOT
                    pe.wait_ge(ld[slot], nth[k])
                    w = ring[:, slot * SLOT:(slot + 1) * SLOT]
                    for b in range(2):
                        for h in range(2):
                            c = 2 * b + h
                            mm = pe.matmul(hid[h * 64:(h + 1) * 64, b, :], cols[:, k, :], w[:, c * 512:(c + 1) * 512],
                                           start=False, stop=(k == 7), skip_group_check=True)
                    if k < 7:
                        mm.then_inc(chunk_used, 1)
                mm.then_inc(h_full, 1)

            def turn_hidden(use, count):
                pe.wait_ge(hact_ready, count)
                pe.wait_ge(t_free, use)
                for i in range(4):
                    mm = pe.transpose(tbk[:, i * P:(i + 1) * P], hact[:, i // 2, (i % 2) * P:(i % 2 + 1) * P], ident)
                mm.then_inc(t_full, 1)

            def second(pos, odd, c0, nth, count, turned):
                pe.wait_ge(y_used, count)
                for h in range(2):
                    wd = h ^ odd
                    pe.matmul(ybk[h * 64:(h + 1) * 64, :], selB[:, pos, :], b2p[:, wd * 512:(wd + 1) * 512],
                              start=True, stop=False, skip_group_check=True)
                pe.wait_ge(t_free, turned)
                for m in range(4):
                    slot = (c0 + 8 + m) % NSLOT
                    pe.wait_ge(ld[slot], nth[8 + m])
                    w = ring[:, slot * SLOT:(slot + 1) * SLOT].rearrange("p (k n) -> p k n", k=2)
                    for kk in range(2):
                        f = 2 * m + kk
                        b, half, r = f // 4, (f // 2) % 2, f % 2
                        lhs = hT[:, 2 * b + r, half * 64:(half + 1) * 64]
                        for h in range(2):
                            wd = h ^ odd
                            mm = pe.matmul(ybk[h * 64:(h + 1) * 64, :], lhs, w[:, kk, wd * 512:(wd + 1) * 512],
                                           start=False, stop=(f == 7), skip_group_check=True)
                    if m < 3:
                        mm.then_inc(chunk_used, 1)
                    else:
                        mm.then_inc(y_full, 1)

            def turn_gates(use, count):
                pe.wait_ge(selg_ready, count)
                pe.wait_ge(t_free, use)
                for w in range(2):
                    for t in range(2):
                        mm = pe.transpose(tbk[:, (2 * w + t) * P:(2 * w + t + 1) * P],
                                          selG[:, t, w * SLOTS:(w + 2) * SLOTS], ident)
                mm.then_inc(t_full, 1)

            def combine(ready, turned):
                pe.wait_ge(y_used, ready)
                pe.wait_ge(t_free, turned)
                for t in range(2):
                    for w in range(2):
                        pe.matmul(acc[t][w], gT[:, 2 * w + t, :], yab[:, w, :], start=False, stop=False,
                                  skip_group_check=True).then_inc(comb if t and w else added, 1)

            for t in range(2):
                pe.wait_ge(lo_ready[t], 1)
            wait_drained(pe, "th11")
            gather(0, 0, 1, 1)
            pe.wait_ge(over_ready, 1)
            bk = begin("lp")
            end(pe.matmul(bk[0:96, 0:1], tri16[0:96, 0:96], over[0:96, :], start=True, stop=True), "lp")
            gather(0, 1, 2, 1)
            pe.wait_ge(pos_ready, 1)
            bk = begin("ls")
            pe.matmul(bk[0:1, 0:NLIST], eb16[0:96, 0:1], onehot[0:96, :], start=True, stop=True)
            pe.matmul(bk[0:1, NLIST:2 * NLIST], eb16[0:96, 1:2], onehot[0:96, :], start=True, stop=True)
            end(pe.matmul(bk[0:1, 2 * NLIST:2 * NLIST + 1], over[0:96, :], ones16[0:96, 0:1], start=True, stop=True), "ls")
            for g in ("rk", "lp", "ls"):
                wait_drained(pe, g)
            pe.wait_ge(b2_ready, 1)
            with pe.Fori(0, TURNS) as it:
                use = it * 10 + 3
                for j in range(GROUP):
                    c0 = CHUNKS * j
                    nth = [it * 48 + 16 * ((c0 + k) // NSLOT + 1) for k in range(CHUNKS)]
                    e1 = it * GROUP + (j + 1)
                    hidden(j % 2, c0, nth, e1, e1, use, xg[:, j // 2, :, (j % 2) * SLOTS:(j % 2 + 1) * SLOTS])
                    if j == 0:
                        turn_gates(use, it * 2 + 1)
                        gather(1, 0, use + 1, it * 2 + 2)
                        use = use + 2
                    elif j == 1:
                        gather(1, 1, use, it * 2 + 2)
                        use = use + 1
                    elif j == 2:
                        combine(it * 4 + 3, it * 10 + 4)
                        turn_gates(use, it * 2 + 2)
                        use = use + 1
                    else:
                        gather(0, 0, use, it * 2 + 3)
                        gather(0, 1, use + 1, it * 2 + 3)
                        use = use + 2
                    turn_hidden(use, e1)
                    use = use + 1
                    second(j % 2, j % 2, c0, nth, e1, use)
                combine(it * 4 + 5, it * 10 + 9)

            pe.wait_ge(list_ready, 1)
            n_over = pe.value_load(olist[0:1, 2 * NLIST:2 * NLIST + 1], min_val=0, max_val=NLIST)
            OU = 2 + 10 * TURNS + 1
            with pe.If(n_over > 0):
                with pe.Fori(0, n_over) as i:
                    use = i * 4 + OU
                    gather(0, 0, use, i + (2 * TURNS + 2))
                    gather(0, 1, use + 1, i + (2 * TURNS + 2))
                    nth = [i * 16 + 16 * (NCH // NSLOT + 1)] * CHUNKS
                    hidden(0, 0, nth, i + (NE + 1), i + (NE + 2), use + 2, xg[:, 0, :, 0:SLOTS])
                    turn_gates(use + 2, i + (2 * TURNS + 1))
                    turn_hidden(use + 3, i + (NE + 1))
                    second(0, 0, 0, nth, i + (NE + 1), use + 4)
                    pe.wait_ge(y_used, i + (NE + 2))
                    for t in range(2):
                        for w in range(2):
                            pe.matmul(acc[t][w], gT[w * 64:(w + 1) * 64, 2 * w + t, :],
                                      yab[w * 64:(w + 1) * 64, w, :], start=False, stop=False,
                                      skip_group_check=True).then_inc(comb if t and w else added, 1)

        @block.scalar
        def _(act):
            for t in range(2):
                act.wait_ge(in_x[t], 16)
                act.activation(u[:, t, :], xh[:, t, :], ACT.Square, accum_out=stat[:, t:t + 1]).then_inc(x_ss, 1)
            act.wait_ge(x_var, 1)
            act.activation(stat[:, 4:6], stat[:, 2:4], ACT.Sqrt).then_inc(x_std, 1)
            act.dma_start(fw3[0:FHID, :], filt_w3[0]).then_inc(in_name["fw3"], 16)
            act.dma_start(fw3[FHID:FHID + 1, :], filt_b3).then_inc(in_name["b3"], 16)
            act.dma_start(decay.rearrange("p t n -> p (t n)"), c_decay).then_inc(in_name["decay"], 16)
            act.dma_start(dft[:], c_dft).then_inc(in_name["dft"], 16)
            for o in range(2):
                act.dma_start(dbc[:, o, :], hyena_d[0, o:o + 1, :].partition_broadcast(P)).then_inc(in_name["dbc"], 16)
            act.dma_start(qkg[:, 0:64], q_norm_g.partition_broadcast(P)).then_inc(in_name["qkg"], 16)
            act.dma_start(qkg[:, 64:128], k_norm_g.partition_broadcast(P)).then_inc(in_name["qkg"], 16)
            for g in range(3):
                act.dma_start(b1raw[32 * g:32 * g + 32, :], expert_b1[0]).then_inc(in_name["b1"], 16)
            for i in range(4):
                wait_filled(act, f"uT{i}")
                drains(act.copy(uT[:, 2 * i:2 * i + 2, :].rearrange("p k t -> p (k t)"), ps[:, BANK[f"uT{i}"], :]), f"uT{i}")
            act.wait_ge(f_arg, 1)
            act.activation(h1, farg, ACT.Sin).then_inc(f_out, 1)

            def scale_z(i):
                wait_drained(act, "vec")
                wait_filled(act, f"z{i}")
                act.activation(zz[i], ps[:, BANK[f"z{i}"], 0:T], ACT.Identity,
                               bias=vecT[:, 36 + i:37 + i], scale=vecT[:, 12 + i:13 + i]).then_inc(z_scaled, 1)

            scale_z(0)
            act.wait_ge(f_arg, 2)
            act.activation(h2e[0:FHID, :], farg, ACT.Sin).then_inc(f_out, 1)
            for i in range(1, 4):
                scale_z(i)
            act.wait_ge(hk_ready, 2)
            for t in range(2):
                for c in range(4):
                    wait_drained(act, f"h{t}{c}")
                act.activation(absf[:, t], hk[:, t], ACT.Abs).then_inc(abs_ready, 1)
            for t in range(2):
                wait_filled(act, f"q{t}")
                act.activation(sq[t][:, 0:512], ps[:, BANK[f"q{t}"], :], ACT.Square).then_inc(qk_sq, 1)
            for t in range(2):
                wait_filled(act, f"kv{t}")
                act.activation(sq[t][:, 512:640], ps[:, BANK[f"kv{t}"], 0:128], ACT.Square).then_inc(qk_sq, 1)
            act.wait_ge(qk_var, 1)
            act.activation(stat[:, 28:48], stat[:, 8:28], ACT.Sqrt).then_inc(qk_std, 1)
            for i in range(4, 8):
                scale_z(i)
            act.wait_ge(b1_ready, 1)
            for g, dst in (("tv0", vT[:, 0, :]), ("tv1", vT[:, 1, :]), ("tx0", x1T[:, 0, :]), ("tx1", x1T[:, 1, :])):
                wait_filled(act, g)
                drains(act.copy(dst, ps[:, BANK[g], :]), g)
            act.wait_ge(qz_zero, 1)
            for t in range(2):
                g = f"tq{t}"
                wait_filled(act, g)
                src = ps[:, BANK[g], :].rearrange("p (j t) -> p j t", j=4)
                act.copy(qz[0:HD, 0:QPK, t * P:(t + 1) * P], src[0:HD])
                drains(act.copy(qz[HD:P, QPK:NH, t * P:(t + 1) * P], src[HD:P]), g)
            wait_filled(act, "tk")
            drains(act.copy(kT, ps[:, BANK["tk"], 0:T]), "tk")
            for i in range(8, 12):
                scale_z(i)
            for t in range(2):
                for j in range(4):
                    g, i = f"sc{t}{j}", 2 * (4 * t + j)
                    act.wait_ge(mx_ready, 4 * t + j + 1)
                    for h in range(2):
                        ins = act.activation(probs[:, t, h * QPK + j, :], ps[:, BANK[g], h * T:(h + 1) * T], ACT.Exp,
                                             bias=smax[:, i + h:i + h + 1], accum_out=smax[:, 16 + i + h:17 + i + h])
                    drains(ins, g)

            def open_gate(groups, dst):
                for i, g in enumerate(groups):
                    wait_filled(act, g)
                    drains(act.activation(dst[:, 2 * i:2 * i + 2, :].rearrange("p m t -> p (m t)"), ps[:, BANK[g], :], ACT.Sigmoid), g)

            open_gate([f"gh{i}" for i in range(4)], ghy)

            def take_probs(j):
                for h in range(2):
                    g = f"pt{j}{h}"
                    wait_filled(act, g)
                    drains(act.copy(ptb[2 * (j % 2) + h].rearrange("p s t -> p (s t)"), ps[:, BANK[g], :]), g)

            take_probs(0)
            take_probs(1)
            for j in range(4):
                wait_filled(act, f"pv{j}")
                drains(act.copy(yat[:, j, :], ps[:, BANK[f"pv{j}"], 0:T]), f"pv{j}")
                if j + 2 < 4:
                    take_probs(j + 2)
            open_gate([f"ga{i}" for i in range(4)], gat)
            for t in range(2):
                for w in range(2):
                    wait_drained(act, f"wo{t}{w}")
                    act.activation(junk, xh[:, t, w * 512:(w + 1) * 512], ACT.Square,
                                   accum_out=stat[:, 48 + 2 * t + w:49 + 2 * t + w]).then_inc(h_ss, 1)
                    act.wait_ge(h_ss, 2 * t + w + 1)
                act.wait_ge(h_var, t + 1)
                act.activation(stat[:, 54 + t:55 + t], stat[:, 52 + t:53 + t], ACT.Sqrt).then_inc(h_std, 1)
                act.wait_ge(hn_ready, t + 1)
                if t == 0:
                    act.copy(parts[:, 0, t, :], hn[:, t, :]).then_inc(hi_ready, 1)
                for i in range(2):
                    g = f"th{t}{i}"
                    wait_filled(act, g)
                    drains(act.copy(hnT[:, 4 * i:4 * i + 4, t * P:(t + 1) * P], ps[:, BANK[g], :].rearrange("p (k t) -> p k t", k=4)), g)
                if t == 1:
                    act.copy(parts[:, 0, t, :], hn[:, t, :]).then_inc(hi_ready, 1)
                act.wait_ge(res_ready[t], 1)
                act.copy(parts[:, 1, t, :], resid[t]).then_inc(mid16_ready, 1)
            act.wait_ge(r_max, 1)
            act.activation(gate[:], gate[:], ACT.Exp).then_inc(r_exp, 1)

            def take_turn(dst, count):
                act.wait_ge(t_full, count)
                act.copy(dst, ps[:, 7, :]).then_inc(t_free, 1)

            def gathered(buf, half):
                return xg[:, buf, 4 * half:4 * half + 4, :].rearrange("p k s -> p (k s)")

            gT_all = gT.rearrange("p w t -> p (w t)")
            hT_all = hT.rearrange("p f s -> p (f s)")

            def sigmoid(count):
                act.wait_ge(glu_ready, count)
                act.activation(sig, glu, ACT.Sigmoid, scale=ALPHA).then_inc(sig_ready, 1)

            take_turn(gathered(0, 0), 1)
            take_turn(gathered(0, 1), 2)
            with act.Fori(0, TURNS) as it:
                n = 3
                for j, takes in enumerate(([gT_all, gathered(1, 0), hT_all], [gathered(1, 1), hT_all],
                                           [gT_all, hT_all], [gathered(0, 0), gathered(0, 1), hT_all])):
                    sigmoid(it * GROUP + (j + 1))
                    for dst in takes:
                        take_turn(dst, it * 10 + n)
                        n += 1
            act.wait_ge(list_ready, 1)
            n_over = act.value_load(olist[0:1, 2 * NLIST:2 * NLIST + 1], min_val=0, max_val=NLIST)
            with act.If(n_over > 0):
                with act.Fori(0, n_over) as i:
                    base = 2 + 10 * TURNS
                    take_turn(gathered(0, 0), i * 4 + (base + 1))
                    take_turn(gathered(0, 1), i * 4 + (base + 2))
                    sigmoid(i + (NE + 1))
                    take_turn(gT_all, i * 4 + (base + 3))
                    take_turn(hT_all, i * 4 + (base + 4))

        @block.vector
        def _(v):
            steps = [0]

            def link(ins):
                steps[0] += 1
                ins.then_inc(dve_step, 1)
                v.wait_ge(dve_step, steps[0])

            link(v.memset(h2e[FHID:FHID + 1, :], 1.0))
            link(v.memset(rankm[:], -1.0))
            v.memset(zlhs[:], 0.0).then_inc(pads_ready, 1)

            def filter_arg(g, b, count):
                wait_filled(v, g)
                if count == 2:
                    v.wait_ge(f_out, 1)
                v.tensor_scalar(farg, ps[0:FHID, BANK[g], 0:T], fvec[:, b:b + 1], fvec[:, b + 1:b + 2], ALU.add, ALU.mult)\
                    .then_inc(drained[BANK[g]], 1)
                wait_drained(v, g)
                magic = 12582912.0
                link(v.tensor_scalar(frnd, farg, 0.15915494309, magic, ALU.mult, ALU.add))
                link(v.tensor_scalar(frnd, frnd, -magic, None, ALU.add))
                for part in (PI2_A, PI2_B, PI2_C):
                    link(v.scalar_tensor_tensor(farg, frnd, -part, farg, ALU.mult, ALU.add))
                v.tensor_scalar(farg, farg, PI_IN, -PI_IN, ALU.min, ALU.max).then_inc(f_arg, 1)

            v.wait_ge(x_ss, 2)
            v.tensor_scalar(stat[:, 2:4], stat[:, 0:2], 1.0 / D, EPS, ALU.mult, ALU.add).then_inc(x_var, 1)
            v.wait_ge(x_std, 1)
            link(v.reciprocal(stat[:, 6:8], stat[:, 4:6]))
            v.wait_ge(in_name["g1b"], 16)
            for t in range(2):
                v.scalar_tensor_tensor(u[:, t, :], xh[:, t, :], stat[:, 6 + t:7 + t], g1b, ALU.mult, ALU.mult).then_inc(u_ready, 1)
            v.wait_ge(u_ready, 2)
            wait_filled(v, "vec")
            drains(v.tensor_copy(vecT, ps[:, BANK["vec"], 0:48]), "vec")
            wait_filled(v, "fv")
            drains(v.tensor_copy(fvec, ps[0:FHID, BANK["fv"], 0:4]), "fv")
            wait_drained(v, "fv")
            filter_arg("f1", 0, 1)

            def outer_taps(i):
                v.wait_ge(z_scaled, i + 1)
                zp = ps[:, BANK[f"z{i}"], 0:T]
                link(v.scalar_tensor_tensor(zz[i][:, 1:T], zp[:, 0:T - 1], vecT[:, i:i + 1], zz[i][:, 1:T], ALU.mult, ALU.add))
                drains(v.scalar_tensor_tensor(zz[i][:, 0:T - 1], zp[:, 1:T], vecT[:, 24 + i:25 + i], zz[i][:, 0:T - 1],
                                              ALU.mult, ALU.add), f"z{i}")

            wait_drained(v, "vec")
            outer_taps(0)
            filter_arg("f2", 2, 2)
            for i in range(1, 4):
                outer_taps(i)
            v.wait_ge(in_name["decay"], 16)
            for t in range(2):
                for c in range(4):
                    g = f"h{t}{c}"
                    wait_filled(v, g)
                    drains(v.tensor_tensor(hk[:, t, c // 2, c % 2, :], ps[:, BANK[g], :], decay[:, t, :], ALU.mult), g)
                    if t == 0 and c % 2:
                        wait_drained(v, g)
                        v.memset(hk[0:1, 0, c // 2, 1, :], 0.0).then_inc(hk_ready, 1)
            v.wait_ge(abs_ready, 2)
            link(v.tensor_tensor(habs, absf[:, 0, :, 0, :], absf[:, 0, :, 1, :], ALU.add))
            link(v.tensor_tensor(habs, habs, absf[:, 1, :, 0, :], ALU.add))
            v.tensor_tensor(habs, habs, absf[:, 1, :, 1, :], ALU.add).then_inc(habs_ready, 1)
            v.wait_ge(in_name["qkg"], 32)
            link(v.tensor_copy(tri16, tri))
            link(v.memset(ones16, 1.0))
            link(v.tensor_copy(eb16, tab[:, C_E:C_E + 2]))
            for t in range(2):
                for a in range(2):
                    g = qkg[:, 64 * a:64 * a + 64].rearrange("p (i two) -> p two i", two=2)
                    scale = HD ** -0.5 if a == 0 else 1.0
                    for n, (eo, trig) in enumerate(((0, cs), (1, sn), (0, sn), (1, cs))):
                        ins = v.scalar_tensor_tensor(rope[:, t, 4 * a + n, :], g[:, eo, :], scale, trig[t], ALU.mult, ALU.mult)
            link(ins)
            v.wait_ge(qk_sq, 4)
            for t in range(2):
                link(v.tensor_reduce(stat[:, 8 + 10 * t:18 + 10 * t], sq[t].rearrange("p (h c) -> p h c", c=HD), AX.X, ALU.add))
            v.tensor_scalar(stat[:, 8:28], stat[:, 8:28], 1.0 / HD, EPS, ALU.mult, ALU.add).then_inc(qk_var, 1)
            v.wait_ge(qk_std, 1)
            link(v.reciprocal(stat[:, 8:28], stat[:, 28:48]))
            for t in range(2):
                rs = stat[:, 8 + 10 * t:18 + 10 * t].unsqueeze(2)
                drains(v.tensor_tensor(qn[t][:, 0:NH, :], ps[:, BANK[f"q{t}"], :].rearrange("p (h c) -> p h c", c=HD),
                                       rs[:, 0:NH, :].to_broadcast([P, NH, HD]), ALU.mult), f"q{t}")
                link(v.tensor_tensor(qn[t][:, NH:NH + NKV, :], ps[:, BANK[f"kv{t}"], 0:128].rearrange("p (h c) -> p h c", c=HD),
                                     rs[:, NH:NH + NKV, :].to_broadcast([P, NKV, HD]), ALU.mult))
                drains(v.tensor_copy(vtok[:, t, :], ps[:, BANK[f"kv{t}"], 128:256]), f"kv{t}")

            def rotate(src, heads, tables, dst):
                x0, x1 = src[:, :, 0::2], src[:, :, 1::2]
                m = [a[:, 0:heads, :] for a in mm4]
                for n, x in enumerate((x0, x1, x0, x1)):
                    ins = v.tensor_tensor(m[n], x, tables[:, n:n + 1, :].to_broadcast([P, heads, 32]), ALU.mult)
                link(ins)
                per = heads // NKV
                view = [a.rearrange("p (g j) i -> p g j i", g=NKV) for a in m]
                out_ = dst.rearrange("p (j g c) -> p g j c", g=NKV, j=per)
                link(v.tensor_tensor(out_[:, :, :, 0::2], view[0], view[1], ALU.subtract))
                v.tensor_tensor(out_[:, :, :, 1::2], view[2], view[3], ALU.add).then_inc(qk_ready, 1)
                done[0] += 1
                v.wait_ge(qk_ready, done[0])

            done = [0]
            for o in range(2):
                wait_filled(v, f"nrm{o}")
                drains(v.reciprocal(rinv[:, o, :], ps[:, BANK[f"nrm{o}"], :]), f"nrm{o}")
            v.wait_ge(in_name["dbc"], 32)
            for o in range(2):
                wait_drained(v, f"nrm{o}")
                for k in range(2):
                    for r in range(2):
                        g = f"kf{o}{r}{k}"
                        wait_filled(v, g)
                        drains(v.scalar_tensor_tensor(kf[:, o, r, k, :], ps[:, BANK[g], :], wk[k], rinv[:, o, :],
                                                      ALU.mult, ALU.mult), g)
                        if r == 0:
                            wait_drained(v, g)
                            link(v.scalar_tensor_tensor(kf[:, o, 0, k, :], dbc[:, o, :], wk[k], kf[:, o, 0, k, :],
                                                        ALU.mult, ALU.add))
            v.memset(qz, 0.0).then_inc(qz_zero, 1)
            for t in range(2):
                rotate(qn[t][:, 0:NH, :], NH, rope[:, t, 0:4, :], qr[t])
                for i in range(4 + 2 * t, 6 + 2 * t):
                    outer_taps(i)
                rotate(qn[t][:, NH:NH + NKV, :], NKV, rope[:, t, 4:8, :], kr[t])

            def filter_product(prefix, o):
                for k in range(2):
                    yr, ys = (ps[:, BANK[f"{prefix}{r}{k}"], :] for r in range(2))
                    kr_, ks = kf[:, o, 0, k, :], kf[:, o, 1, k, :]
                    wait_filled(v, f"{prefix}0{k}")
                    v.tensor_tensor(prod[:, 0, :], yr, kr_, ALU.mult).then_inc(dve_step, 1)
                    steps[0] += 1
                    drains(v.tensor_tensor(prod[:, 2, :], yr, ks, ALU.mult), f"{prefix}0{k}")
                    wait_filled(v, f"{prefix}1{k}")
                    link(v.tensor_tensor(prod[:, 1, :], ys, ks, ALU.mult))
                    drains(v.tensor_tensor(prod[:, 3, :], ys, kr_, ALU.mult), f"{prefix}1{k}")
                    v.tensor_tensor(spec[:, 0, k, :], prod[:, 0, :], prod[:, 1, :], ALU.subtract).then_inc(spec_ready, 1)
                    wait_drained(v, f"{prefix}1{k}")
                    v.tensor_tensor(spec[:, 1, k, :], prod[:, 2, :], prod[:, 3, :], ALU.add).then_inc(spec_ready, 1)
                    v.wait_ge(spec_ready, 4 * o + 2 * k + 2)

            wait_drained(v, "kf111")
            filter_product("fa", 0)
            for i in range(8, 12):
                outer_taps(i)
            for t in range(2):
                wait_drained(v, f"tx{t}")
                wait_filled(v, f"ia{t}")
                drains(v.tensor_tensor(vT[:, t, :], ps[:, BANK[f"ia{t}"], :], x1T[:, t, :], ALU.mult), f"ia{t}")

            def normalise(n):
                t, j = n // 4, n % 4
                wait_drained(v, f"sc{t}{j}")
                link(v.reciprocal(smax[:, 32 + 2 * (n % 4):34 + 2 * (n % 4)], smax[:, 16 + 2 * n:18 + 2 * n]))
                pr = probs[:, t, j::QPK, :]
                rs = smax[:, 32 + 2 * (n % 4):34 + 2 * (n % 4)].unsqueeze(2).to_broadcast([P, 2, T])
                v.tensor_tensor(pr, pr, rs, ALU.mult).then_inc(p_ready, 1)
                v.wait_ge(p_ready, n + 1)

            for n in range(8):
                g = f"sc{n // 4}{n % 4}"
                wait_filled(v, g)
                v.tensor_reduce(smax[:, 2 * n:2 * n + 2], ps[:, BANK[g], :].rearrange("p (h s) -> p h s", h=2), AX.X,
                                ALU.max, negate=True).then_inc(mx_ready, 1)
                if n >= 1:
                    normalise(n - 1)
            normalise(7)
            filter_product("fb", 1)
            for i in range(4):
                g = f"ib{i}"
                wait_filled(v, g)
                drains(v.tensor_tensor(x2z[i], ps[:, BANK[g], 0:T], x2z[i], ALU.mult), g)
            for i in range(4):
                g = f"uh{i}"
                wait_filled(v, g)
                wait_drained(v, f"gh{i}")
                drains(v.tensor_tensor(mT[:, 2 * i:2 * i + 2, :], ps[:, BANK[g], :].rearrange("p (m t) -> p m t", m=2),
                                       ghy[:, 2 * i:2 * i + 2, :], ALU.mult), g)
            for i in range(4):
                g = f"ua{i}"
                sl = slice(2 * i, 2 * i + 2)
                wait_filled(v, g)
                wait_drained(v, f"ga{i}")
                wait_drained(v, f"uh{i}")
                link(v.tensor_tensor(gat[:, sl, :], ps[:, BANK[g], :].rearrange("p (m t) -> p m t", m=2), gat[:, sl, :], ALU.mult))
                drains(v.tensor_tensor(mT[:, sl, :], mT[:, sl, :], gat[:, sl, :], ALU.add), g)
            for t in range(2):
                for w in range(2):
                    g = f"wo{t}{w}"
                    part = xh[:, t, w * 512:(w + 1) * 512]
                    wait_filled(v, g)
                    drains(v.tensor_tensor(part, ps[:, BANK[g], :], part, ALU.add), g)
                v.wait_ge(h_ss, 2 * t + 2)
                link(v.tensor_tensor(stat[:, 52 + t:53 + t], stat[:, 48 + 2 * t:49 + 2 * t], stat[:, 49 + 2 * t:50 + 2 * t], ALU.add))
                v.tensor_scalar(stat[:, 52 + t:53 + t], stat[:, 52 + t:53 + t], 1.0 / D, EPS, ALU.mult, ALU.add).then_inc(h_var, 1)
                v.wait_ge(h_std, t + 1)
                link(v.reciprocal(stat[:, 56 + t:57 + t], stat[:, 54 + t:55 + t]))
                v.wait_ge(in_name["g2b"], 16)
                v.scalar_tensor_tensor(hn[:, t, :], xh[:, t, :], stat[:, 56 + t:57 + t], g2b, ALU.mult, ALU.mult).then_inc(hn_ready, 1)
                v.wait_ge(hn_ready, t + 1)
                take_parts(v, t)
            wait_filled(v, "lg")
            v.wait_ge(in_name["rb"], 16)
            drains(v.tensor_scalar(lgT, ps[0:NE, BANK["lg"], 0:T], rbias[:], None, ALU.add), "lg")
            wait_filled(v, "lt")
            drains(v.tensor_copy(logit[:].rearrange("p t e -> p (t e)"), ps[:, BANK["lt"], 0:2 * NE]), "lt")
            wait_drained(v, "lt")
            for t in range(2):
                ins = v.max(top8[:, t, :], logit[:, t, :])
            link(ins)
            v.tensor_tensor(gate[:], logit[:], top8[:, :, 0:1].to_broadcast([P, TT, NE]), ALU.subtract).then_inc(r_max, 1)
            for t in range(2):
                ins = v.max_index(idx8[:, t, :], top8[:, t, :], logit[:, t, :])
            link(ins)
            link(v.tensor_copy(idxf[:], idx8[:]))
            for t in range(2):
                ins = v.tensor_tensor(hot[:, t], tab[:, C_IOE:C_IOE + NE].unsqueeze(1).to_broadcast([P, TOPK, NE]),
                                      idxf[:, t, 0:TOPK].unsqueeze(2).to_broadcast([P, TOPK, NE]), ALU.is_equal)
            link(ins)
            link(v.tensor_reduce(maskf, hot.rearrange("p t r e -> p t e r"), AX.X, ALU.add))
            v.tensor_copy(mask3[:].rearrange("p t (c e) -> p t c e", c=3), maskf.unsqueeze(2).to_broadcast([P, TT, 3, NE]))\
                .then_inc(mask_ready, 1)
            wait_filled(v, "rk")
            rk = ps[:, BANK["rk"], :]
            link(v.scalar_tensor_tensor(rankm[:, :, 0:NE], rk[:, 0:2 * NE].rearrange("p (t e) -> p t e", t=2), 1.0, maskf, ALU.add, ALU.mult))

            def overflow_list():
                v.tensor_scalar(overf[0:96, :], rk[0:96, 64:65], tab[0:96, C_BASE:C_BASE + 1], None, ALU.is_gt)\
                    .then_inc(drained[BANK["rk"]], 1)
                wait_drained(v, "rk")
                v.tensor_copy(over[0:96, :], overf[0:96, :]).then_inc(over_ready, 1)
                wait_filled(v, "lp")
                drains(v.tensor_copy(pos[0:96, :], ps[0:96, BANK["lp"], 0:1]), "lp")
                wait_drained(v, "lp")
                v.tensor_scalar(onehot[0:96, :], tab[0:96, C_IOL:C_IOL + NLIST], pos[0:96, :], overf[0:96, :],
                                ALU.is_equal, ALU.mult).then_inc(pos_ready, 1)
                wait_filled(v, "ls")
                drains(v.tensor_copy(olist[0:1, 0:2 * NLIST + 1], ps[0:1, BANK["ls"], 0:2 * NLIST + 1]), "ls")
                wait_drained(v, "ls")
                v.memset(mark[:, 3:4], 0.0).then_inc(list_ready, 1)

            iota = tab[:, C_IOTA:C_IOTA + T]
            iota0 = iota[:, 0:SLOTS]

            def select(e, block, first=iota0):
                for t in range(2):
                    ins = v.tensor_scalar(sel[:, t, block * SLOTS:(block + 1) * SLOTS], first, rankm[:, t, ds(e, 1)], None, ALU.is_equal)
                return ins

            def select_gates(e, block, first=iota0):
                for t in range(2):
                    ins = v.tensor_scalar(selG[:, t, block * SLOTS:(block + 1) * SLOTS], first, rankm[:, t, ds(e, 1)],
                                          gate[:, t, ds(e, 1)], ALU.is_equal, ALU.mult)
                return ins

            def select_bias(pos_, e):
                v.tensor_scalar(selB[:, pos_, :], ones[:, 0:SLOTS], tab[:, ds(e + C_ID3, 1)], None, ALU.mult).then_inc(selb_ready, 1)

            def swiglu(count):
                v.wait_ge(h_full, count)
                hid = ps[:, 4:6, :]
                v.tensor_scalar(glu, hid[:, :, 0::2], LIMIT, None, ALU.min).then_inc(glu_ready, 1)
                v.tensor_scalar(lin, hid[:, :, 1::2], LIMIT, -LIMIT, ALU.min, ALU.max).then_inc(h_used, 1)
                v.wait_ge(glu_ready, count)
                v.wait_ge(h_used, count + 1)
                v.scalar_tensor_tensor(lin, lin, 1.0, glu, ALU.add, ALU.mult).then_inc(mid_ready, 1)
                v.wait_ge(mid_ready, count)
                v.wait_ge(sig_ready, count)
                v.tensor_tensor(hact, lin, sig, ALU.mult).then_inc(hact_ready, 1)

            def take_y(odd, count, combined):
                v.wait_ge(comb, combined)
                v.wait_ge(y_full, count)
                v.tensor_copy(yab[0:64, odd, :], ps[0:64, 6, :])
                v.tensor_copy(yab[64:P, 1 - odd, :], ps[64:P, 6, :]).then_inc(y_used, 1)

            select(0, 0)
            select(1, 1).then_inc(sel_ready, 1)
            v.memset(mark[:, 0:1], 0.0).then_inc(t_free, 1)
            v.memset(mark[:, 1:2], 0.0).then_inc(h_used, 1)
            v.memset(mark[:, 2:3], 0.0).then_inc(y_used, 1)
            select_bias(0, 0)
            overflow_list()
            v.wait_ge(r_exp, 1)
            link(v.tensor_tensor(gate[:], gate[:], maskf, ALU.mult))
            link(v.tensor_reduce(smax[:, 50:52], gate[:], AX.X, ALU.add))
            link(v.reciprocal(smax[:, 52:54], smax[:, 50:52]))
            v.tensor_tensor(gate[:], gate[:], smax[:, 52:54].unsqueeze(2).to_broadcast([P, TT, NE]), ALU.mult).then_inc(gate_ready, 1)
            v.wait_ge(gate_ready, 1)
            with v.Fori(0, TURNS) as it:
                e = it * GROUP
                v.wait_ge(t_full, it * 10 + 2)
                select(e + 2, 0)
                select(e + 3, 1).then_inc(sel_ready, 1)
                select_gates(e, 0)
                select_gates(e + 1, 1)
                select_gates(e, 2).then_inc(selg_ready, 1)
                for j in range(GROUP):
                    select_bias((j + 1) % 2, e + (j + 1))
                    swiglu(e + (j + 1))
                    take_y(j % 2, e + (j + 1), it * 2 + (j // 2 + 1))
                    if j == 1:
                        select(e + 4, 0)
                        select(e + 5, 1).then_inc(sel_ready, 1)
                        select_gates(e + 2, 0)
                        select_gates(e + 3, 1)
                        select_gates(e + 2, 2).then_inc(selg_ready, 1)
            n_over = v.value_load(olist[0:1, 2 * NLIST:2 * NLIST + 1], min_val=0, max_val=NLIST)
            with v.If(n_over > 0):
                with v.Fori(0, n_over) as i:
                    e = v.value_load(olist[0:1, ds(i, 1)], min_val=0, max_val=NE - 1)
                    base = v.value_load(olist[0:1, ds(i + NLIST, 1)], min_val=0, max_val=T - SLOTS)
                    v.wait_ge(comb, i + (NE // 2 + 1))
                    window = iota[:, ds(base, SLOTS)]
                    select(e, 0, window).then_inc(sel_ready, 1)
                    select_gates(e, 0, window)
                    select_gates(e, 2, window).then_inc(selg_ready, 1)
                    select_bias(0, e)
                    swiglu(i + (NE + 1))
                    take_y(0, i + (NE + 1), i + (NE // 2 + 1))
            for t in range(2):
                for w in range(2):
                    if t and w:
                        v.wait_ge(comb, n_over + (NE // 2 + 1))
                    else:
                        v.wait_ge(added, n_over * 3 + (3 * (NE // 2 - 1) + 2 * t + w + 1))
                    part = xh[:, t, w * 512:(w + 1) * 512]
                    v.tensor_tensor(part, ps[:, 2 * t + w, :], part, ALU.add).then_inc(out_ready, 1)

        @block.gpsimd
        def _(pool):
            def link(ins, n):
                ins.then_inc(pool_step, 1)
                pool.wait_ge(pool_step, n)

            count = [0]

            def step(ins):
                count[0] += 1
                link(ins, count[0])

            def split(out_, raw, done):
                step(pool.memset(out_[96:P, :], 0.0))
                step(pool.tensor_copy(out_[0:96, :], raw))
                step(pool.tensor_tensor(raw, raw, out_[0:96, :], ALU.subtract))
                step(pool.tensor_copy(out_[32:64, :], raw[32:64, :]))
                step(pool.tensor_copy(out_[64:96, :], raw[64:96, :]))
                pool.tensor_tensor(out_[64:96, :], raw[64:96, :], out_[64:96, :], ALU.subtract).then_inc(done, 1)
                pool.wait_ge(done, 1)

            for t in range(2):
                pool.wait_ge(abs_ready, t + 1)
                for o in range(2):
                    f, b = hk[:, t, o, 0, :], hk[:, t, o, 1, :]
                    pool.tensor_tensor(fsum[:, t, o, :], f, b, ALU.add).then_inc(pm_ready, 1)
                    pool.wait_ge(pm_ready, 4 * t + 2 * o + 1)
                    pool.tensor_tensor(b, f, b, ALU.subtract).then_inc(pm_ready, 1)
                    pool.wait_ge(pm_ready, 4 * t + 2 * o + 2)
            pool.wait_ge(in_name["b1"], 48)
            split(b1p, b1raw, b1_ready)
            pool.wait_ge(in_name["b2"], 48)
            split(b2p, b2raw, b2_ready)


_INS = ["x", "norm1_g", "w_in", "conv_w", "conv_b", "filt_w1", "filt_b1", "filt_freq1", "filt_w2",
        "filt_b2", "filt_freq2", "filt_w3", "filt_b3", "hyena_d", "q_norm_g", "k_norm_g",
        "w_hyena_up", "w_attn_up", "w_out", "norm2_g", "router_w", "router_b", "expert_w1",
        "expert_b1", "expert_w2", "expert_b2"]


def kernel(**inputs):
    import numpy as _np
    import concourse.bacc as _bacc
    from concourse import mybir as _mybir
    from concourse.bass_utils import run_bass_kernel_spmd as _run

    nc = _bacc.Bacc("TRN2", target_bir_lowering=False, num_devices=1)
    arrays, args = {}, []
    named = [(n, inputs[n]) for n in _INS]
    named += list(zip(("c_tab", "c_dft", "c_decay"), tables()))
    for name, value in named:
        a = _np.ascontiguousarray(value)
        arrays[f"in_{name}"] = a
        args.append(nc.dram_tensor(f"in_{name}", a.shape, _mybir.dt.from_np(a.dtype), kind="ExternalInput").ap())
    out = nc.dram_tensor("out_0", (1, T, D), F32, kind="ExternalOutput").ap()
    hybrid_block(nc, *args, out)
    r = _run(nc, [arrays], core_ids=[0])
    return r.results[0]["out_0"]
```

```python
from contextlib import ExitStack

import numpy as np

import concourse.bass as bass
from concourse import mybir
from concourse.alu_op_type import AluOpType as ALU

ACT = mybir.ActivationFunctionType
AX = mybir.AxisListType
F32 = mybir.dt.float32
F32R = mybir.dt.float32r
BF16 = mybir.dt.bfloat16
I32 = mybir.dt.int32
U32 = mybir.dt.uint32
ds = bass.ds

P = 128
T = 256
TT = T // P
D = 1024
KD = D // P
HW = 512
NH, NKV, HD = 8, 2, 64
QPK = NH // NKV
NE, TOPK = 32, 4
FF = 1024
EPS = 1e-6
LIMIT, ALPHA = 7.0, 1.702
FEMB, FHID = 33, 64
NDFT = 2 * T - 1
SLOTS = 64
SLOT = 2048
NSLOT = 16
CHUNKS = 12
GROUP = 4
TURNS = NE // GROUP
NLIST = 32
NWIN = T // SLOTS
PI_IN = 3.1415925
PI2_A, PI2_B, PI2_C = 6.28125, 1.9340515136718750e-03, 1.2556659146e-06

C_ID, C_TRI, C_IOTA, C_WK = 0, 128, 256, 512
C_COS, C_SIN, C_IOL, C_E, C_BASE, C_ID4, C_ONE, C_IOE = 514, 578, 642, 674, 675, 676, 708, 836
C_FEAT = 868
C_COLS = C_FEAT + T


def tables():
    c = np.zeros((P, C_COLS), np.float32)
    c[:, C_ID:C_ID + P] = np.eye(P)
    c[:, C_TRI:C_TRI + P] = np.triu(np.ones((P, P)), 1)
    c[:, C_IOTA:C_IOTA + T] = 1 + np.arange(T)
    bins = np.full(T, 2.0 / NDFT)
    bins[0] = 1.0 / NDFT
    c[:, C_WK:C_WK + 2] = bins.reshape(2, P).T
    half = HD // 2
    freqs = np.float32(10000.0) ** (-np.arange(0, half, 2, dtype=np.float32) / half)
    row = np.repeat(np.arange(T // 64, dtype=np.float32), 64)
    col = np.tile(np.arange(64, dtype=np.float32), T // 64)
    ang = np.concatenate([row[:, None] * freqs, col[:, None] * freqs], -1).astype(np.float32)
    c[:, C_COS:C_COS + 64] = np.cos(ang).reshape(2, P, 32).transpose(1, 0, 2).reshape(P, 64)
    c[:, C_SIN:C_SIN + 64] = np.sin(ang).reshape(2, P, 32).transpose(1, 0, 2).reshape(P, 64)
    c[:, C_IOL:C_IOL + NLIST] = np.arange(NLIST)
    j = np.arange((NWIN - 1) * NE)
    c[:j.size, C_E] = j % NE
    c[:j.size, C_BASE] = SLOTS * (1 + j // NE)
    c[:, C_ID4:C_ID4 + NE] = np.tile(np.eye(NE), (P // NE, 1))
    c[:, C_ONE:C_ONE + P] = 1.0
    c[:, C_IOE:C_IOE + NE] = np.arange(NE)
    n = np.arange(T)
    w = 2 * np.pi * (np.outer(n, n) % NDFT) / NDFT
    dft = np.stack([np.cos(w), np.sin(w)]).astype(np.float32)
    dft = np.ascontiguousarray(dft.reshape(2, 2, P, T).transpose(2, 0, 1, 3)).reshape(P, 4 * T)
    f32 = np.float32
    t = np.linspace(0.0, 1.0, T, dtype=f32)[:, None]
    bands = (FEMB - 1) // 2
    wt = (f32(2.0 * np.pi) * np.arange(T, dtype=f32)[:, None] / f32(T)).astype(f32)
    fr = np.linspace(1e-4, bands - 1, bands, dtype=f32)[None, :]
    a = (wt * fr).astype(f32)
    feats = np.concatenate([t, np.cos(a), -np.sin(a)], -1).astype(f32)
    c[:FEMB, C_FEAT:C_FEAT + T] = feats.T
    lo, hi = np.log(1e-2) / 1.5, np.log(1e-2) / 0.3
    deltas = np.abs(np.linspace(lo, hi, HW, dtype=f32))
    decay = np.exp(-t * deltas).astype(f32)
    decay = np.ascontiguousarray(decay.reshape(2, P, HW).transpose(1, 0, 2)).reshape(P, 2 * HW)
    return c, dft, decay


GROUPS = (
    [f"uT{i}" for i in range(4)] + ["vec", "fv", "f1"] + ["z0", "z1", "f2", "z2", "z3"]
    + [f"h{t}{c}" for t in range(2) for c in range(4)]
    + ["q0", "q1", "kv0", "kv1"]
    + ["nrm0"] + [f"kf0{r}{k}" for k in range(2) for r in range(2)]
    + [f"z{i}" for i in range(4, 8)]
    + ["nrm1"] + [f"kf1{r}{k}" for k in range(2) for r in range(2)]
    + ["tv0", "tv1"] + [f"fa{r}{k}" for k in range(2) for r in range(2)]
    + ["tx0", "tx1", "tq0", "tq1", "tk"]
    + [f"z{i}" for i in range(8, 12)]
    + ["ia0", "ia1"] + [f"sc{t}{j}" for t in range(2) for j in range(4)]
    + [f"gh{i}" for i in range(4)]
    + [f"fb{r}{k}" for k in range(2) for r in range(2)]
    + ["pt00", "pt01", "pt10", "pt11", "pv0", "pt20", "pt21", "pv1", "pt30", "pt31", "pv2", "pv3"]
    + [f"ga{i}" for i in range(4)]
    + [f"ib{i}" for i in range(4)]
    + [f"uh{i}" for i in range(4)] + [f"ua{i}" for i in range(4)]
)
BANK = {g: n % 8 for n, g in enumerate(GROUPS)}
BANK |= {"wo00": 0, "wo01": 1, "wo10": 2, "th00": 4, "th01": 5, "wo11": 3, "th10": 6, "th11": 7,
         "lg": 4, "lt": 5, "rk": 6, "lp": 5, "ls": 4}
ORDER = list(BANK)
NTH = {g: sum(BANK[x] == BANK[g] for x in ORDER[:n + 1]) for n, g in enumerate(ORDER)}

UNITS = [("v0", "z1"), ("v1", "z3"), ("q0", "q0"), ("q1", "q1"), ("kv", "kv1"), ("x10", "z5"), ("x11", "z7"),
         ("x20", "z9"), ("x21", "z11")] + [(f"gh{i}", f"gh{i}") for i in range(4)] + [(f"ga{i}", f"ga{i}") for i in range(4)]
UNITS += [("hu0", "uh1"), ("hu1", "uh3"), ("au0", "ua1"), ("au1", "ua3")] + [(f"wo{i}", "wo11") for i in range(4)]
UNIT = {name: n for n, (name, _) in enumerate(UNITS)}
UNIT_RAW = (10, 11, 12) * 4 + (0, 1, 2, 10, 11) + (8, 9, 4, 5) + (10, 11, 12, 15)
UNIT_HI, U_LO = (13, 14), 15
UP_HI = 3
U_HI = 10240


def hybrid_block(nc, x, norm1_g, w_in, conv_w, conv_b, filt_w1, filt_b1, filt_freq1, filt_w2,
                 filt_b2, filt_freq2, filt_w3, filt_b3, hyena_d, q_norm_g, k_norm_g, w_hyena_up,
                 w_attn_up, w_out, norm2_g, router_w, router_b, expert_w1, expert_b1, expert_w2,
                 expert_b2, c_tab, c_dft, c_decay, out):
    with ExitStack() as ctx:
        def sb(name, shape, dt=F32):
            return ctx.enter_context(nc.sbuf_tensor(name, shape, dt))

        def sem(name):
            return ctx.enter_context(nc.semaphore(name))

        ps = ctx.enter_context(nc.psum_tensor("ps", [P, 8, 512], F32))

        ring_at = -(-nc.sbuf_base // 32) * 32
        ring = sb("ring", [P, NSLOT * SLOT])
        shared_at = -(-nc.sbuf_base // 32) * 32
        shared = sb("shared", [P, 14336])
        slotr = {s: nc.alloc_sbuf_tensor_at(f"slot{s}_parts", [P, SLOT], F32R, offset=ring_at + s * SLOT * 4)
                 for s in sorted({*UNIT_RAW, *UNIT_HI, U_LO, UP_HI})}
        mhir = nc.alloc_sbuf_tensor_at("merged_parts", [P, 2048], F32R, offset=shared_at + 6144 * 4)
        mlor = nc.alloc_sbuf_tensor_at("merged_rests", [P, 2048], F32R, offset=shared_at + 8192 * 4)
        restr = nc.alloc_sbuf_tensor_at("mixer_rests", [P, 2048], F32R, offset=shared_at + 12288 * 4)
        uparts = nc.alloc_sbuf_tensor_at("u_parts", [P, 2048], F32R, offset=shared_at + U_HI * 4)
        xh = sb("xh", [P, TT, D])
        tab = sb("tab", [P, C_FEAT])
        dft = sb("dft", [P, 4 * T])
        b1p = sb("b1p", [P, 2 * FF], BF16)
        selB = sb("selB", [P, 2, SLOTS], BF16)
        sel = sb("sel", [P, TT, 2 * SLOTS], BF16)
        gate = sb("gate", [P, TT, NE])
        rankm = sb("rankm", [P, TT, NE + 4])
        stat = sb("stat", [P, 64])
        smax = sb("smax", [P, 56])
        c16 = sb("c16", [P, 2 * P + 2], BF16)
        zlhs = sb("zlhs", [P, P], BF16)
        mask3 = sb("mask3", [P, TT, 3 * NE], BF16)
        over = sb("over", [P, 1], BF16)
        overf = sb("overf", [P, 1])
        pos = sb("pos", [P, 1])
        onehot = sb("onehot", [P, NLIST], BF16)
        rbias = sb("rbias", [P, 1])
        mark = sb("mark", [P, 8])
        top8 = sb("top8", [P, TT, 8])
        idx8 = sb("idx8", [P, TT, 8], U32)
        idxf = sb("idxf", [P, TT, 8])
        olist = sb("olist", [1, 2 * NLIST + 8], I32)

        def ringw(slot, off, n, parts=P):
            return ring[0:parts, slot * SLOT + off:slot * SLOT + off + n]

        def sh(off, n, parts=P):
            return shared[0:parts, off:off + n]

        tri16, ones16, eb16 = c16[:, 0:P], c16[:, P:2 * P], c16[:, 2 * P:2 * P + 2]
        ident = tab[:, C_ID:C_ID + P]
        tri = tab[:, C_TRI:C_TRI + P]
        ones = tab[:, C_ONE:C_ONE + P]
        wk = [tab[:, C_WK + k:C_WK + k + 1] for k in range(2)]
        cs = [tab[:, C_COS + 32 * t:C_COS + 32 * t + 32] for t in range(2)]
        sn = [tab[:, C_SIN + 32 * t:C_SIN + 32 * t + 32] for t in range(2)]
        basis = [[dft[:, (2 * r + t) * T:(2 * r + t + 1) * T] for t in range(2)] for r in range(2)]

        decay = ringw(0, 0, 1024).rearrange("p (t n) -> p t n", t=2)
        dbc = ringw(0, 1024, 1024).rearrange("p (o n) -> p o n", o=2)
        fw3 = ringw(1, 0, 2048, FHID + 1)
        qz = ringw(1, 0, 2048).rearrange("p (h t) -> p h t", h=NH)
        zz = [ringw(2, 256 * i, 256) for i in range(8)] + [sh(12288 + 256 * i, 256) for i in range(4)]
        vT = ringw(3, 0, 1024).rearrange("p (t n) -> p t n", t=2)
        x1T = ringw(3, 1024, 1024).rearrange("p (t n) -> p t n", t=2)
        hk = ring[:, 4 * SLOT:6 * SLOT].rearrange("p (t o d n) -> p t o d n", t=2, o=2, d=2)
        probs = ring[:, 4 * SLOT:6 * SLOT].rearrange("p (t h s) -> p t h s", t=2, h=NH)
        g1b = ringw(4, 0, 1024)
        u = ringw(6, 0, 2048).rearrange("p (t n) -> p t n", t=2)
        spec = ringw(6, 0, 2048).rearrange("p (r k n) -> p r k n", r=2, k=2)
        m7 = 7 * SLOT
        feats = ring[0:FEMB, m7:m7 + 256]
        h1 = ring[0:FHID, m7 + 256:m7 + 512]
        h2e = ring[0:FHID + 1, m7 + 512:m7 + 768]
        rope = ring[:, m7 + 768:m7 + 1280].rearrange("p (t a i) -> p t a i", t=2, a=8)
        kT = ring[:, m7 + 1280:m7 + 1536]
        vtok = ring[:, m7 + 1536:m7 + 1792].rearrange("p (t n) -> p t n", t=2)
        rows = ring[0:48, m7 + 1792:m7 + 1920]
        frow = ring[0:4, m7 + 1280:m7 + 1280 + FHID]
        fvec = ring[0:FHID, m7 + 1968:m7 + 1972]
        vecT = ring[:, m7 + 1920:m7 + 1968]
        m8_ = 8 * SLOT
        qn = [ring[:, m8_ + 640 * t:m8_ + 640 * t + 640].rearrange("p (h c) -> p h c", c=HD) for t in range(2)]
        mm4 = [ring[:, m8_ + 1280 + 256 * i:m8_ + 1536 + 256 * i].rearrange("p (h i) -> p h i", i=32) for i in range(4)]
        qr = [ring[:, m8_ + 2304 + 512 * t:m8_ + 2816 + 512 * t] for t in range(2)]
        kr = [ring[:, m8_ + 3328 + 128 * t:m8_ + 3456 + 128 * t] for t in range(2)]
        ptb = [ring[:, m8_ + 512 * i:m8_ + 512 * i + 512].rearrange("p (s t) -> p s t", s=2) for i in range(4)]
        fw1 = ring[0:FEMB, m8_ + 3584:m8_ + 3584 + 64]
        fw2 = ring[0:FHID, m8_ + 3648:m8_ + 3648 + 64]
        qkg = ring[:, m8_ + 3712:m8_ + 3840]
        farg = ring[0:FHID, m8_ + 3840:m8_ + 4096]
        kf = sh(0, 4096).rearrange("p (o r k n) -> p o r k n", o=2, r=2, k=2)
        ghy = sh(4096, 2048).rearrange("p (m t) -> p m t", m=8)
        gat = sh(6144, 2048).rearrange("p (m t) -> p m t", m=8)
        mT = sh(8192, 2048).rearrange("p (m t) -> p m t", m=8)
        uhi = uparts[:].rearrange("p (k t) -> p k t", k=8)
        ulo = slotr[U_LO][:].rearrange("p (k t) -> p k t", k=8)
        x2z = zz[8:12]
        mhi = mhir[:].rearrange("p (m t) -> p m t", m=8)
        mlo = mlor[:].rearrange("p (m t) -> p m t", m=8)
        x2hi, yhi = (slotr[UP_HI][:, 1024 * a:1024 * a + 1024].rearrange("p (k t) -> p k t", k=4) for a in range(2))
        x2lo, ylo = (restr[:, 1024 * a:1024 * a + 1024].rearrange("p (k t) -> p k t", k=4) for a in range(2))
        sq = [sh(4096 + 640 * t, 640) for t in range(2)]
        fsum = sh(8192, 2048).rearrange("p (t o n) -> p t o n", t=2, o=2)
        absf = sh(0, 4096).rearrange("p (t o d n) -> p t o d n", t=2, o=2, d=2)
        habs = sh(6144, 1024).rearrange("p (o n) -> p o n", o=2)
        rinv = sh(7168, 1024).rearrange("p (o n) -> p o n", o=2)
        prod = sh(8192, 2048).rearrange("p (i n) -> p i n", i=4)
        frnd = sh(12288, 256, FHID)
        b1raw = sh(4096, 2048, 96)
        parts = shared[:, 0:3072].bitcast(BF16).rearrange("p (a t n) -> p a t n", a=3, t=2)
        b2raw = sh(3072, 1024, 96)
        hn = sh(4096, 2048).rearrange("p (t n) -> p t n", t=2)
        junk = sh(12288, 512)
        hot = sh(12288, 256).rearrange("p (t r e) -> p t r e", t=2, r=TOPK)
        maskf = sh(12544, 64).rearrange("p (t e) -> p t e", t=2)
        hnT = sh(6144, 2048).rearrange("p (k t) -> p k t", k=8)
        glu = sh(6144, 512).rearrange("p (b n) -> p b n", b=2)
        lin = sh(6656, 512).rearrange("p (b n) -> p b n", b=2)
        sig = sh(7168, 512).rearrange("p (b n) -> p b n", b=2)
        hact = sh(7680, 512).rearrange("p (b n) -> p b n", b=2)
        xg = sh(8192, 2048).rearrange("p (b k s) -> p b k s", b=2, k=8)
        resid = [sh(10240, 1024), sh(8192, 1024)]
        yab = sh(10240, 1024).rearrange("p (w n) -> p w n", w=2)
        g2b = sh(11264, 1024)
        hT = sh(12288, 512).rearrange("p (f s) -> p f s", f=4)
        selG = sh(12800, 2 * 3 * SLOTS).rearrange("p (t s) -> p t s", t=2)
        gT = sh(13312, 512).rearrange("p (w t) -> p w t", w=4)
        b2p = dft[:, 0:512].bitcast(BF16)
        rw = dft[:, 512:768].rearrange("p (k e) -> p k e", k=8)
        lgT = dft[:, 768:1024]
        filled = [sem(f"bank_filled{b}") for b in range(8)]
        drained = [sem(f"bank_drained{b}") for b in range(8)]
        in_x = [sem(f"in_x{t}") for t in range(TT)]
        in_ident = sem("in_ident")
        in_tab = sem("in_tab")
        in_name = {n: sem("in_" + n) for n in
                   ("g1b", "feats", "rows", "fw1", "fw2", "fw3", "b3", "fvec", "decay", "dft", "dbc", "qkg", "b1", "rw", "rb", "g2b", "b2")}
        in_unit = [sem(f"in_unit{i}") for i in range(8)]
        unit_hi, unit_lo = sem("unit_rounded"), [sem(f"unit_rest{i}") for i in range(2)]
        tile_hi, tile_lo = sem("first_tile_rounded"), sem("first_tile_rest")
        uhi_ready = sem("u_rounded")
        x2_hi, x2_lo = sem("hyena_out_rounded"), sem("hyena_out_rest")
        y_hi = sem("attention_out_rounded")
        m_hi, m_lo = sem("merged_rounded"), sem("merged_rest")
        out_used = sem("unit_wo_used")
        q_left = sem("unit_q0_used")
        dve_step = sem("dve_step")
        pool_step = sem("pool_step")
        x_ss = sem("x_sumsq")
        x_std = sem("x_std")
        x_var = sem("x_var")
        u_ready = sem("u_ready")
        f_arg = sem("filter_arg")
        f_out = sem("filter_sin")
        z_scaled = sem("z_scaled")
        abs_ready = sem("abs_ready")
        habs_ready = sem("habs_ready")
        hk_ready = sem("hk_ready")
        pm_ready = sem("filter_sums_ready")
        qk_sq = sem("qk_squared")
        qk_var = sem("qk_var")
        qk_std = sem("qk_std")
        qk_ready = sem("qk_rotated")
        qz_zero = sem("qz_zeroed")
        spec_ready = sem("spec_ready")
        mx_ready = sem("max_ready")
        p_ready = sem("probs_ready")
        b1_ready, b2_ready = sem("b1_parts_ready"), sem("b2_parts_ready")
        h_ss = sem("h_sumsq")
        h_var = sem("h_var")
        h_std = sem("h_std")
        hn_ready = sem("hn_ready")
        hi_ready, mid16_ready = sem("hi_ready"), sem("mid16_ready")
        lo_ready = [sem(f"lo_ready{t}") for t in range(2)]
        res_ready = [sem(f"residue_ready{t}") for t in range(2)]
        r_exp = sem("router_exp")
        gate_ready = sem("gate_ready")
        mask_ready = sem("mask_ready")
        over_ready = sem("over_ready")
        pos_ready = sem("onehot_ready")
        list_ready = sem("list_ready")
        pads_ready = sem("pads_ready")
        ld = [sem(f"slot_loaded{s}") for s in range(NSLOT)]
        chunk_used = sem("chunk_used")
        t_full, t_free = sem("turn_full"), sem("turn_free")
        h_full, h_used = sem("hidden_full"), sem("hidden_used")
        y_full, y_used = sem("y_full"), sem("y_used")
        comb = sem("combined")
        added = sem("bank_combined")
        selb_ready, sel_ready, selg_ready = sem("bias_select"), sem("gather_select"), sem("combine_select")
        glu_ready, sig_ready, mid_ready, hact_ready = (
            sem("glu_ready"), sem("sig_ready"), sem("glulin_ready"), sem("hact_ready"))
        out_ready, out_stored = sem("out_ready"), sem("out_stored")

        def wait_filled(eng, g):
            eng.wait_ge(filled[BANK[g]], NTH[g])

        def wait_drained(eng, g):
            eng.wait_ge(drained[BANK[g]], NTH[g])

        def drains(ins, g):
            ins.then_inc(drained[BANK[g]], 1)

        def unit_raw(n):
            return ringw(UNIT_RAW[n], 0, 2048)

        def unit_parts(n):
            return [slotr[s][:] for s in (UNIT_HI[n % 2], UNIT_RAW[n])]

        def wait_unit_used(eng, n):
            if UNITS[n][0] == "q0":
                eng.wait_ge(q_left, 1)
            elif UNITS[n][0] in ("wo0", "wo1", "wo2"):
                eng.wait_ge(out_used, int(UNITS[n][0][2]) + 1)
            else:
                wait_filled(eng, UNITS[n][1])

        def chunk_src(e, part):
            if part < 8:
                src = expert_w1[0, ds(e, 1), P * part:P * part + P, :]
                return src.rearrange("o p n -> (o p) n")
            m = part - 8
            src = expert_w2[0, ds(e, 1), 2 * P * m:2 * P * (m + 1), :]
            return src.rearrange("o (k p) n -> p (o k) n", k=2)

        def slot_dst(slot, part):
            dst = ring[:, slot * SLOT:(slot + 1) * SLOT]
            return dst if part < 8 else dst.rearrange("p (k n) -> p k n", k=2)

        def take_parts(eng, t):
            eng.wait_ge(hi_ready, t + 1)
            eng.tensor_tensor(resid[t], hn[:, t, :], parts[:, 0, t, :], ALU.subtract).then_inc(res_ready[t], 1)

        def third_part(eng, t):
            eng.wait_ge(mid16_ready, t + 1)
            eng.tensor_tensor(parts[:, 2, t, :], resid[t], parts[:, 1, t, :], ALU.subtract).then_inc(lo_ready[t], 1)
            eng.wait_ge(lo_ready[t], 1)

        def tile_of(words, i):
            return words.rearrange("p (k n) -> p k n", k=KD)[:, :, i * P:(i + 1) * P]

        def rest_of_unit(eng, n):
            eng.wait_ge(unit_hi, n + 1)
            rounded, rest = unit_parts(n)
            eng.tensor_tensor(rest, unit_raw(n), rounded.bitcast(F32), ALU.subtract).then_inc(unit_lo[n % 2], 1)

        NCH = NE * CHUNKS
        block = ctx.enter_context(nc.Block())

        @block.sync
        def _(sp):
            for t in range(TT):
                sp.dma_start(xh[:, t, :], x[0, P * t:P * t + P, :]).then_inc(in_x[t], 16)
            sp.dma_start(g1b, norm1_g.partition_broadcast(P)).then_inc(in_name["g1b"], 16)
            sp.dma_start(ident, c_tab[:, C_ID:C_ID + P]).then_inc(in_ident, 16)
            c_kv = 3 * HW + NH * HD
            c_g = c_kv + 2 * NKV * HD
            cols = {"v": 0, "x1": HW, "x2": 2 * HW, "q": 3 * HW, "gh": c_g, "ga": c_g + D}

            def load_unit(n):
                name = UNITS[n][0]
                if UNIT_RAW[n] in UNIT_RAW[:n]:
                    wait_unit_used(sp, max(m for m in range(n) if UNIT_RAW[m] == UNIT_RAW[n]))
                done = in_unit[n % 8]
                if name[:2] == "wo":
                    i = int(name[2])
                    sp.dma_start(unit_raw(n).rearrange("p (k n) -> p k n", k=2),
                                 w_out[0, 256 * i:256 * i + 256, :].rearrange("(k p) n -> p k n", p=P)).then_inc(done, 16)
                    return
                if name[1] == "u":
                    half = slice(512 * int(name[2]), 512 * int(name[2]) + 512)
                    dst = unit_raw(n).rearrange("p (k n) -> p k n", k=4)
                    if name[0] == "h":
                        sp.dma_start(dst, w_hyena_up[0, :, half].rearrange("(k p) n -> p k n", p=P)).then_inc(done, 16)
                        return
                    for g in range(NKV):
                        sp.dma_start(dst[HD * g:HD * g + HD], w_attn_up[0, g * QPK * HD:(g + 1) * QPK * HD, half]
                                     .rearrange("(j c) n -> c j n", c=HD)).then_inc(done, 16)
                    return
                c = c_kv if name == "kv" else cols[name[:-1]] + 256 * int(name[-1])
                sp.dma_start(unit_raw(n).rearrange("p (k n) -> p k n", k=8),
                             w_in[0, :, c:c + 256].rearrange("(k p) n -> p k n", p=P)).then_inc(done, 16)

            def first(c):
                sp.dma_start(slot_dst(c, c % CHUNKS), chunk_src(c // CHUNKS, c % CHUNKS)).then_inc(ld[c], 16)

            def wait_used(e, before, part):
                if part == 7:
                    sp.wait_ge(h_full, e + 1)
                elif part == 11:
                    sp.wait_ge(y_full, e + 1)
                else:
                    sp.wait_ge(chunk_used, before + (part + 1 if part < 7 else part))

            load_unit(0)
            sp.dma_start(rows[0:36, :], conv_w[0].rearrange("a (c p) -> (a c) p", p=P)).then_inc(in_name["rows"], 16)
            sp.dma_start(rows[36:48, :], conv_b[0].rearrange("(c p) -> c p", p=P)).then_inc(in_name["rows"], 16)
            for i, v in enumerate((filt_b1, filt_freq1, filt_b2, filt_freq2)):
                sp.dma_start(frow[i:i + 1, :], v).then_inc(in_name["fvec"], 16)
            sp.dma_start(feats, c_tab[0:FEMB, C_FEAT:C_COLS]).then_inc(in_name["feats"], 16)
            sp.dma_start(fw1, filt_w1[0]).then_inc(in_name["fw1"], 16)
            sp.dma_start(tab[:, P:], c_tab[:, P:C_FEAT]).then_inc(in_tab, 16)
            sp.dma_start(fw2, filt_w2[0]).then_inc(in_name["fw2"], 16)
            for n in range(1, 12):
                load_unit(n)
            wait_drained(sp, "z11")
            wait_drained(sp, "ia1")
            wait_filled(sp, "sc13")
            for n in range(12, 17):
                load_unit(n)
            wait_filled(sp, "gh3")
            first(0)
            wait_filled(sp, "pv3")
            for n in range(17, 21):
                load_unit(n)
            first(7)
            for c, g in ((1, "ga0"), (2, "ga1")):
                wait_filled(sp, g)
                first(c)
            wait_filled(sp, "ga3")
            for n in range(21, 25):
                load_unit(n)
            sp.dma_start(rbias[0:NE, :], router_b[0].unsqueeze(1)).then_inc(in_name["rb"], 16)
            wait_filled(sp, "ib3")
            sp.dma_start(rw, router_w[0].rearrange("(k p) e -> p k e", p=P)).then_inc(in_name["rw"], 16)
            sp.wait_ge(spec_ready, 8)
            for i in range(3):
                sp.dma_start(b2raw[32 * i:32 * i + 32, :], expert_b2[0]).then_inc(in_name["b2"], 16)
            sp.dma_start(g2b, norm2_g.partition_broadcast(P)).then_inc(in_name["g2b"], 16)
            first(6)
            for c, g in ((8, "uh1"), (9, "uh3"), (4, "ua1"), (5, "ua3"), (3, "ua3")):
                wait_filled(sp, g)
                first(c)
            for c in (10, 11, 12, 15, 13, 14):
                wait_unit_used(sp, max(n for n in range(len(UNITS)) if c in (UNIT_RAW[n], UNIT_HI[n % 2])))
                first(c)
            with sp.Fori(0, TURNS - 1) as it:
                for c in range(GROUP * CHUNKS):
                    n = c + NSLOT
                    wait_used(it * GROUP + c // CHUNKS, it * (GROUP * 10) + 10 * (c // CHUNKS), c % CHUNKS)
                    sp.dma_start(slot_dst(n % NSLOT, n % CHUNKS),
                                 chunk_src(it * GROUP + n // CHUNKS, n % CHUNKS)).then_inc(ld[n % NSLOT], 16)
            for n in range((TURNS - 1) * GROUP * CHUNKS + NSLOT, NCH):
                e, part = divmod(n - NSLOT, CHUNKS)
                wait_used(e, 10 * e, part)
                sp.dma_start(slot_dst(n % NSLOT, n % CHUNKS), chunk_src(n // CHUNKS, n % CHUNKS)).then_inc(ld[n % NSLOT], 16)
            sp.wait_ge(list_ready, 1)
            n_over = sp.value_load(olist[0:1, 2 * NLIST:2 * NLIST + 1], min_val=0, max_val=NLIST)
            with sp.If(n_over > 0):
                with sp.Fori(0, n_over) as i:
                    e = sp.value_load(olist[0:1, ds(i, 1)], min_val=0, max_val=NE - 1)
                    sp.wait_ge(y_full, i + NE)
                    for c in range(CHUNKS):
                        sp.dma_start(slot_dst(c, c), chunk_src(e, c)).then_inc(ld[c], 16)
            for t in range(TT):
                for w in range(2):
                    half = slice(w * 512, (w + 1) * 512)
                    sp.wait_ge(out_ready, 2 * t + w + 1)
                    sp.dma_start(out[0, P * t:P * t + P, half], xh[:, t, half]).then_inc(out_stored, 16)
            sp.wait_ge(out_stored, 32 * TT)

        @block.tensor
        def _(pe):
            def begin(g):
                if NTH[g] > 1:
                    pe.wait_ge(drained[BANK[g]], NTH[g] - 1)
                return ps[:, BANK[g], :]

            def end(mm, g):
                mm.then_inc(filled[BANK[g]], 1)

            def unit(name, k=KD):
                n = UNIT[name]
                pe.wait_ge(unit_lo[n % 2], n // 2 + 1)
                return [a.rearrange("p (k n) -> p k n", k=k) for a in unit_parts(n)]

            pe.wait_ge(in_ident, 16)
            for t in range(2):
                pe.wait_ge(u_ready, t + 1)
                for i in range(4):
                    bk = begin(f"uT{i}")
                    for k in range(2):
                        mm = pe.transpose(bk[:, (2 * k + t) * P:(2 * k + t + 1) * P],
                                          u[:, t, (2 * i + k) * P:(2 * i + k + 1) * P], ident)
                    if t == 1:
                        end(mm, f"uT{i}")
            pe.wait_ge(in_name["rows"], 32)
            bk = begin("vec")
            end(pe.transpose(bk[:, 0:48], rows, ident[0:48, 0:48]), "vec")
            pe.wait_ge(in_name["fvec"], 64)
            bk = begin("fv")
            end(pe.transpose(bk[0:FHID, 0:4], frow, ident[0:4, 0:4]), "fv")
            pe.wait_ge(in_name["feats"], 16)
            pe.wait_ge(in_name["fw1"], 16)
            bk = begin("f1")
            end(pe.matmul(bk[0:FHID, 0:T], fw1, feats, start=True, stop=True), "f1")

            def project_tile(w, i, out_):
                whi, wlo = (a[:, :, i * P:(i + 1) * P] for a in w)
                for k in range(KD):
                    if out_ is z0_bank and k % 2 == 0:
                        wait_drained(pe, f"uT{k // 2}")
                    pe.matmul(out_, wlo[:, k, :], uhi[:, k, :], start=(k == 0), stop=False)
                    pe.matmul(out_, whi[:, k, :], ulo[:, k, :], start=False, stop=False)
                    mm = pe.matmul(out_, whi[:, k, :], uhi[:, k, :], start=False, stop=(k == KD - 1))
                return mm

            def project_z(name, first):
                w = unit(name)
                for i in range(2):
                    g = f"z{first + i}"
                    end(project_tile(w, i, begin(g)[:, 0:T]), g)

            def project_gate(g):
                w = unit(g)
                bk = begin(g)
                for i in range(2):
                    mm = project_tile(w, i, bk[:, i * T:(i + 1) * T])
                end(mm, g)

            def project_rows(w, t, out_):
                whi, wlo = w
                tok = slice(t * P, (t + 1) * P)
                for k in range(KD):
                    pe.matmul(out_, uhi[:, k, tok], wlo[:, k, :], start=(k == 0), stop=False)
                    pe.matmul(out_, ulo[:, k, tok], whi[:, k, :], start=False, stop=False)
                    mm = pe.matmul(out_, uhi[:, k, tok], whi[:, k, :], start=False, stop=(k == KD - 1))
                return mm

            pe.wait_ge(tile_lo, 1)
            z0_bank = begin("z0")[:, 0:T]
            end(project_tile([a.rearrange("p (k n) -> p k n", k=KD) for a in unit_parts(0)], 0, z0_bank), "z0")
            z0_bank = None
            end(project_tile(unit("v0"), 1, begin("z1")[:, 0:T]), "z1")
            pe.wait_ge(in_name["fw2"], 16)
            pe.wait_ge(f_out, 1)
            bk = begin("f2")
            end(pe.matmul(bk[0:FHID, 0:T], fw2, h1, start=True, stop=True), "f2")
            project_z("v1", 2)

            pe.wait_ge(f_out, 2)
            pe.wait_ge(pads_ready, 1)
            pe.wait_ge(in_name["fw3"], 16)
            pe.wait_ge(in_name["b3"], 16)
            for t in range(2):
                for c in range(4):
                    g = f"h{t}{c}"
                    bk = begin(g)
                    end(pe.matmul(bk, h2e[:, t * P:(t + 1) * P], fw3[:, c * HW:(c + 1) * HW],
                                  start=True, stop=True), g)
            w = unit("q0")
            for t in range(2):
                mm = project_rows(w, t, begin(f"q{t}")[:, 0:256])
            mm.then_inc(q_left, 1)
            w = unit("q1")
            for t in range(2):
                end(project_rows(w, t, ps[:, BANK[f"q{t}"], 256:512]), f"q{t}")
            w = unit("kv")
            for t in range(2):
                end(project_rows(w, t, begin(f"kv{t}")[:, 0:256]), f"kv{t}")
            pe.wait_ge(in_tab, 16)
            pe.wait_ge(habs_ready, 1)
            pe.wait_ge(pm_ready, 8)
            pe.wait_ge(in_name["dft"], 16)

            def filter_spectrum(o):
                end(pe.matmul(begin(f"nrm{o}"), ones, habs[:, o, :], start=True, stop=True), f"nrm{o}")
                for k in range(2):
                    for r in range(2):
                        g = f"kf{o}{r}{k}"
                        bk = begin(g)
                        for t in range(2):
                            src = fsum[:, t, o, :] if r == 0 else hk[:, t, o, 1, :]
                            mm = pe.matmul(bk, basis[r][t][:, k * P:(k + 1) * P], src, start=(t == 0), stop=(t == 1))
                        end(mm, g)

            filter_spectrum(0)
            project_z("x10", 4)
            project_z("x11", 6)
            filter_spectrum(1)

            def turn_z(groups, first):
                for i in range(4):
                    wait_drained(pe, f"z{first + i}")
                for t in range(2):
                    bk = begin(groups[t])
                    for i in range(4):
                        mm = pe.transpose(bk[:, i * P:(i + 1) * P], zz[first + i][:, t * P:(t + 1) * P], ident)
                    end(mm, groups[t])

            def forward(prefix, y):
                for k in range(2):
                    for r in range(2):
                        g = f"{prefix}{r}{k}"
                        bk = begin(g)
                        for t in range(2):
                            mm = pe.matmul(bk, basis[r][t][:, k * P:(k + 1) * P], y[:, t, :], start=(t == 0), stop=(t == 1))
                        end(mm, g)

            turn_z(["tv0", "tv1"], 0)
            wait_drained(pe, "tv0")
            wait_drained(pe, "tv1")
            forward("fa", vT)
            turn_z(["tx0", "tx1"], 4)
            pe.wait_ge(qk_ready, 4)
            for t in range(2):
                bk = begin(f"tq{t}")
                for j in range(4):
                    mm = pe.transpose(bk[:, j * P:(j + 1) * P], qr[t][:, j * P:(j + 1) * P], ident)
                end(mm, f"tq{t}")
            bk = begin("tk")
            for t in range(2):
                mm = pe.transpose(bk[:, t * P:(t + 1) * P], kr[t], ident)
            end(mm, "tk")
            project_z("x20", 8)
            project_z("x21", 10)
            pe.wait_ge(spec_ready, 4)
            for t in range(2):
                bk = begin(f"ia{t}")
                for n, (r, k) in enumerate([(r, k) for k in range(2) for r in range(2)]):
                    mm = pe.matmul(bk, basis[r][k][:, t * P:(t + 1) * P], spec[:, r, k, :], start=(n == 0), stop=(n == 3))
                end(mm, f"ia{t}")
            for t in range(2):
                wait_drained(pe, f"tq{t}")
            wait_drained(pe, "tk")
            for t in range(2):
                for j in range(4):
                    g = f"sc{t}{j}"
                    bk = begin(g)
                    for h in range(2):
                        mm = pe.matmul(bk[:, h * T:(h + 1) * T], qz[:, h * QPK + j, t * P:(t + 1) * P], kT,
                                       start=True, stop=True)
                    end(mm, g)
            for i in range(4):
                project_gate(f"gh{i}")
            wait_drained(pe, "ia0")
            wait_drained(pe, "ia1")
            forward("fb", vT)

            def turn_probs(j, h):
                g = f"pt{j}{h}"
                pe.wait_ge(p_ready, 8)
                bk = begin(g)
                for s in range(2):
                    for t in range(2):
                        mm = pe.transpose(bk[:, s * T + t * P:s * T + (t + 1) * P],
                                          probs[:, t, h * QPK + j, s * P:(s + 1) * P], ident)
                end(mm, g)

            def attend(j):
                bk = begin(f"pv{j}")
                for h in range(2):
                    wait_drained(pe, f"pt{j}{h}")
                for s in range(2):
                    for h in range(2):
                        mm = pe.matmul(bk[h * HD:(h + 1) * HD, 0:T], vtok[:, s, h * HD:(h + 1) * HD],
                                       ptb[2 * (j % 2) + h][:, s, :], start=(s == 0), stop=(s == 1))
                end(mm, f"pv{j}")

            for h in range(2):
                turn_probs(0, h)
            for j in range(4):
                if j + 1 < 4:
                    for h in range(2):
                        turn_probs(j + 1, h)
                attend(j)
            for i in range(4):
                project_gate(f"ga{i}")
            pe.wait_ge(spec_ready, 8)
            for i in range(4):
                bk = begin(f"ib{i}")
                for n, (r, k) in enumerate([(r, k) for k in range(2) for r in range(2)]):
                    mm = pe.matmul(bk[:, 0:T], spec[:, r, k, i * P:(i + 1) * P], basis[r][k], start=(n == 0), stop=(n == 3))
                end(mm, f"ib{i}")

            def up(load, groups, src, ready):
                whi, wlo = unit(load, 4)
                shi, slo = src
                for i in range(2):
                    bk = begin(groups[i])
                    for s in range(2):
                        m, out_ = 2 * i + s, bk[:, s * T:(s + 1) * T]
                        for k in range(4):
                            if m == 0:
                                ready(k)
                            cols = slice(m * P, (m + 1) * P)
                            pe.matmul(out_, wlo[:, k, cols], shi[:, k, :], start=(k == 0), stop=False)
                            pe.matmul(out_, whi[:, k, cols], slo[:, k, :], start=False, stop=False)
                            mm = pe.matmul(out_, whi[:, k, cols], shi[:, k, :], start=False, stop=(k == 3))
                    end(mm, groups[i])

            for h in range(2):
                up(f"hu{h}", [f"uh{2 * h}", f"uh{2 * h + 1}"], (x2hi, x2lo), lambda k: pe.wait_ge(x2_lo, k + 1))
            for h in range(2):
                up(f"au{h}", [f"ua{2 * h}", f"ua{2 * h + 1}"], (yhi, ylo), lambda k: wait_drained(pe, f"pv{k}"))
            outs = {}
            for i in range(4):
                whi, wlo = unit(f"wo{i}", 2)
                pe.wait_ge(m_lo, i + 1)
                for t in range(2):
                    for h in range(2):
                        if i == 0:
                            outs[t, h] = begin(f"wo{t}{h}")
                        for k in range(2):
                            m, tok, cols = 2 * i + k, slice(t * P, (t + 1) * P), slice(h * 512, (h + 1) * 512)
                            pe.matmul(outs[t, h], mhi[:, m, tok], wlo[:, k, cols], start=(m == 0), stop=False)
                            pe.matmul(outs[t, h], mlo[:, m, tok], whi[:, k, cols], start=False, stop=False)
                            mm = pe.matmul(outs[t, h], mhi[:, m, tok], whi[:, k, cols], start=False, stop=(m == 7))
                        if i == 3:
                            end(mm, f"wo{t}{h}")
                if i < 3:
                    mm.then_inc(out_used, 1)

            def turn_hn(t):
                pe.wait_ge(hn_ready, t + 1)
                for i in range(2):
                    g = f"th{t}{i}"
                    bk = begin(g)
                    for k in range(4):
                        kk = 4 * i + k
                        mm = pe.transpose(bk[:, k * P:(k + 1) * P], hn[:, t, kk * P:(kk + 1) * P], ident)
                    end(mm, g)

            for g in ("wo00", "wo01", "wo10", "wo11"):
                wait_drained(pe, g)
            pe.wait_ge(b1_ready, 1)
            pe.wait_ge(pads_ready, 1)
            for b in range(4):
                mm = pe.matmul(ps[:, b, :], zlhs[:], b1p[:, 0:512], start=True, stop=False, skip_group_check=True)
            mm.then_inc(comb, 1)
            turn_hn(0)
            turn_hn(1)
            pe.wait_ge(in_name["rw"], 16)
            bk = begin("lg")
            for half in range(2):
                for t in range(2):
                    wait_drained(pe, f"th{t}{half}")
                for c in range(4):
                    k = 4 * half + c
                    mm = pe.matmul(bk[c * NE:(c + 1) * NE, 0:T], rw[:, k, :], hnT[:, k, :], start=(half == 0),
                                   stop=(half == 1), skip_group_check=True)
            end(mm, "lg")
            wait_drained(pe, "lg")
            bk = begin("lt")
            for t in range(2):
                mm = pe.matmul(bk[:, t * NE:(t + 1) * NE], lgT[:, t * P:(t + 1) * P], tab[:, C_ID4:C_ID4 + NE],
                               start=True, stop=True)
            end(mm, "lt")
            pe.wait_ge(mask_ready, 1)
            bk = begin("rk")
            pe.matmul(bk[:, 0:NE], tri16, mask3[:, 0, 0:NE], start=True, stop=True)
            pe.matmul(bk[:, NE:2 * NE], ones16, mask3[:, 0, 0:NE], start=True, stop=False)
            pe.matmul(bk[:, NE:2 * NE], tri16, mask3[:, 1, 0:NE], start=False, stop=True)
            pe.matmul(bk[0:96, 64:65], mask3[:, 0, :], ones16[:, 0:1], start=True, stop=False)
            end(pe.matmul(bk[0:96, 64:65], mask3[:, 1, :], ones16[:, 0:1], start=False, stop=True), "rk")
            hid = ps[:, 4:6, :]
            ybk = ps[:, 6, :]
            tbk = ps[:, 7, :]
            acc = [[ps[:, 2 * t + w, :] for w in range(2)] for t in range(2)]
            def gather(buf, half, use, ready, bank=tbk):
                pe.wait_ge(sel_ready, ready)
                pe.wait_ge(t_free, use)
                for k in range(4):
                    kk = 4 * half + k
                    for t in range(2):
                        for a in range(3):
                            mm = pe.matmul(bank[:, k * P:(k + 1) * P], parts[:, a, t, kk * P:(kk + 1) * P],
                                           sel[:, t, :], start=(t == 0 and a == 0), stop=(t == 1 and a == 2))
                mm.then_inc(t_full, 1)

            def hidden(pos, c0, nth, count, selected, gathered, cols):
                pe.wait_ge(selb_ready, selected)
                pe.wait_ge(h_used, count)
                for b in range(2):
                    for h in range(2):
                        c = 2 * b + h
                        pe.matmul(hid[h * 64:(h + 1) * 64, b, :], selB[:, pos, :], b1p[:, c * 512:(c + 1) * 512],
                                  start=True, stop=False, skip_group_check=True)
                pe.wait_ge(t_free, gathered)
                for k in range(8):
                    slot = (c0 + k) % NSLOT
                    pe.wait_ge(ld[slot], nth[k])
                    w = ring[:, slot * SLOT:(slot + 1) * SLOT]
                    for b in range(2):
                        for h in range(2):
                            c = 2 * b + h
                            mm = pe.matmul(hid[h * 64:(h + 1) * 64, b, :], cols[:, k, :], w[:, c * 512:(c + 1) * 512],
                                           start=False, stop=(k == 7), skip_group_check=True)
                    if k < 7:
                        mm.then_inc(chunk_used, 1)
                mm.then_inc(h_full, 1)

            def turn_hidden(use, count):
                pe.wait_ge(hact_ready, count)
                pe.wait_ge(t_free, use)
                for i in range(4):
                    mm = pe.transpose(tbk[:, i * P:(i + 1) * P], hact[:, i // 2, (i % 2) * P:(i % 2 + 1) * P], ident)
                mm.then_inc(t_full, 1)

            def second(pos, odd, c0, nth, count, turned):
                pe.wait_ge(y_used, count)
                for h in range(2):
                    wd = h ^ odd
                    pe.matmul(ybk[h * 64:(h + 1) * 64, :], selB[:, pos, :], b2p[:, wd * 512:(wd + 1) * 512],
                              start=True, stop=False, skip_group_check=True)
                pe.wait_ge(t_free, turned)
                for m in range(4):
                    slot = (c0 + 8 + m) % NSLOT
                    pe.wait_ge(ld[slot], nth[8 + m])
                    w = ring[:, slot * SLOT:(slot + 1) * SLOT].rearrange("p (k n) -> p k n", k=2)
                    for kk in range(2):
                        f = 2 * m + kk
                        b, half, r = f // 4, (f // 2) % 2, f % 2
                        lhs = hT[:, 2 * b + r, half * 64:(half + 1) * 64]
                        for h in range(2):
                            wd = h ^ odd
                            mm = pe.matmul(ybk[h * 64:(h + 1) * 64, :], lhs, w[:, kk, wd * 512:(wd + 1) * 512],
                                           start=False, stop=(f == 7), skip_group_check=True)
                    if m < 3:
                        mm.then_inc(chunk_used, 1)
                    else:
                        mm.then_inc(y_full, 1)

            def turn_gates(use, count):
                pe.wait_ge(selg_ready, count)
                pe.wait_ge(t_free, use)
                for w in range(2):
                    for t in range(2):
                        mm = pe.transpose(tbk[:, (2 * w + t) * P:(2 * w + t + 1) * P],
                                          selG[:, t, w * SLOTS:(w + 2) * SLOTS], ident)
                mm.then_inc(t_full, 1)

            def combine(ready, turned):
                pe.wait_ge(y_used, ready)
                pe.wait_ge(t_free, turned)
                for t in range(2):
                    for w in range(2):
                        pe.matmul(acc[t][w], gT[:, 2 * w + t, :], yab[:, w, :], start=False, stop=False,
                                  skip_group_check=True).then_inc(comb if t and w else added, 1)

            for t in range(2):
                pe.wait_ge(lo_ready[t], 1)
            wait_drained(pe, "th11")
            gather(0, 0, 1, 1)
            pe.wait_ge(over_ready, 1)
            bk = begin("lp")
            end(pe.matmul(bk[0:96, 0:1], tri16[0:96, 0:96], over[0:96, :], start=True, stop=True), "lp")
            wait_drained(pe, "rk")
            gather(0, 1, 1, 1, ybk)
            pe.wait_ge(pos_ready, 1)
            bk = begin("ls")
            pe.matmul(bk[0:1, 0:NLIST], eb16[0:96, 0:1], onehot[0:96, :], start=True, stop=True)
            pe.matmul(bk[0:1, NLIST:2 * NLIST], eb16[0:96, 1:2], onehot[0:96, :], start=True, stop=True)
            end(pe.matmul(bk[0:1, 2 * NLIST:2 * NLIST + 1], over[0:96, :], ones16[0:96, 0:1], start=True, stop=True), "ls")
            for g in ("rk", "lp", "ls"):
                wait_drained(pe, g)
            pe.wait_ge(b2_ready, 1)
            with pe.Fori(0, TURNS) as it:
                use = it * 10 + 3
                for j in range(GROUP):
                    c0 = CHUNKS * j
                    nth = [it * 48 + 16 * ((c0 + k) // NSLOT + 1) for k in range(CHUNKS)]
                    e1 = it * GROUP + (j + 1)
                    hidden(j % 2, c0, nth, e1, e1, use, xg[:, j // 2, :, (j % 2) * SLOTS:(j % 2 + 1) * SLOTS])
                    if j == 0:
                        turn_gates(use, it * 2 + 1)
                        gather(1, 0, use + 1, it * 2 + 2)
                        use = use + 2
                    elif j == 1:
                        gather(1, 1, use, it * 2 + 2)
                        use = use + 1
                    elif j == 2:
                        combine(it * 4 + 3, it * 10 + 4)
                        turn_gates(use, it * 2 + 2)
                        use = use + 1
                    else:
                        gather(0, 0, use, it * 2 + 3)
                        gather(0, 1, use + 1, it * 2 + 3)
                        use = use + 2
                    turn_hidden(use, e1)
                    use = use + 1
                    second(j % 2, j % 2, c0, nth, e1, use)
                combine(it * 4 + 5, it * 10 + 9)

            pe.wait_ge(list_ready, 1)
            n_over = pe.value_load(olist[0:1, 2 * NLIST:2 * NLIST + 1], min_val=0, max_val=NLIST)
            OU = 2 + 10 * TURNS + 1
            with pe.If(n_over > 0):
                with pe.Fori(0, n_over) as i:
                    use = i * 4 + OU
                    gather(0, 0, use, i + (2 * TURNS + 2))
                    gather(0, 1, use + 1, i + (2 * TURNS + 2))
                    nth = [i * 16 + 16 * (NCH // NSLOT + 1)] * CHUNKS
                    hidden(0, 0, nth, i + (NE + 1), i + (NE + 2), use + 2, xg[:, 0, :, 0:SLOTS])
                    turn_gates(use + 2, i + (2 * TURNS + 1))
                    turn_hidden(use + 3, i + (NE + 1))
                    second(0, 0, 0, nth, i + (NE + 1), use + 4)
                    pe.wait_ge(y_used, i + (NE + 2))
                    for t in range(2):
                        for w in range(2):
                            pe.matmul(acc[t][w], gT[w * 64:(w + 1) * 64, 2 * w + t, :],
                                      yab[w * 64:(w + 1) * 64, w, :], start=False, stop=False,
                                      skip_group_check=True).then_inc(comb if t and w else added, 1)

        @block.scalar
        def _(act):
            act.wait_ge(dve_step, 2)
            act.activation(mark[:, 4:5], mark[:, 5:6], ACT.Sqrt)
            for t in range(2):
                act.wait_ge(in_x[t], 16)
                act.activation(u[:, t, :], xh[:, t, :], ACT.Square, accum_out=stat[:, t:t + 1]).then_inc(x_ss, 1)
            act.wait_ge(x_var, 1)
            act.activation(stat[:, 4:6], stat[:, 2:4], ACT.Sqrt).then_inc(x_std, 1)
            def round_unit(n):
                act.wait_ge(in_unit[n % 8], 16 * (n // 8 + 1) + 16 * (UNITS[n][0][:2] == "au"))
                if n >= 2:
                    wait_unit_used(act, n - 2)
                act.copy(unit_parts(n)[0], unit_raw(n)).then_inc(unit_hi, 1)

            act.wait_ge(in_unit[0], 16)
            act.copy(tile_of(unit_parts(0)[0], 0), tile_of(unit_raw(0), 0)).then_inc(tile_hi, 1)
            for i in range(4):
                wait_filled(act, f"uT{i}")
                act.copy(uhi[:, 2 * i:2 * i + 2, :].rearrange("p k t -> p (k t)"), ps[:, BANK[f"uT{i}"], :]).then_inc(uhi_ready, 1)

            act.copy(tile_of(unit_parts(0)[0], 1), tile_of(unit_raw(0), 1)).then_inc(unit_hi, 1)
            act.dma_start(fw3[0:FHID, :], filt_w3[0]).then_inc(in_name["fw3"], 16)
            act.dma_start(fw3[FHID:FHID + 1, :], filt_b3).then_inc(in_name["b3"], 16)
            act.dma_start(decay.rearrange("p t n -> p (t n)"), c_decay).then_inc(in_name["decay"], 16)
            act.dma_start(dft[:], c_dft).then_inc(in_name["dft"], 16)
            for o in range(2):
                act.dma_start(dbc[:, o, :], hyena_d[0, o:o + 1, :].partition_broadcast(P)).then_inc(in_name["dbc"], 16)
            act.dma_start(qkg[:, 0:64], q_norm_g.partition_broadcast(P)).then_inc(in_name["qkg"], 16)
            act.dma_start(qkg[:, 64:128], k_norm_g.partition_broadcast(P)).then_inc(in_name["qkg"], 16)
            round_unit(1)
            act.wait_ge(f_arg, 1)
            act.activation(h1, farg, ACT.Sin).then_inc(f_out, 1)

            def scale_z(i):
                wait_drained(act, "vec")
                wait_filled(act, f"z{i}")
                act.activation(zz[i], ps[:, BANK[f"z{i}"], 0:T], ACT.Identity,
                               bias=vecT[:, 36 + i:37 + i], scale=vecT[:, 12 + i:13 + i]).then_inc(z_scaled, 1)

            scale_z(0)
            scale_z(1)
            act.wait_ge(f_arg, 2)
            act.activation(h2e[0:FHID, :], farg, ACT.Sin).then_inc(f_out, 1)
            round_unit(2)
            for i in range(2, 4):
                scale_z(i)
            round_unit(3)
            act.wait_ge(hk_ready, 2)
            for t in range(2):
                for c in range(4):
                    wait_drained(act, f"h{t}{c}")
                act.activation(absf[:, t], hk[:, t], ACT.Abs).then_inc(abs_ready, 1)
                if t == 0:
                    round_unit(4)
            for t in range(2):
                wait_filled(act, f"q{t}")
                act.activation(sq[t][:, 0:512], ps[:, BANK[f"q{t}"], :], ACT.Square).then_inc(qk_sq, 1)
            round_unit(5)
            for t in range(2):
                wait_filled(act, f"kv{t}")
                act.activation(sq[t][:, 512:640], ps[:, BANK[f"kv{t}"], 0:128], ACT.Square).then_inc(qk_sq, 1)
            act.wait_ge(qk_var, 1)
            act.activation(stat[:, 28:48], stat[:, 8:28], ACT.Sqrt).then_inc(qk_std, 1)
            for g in range(3):
                act.dma_start(b1raw[32 * g:32 * g + 32, :], expert_b1[0]).then_inc(in_name["b1"], 16)
            round_unit(6)
            for i in range(4, 8):
                scale_z(i)
                if i % 2:
                    round_unit(7 + (i - 5) // 2)
            for g, dst in (("tv0", vT[:, 0, :]), ("tv1", vT[:, 1, :]), ("tx0", x1T[:, 0, :]), ("tx1", x1T[:, 1, :])):
                wait_filled(act, g)
                drains(act.copy(dst, ps[:, BANK[g], :]), g)
            act.wait_ge(qz_zero, 1)
            for t in range(2):
                g = f"tq{t}"
                wait_filled(act, g)
                src = ps[:, BANK[g], :].rearrange("p (j t) -> p j t", j=4)
                act.copy(qz[0:HD, 0:QPK, t * P:(t + 1) * P], src[0:HD])
                drains(act.copy(qz[HD:P, QPK:NH, t * P:(t + 1) * P], src[HD:P]), g)
            wait_filled(act, "tk")
            drains(act.copy(kT, ps[:, BANK["tk"], 0:T]), "tk")
            for i in range(8, 12):
                scale_z(i)
                if i % 2:
                    round_unit(9 + (i - 9) // 2)
            for t in range(2):
                for j in range(4):
                    g, i = f"sc{t}{j}", 2 * (4 * t + j)
                    act.wait_ge(mx_ready, 4 * t + j + 1)
                    for h in range(2):
                        ins = act.activation(probs[:, t, h * QPK + j, :], ps[:, BANK[g], h * T:(h + 1) * T], ACT.Exp,
                                             bias=smax[:, i + h:i + h + 1], accum_out=smax[:, 16 + i + h:17 + i + h])
                    drains(ins, g)

            def open_gate(groups, dst, first, last):
                for i, g in enumerate(groups):
                    wait_filled(act, g)
                    if first + i <= last:
                        round_unit(first + i)
                    drains(act.activation(dst[:, 2 * i:2 * i + 2, :].rearrange("p m t -> p (m t)"), ps[:, BANK[g], :], ACT.Sigmoid), g)

            act.wait_ge(b1_ready, 1)
            open_gate([f"gh{i}" for i in range(4)], ghy, UNIT["gh2"], UNIT["ga1"])

            def take_probs(j):
                for h in range(2):
                    g = f"pt{j}{h}"
                    wait_filled(act, g)
                    drains(act.copy(ptb[2 * (j % 2) + h].rearrange("p s t -> p (s t)"), ps[:, BANK[g], :]), g)

            take_probs(0)
            take_probs(1)
            for j in range(4):
                wait_filled(act, f"pv{j}")
                act.copy(yhi[:, j, :], ps[:, BANK[f"pv{j}"], 0:T]).then_inc(y_hi, 1)
                if j + 2 < 4:
                    take_probs(j + 2)
            open_gate([f"ga{i}" for i in range(4)], gat, UNIT["ga2"], UNIT["hu1"])
            for i in range(4):
                wait_drained(act, f"ib{i}")
                act.copy(x2hi[:, i, :], x2z[i]).then_inc(x2_hi, 1)
            round_unit(UNIT["au0"])
            round_unit(UNIT["au1"])
            for i in range(4):
                wait_drained(act, f"ua{i}")
                act.copy(mhi[:, 2 * i:2 * i + 2, :], mT[:, 2 * i:2 * i + 2, :]).then_inc(m_hi, 1)
                if i < 2:
                    round_unit(UNIT[f"wo{i}"])
            round_unit(UNIT["wo2"])
            round_unit(UNIT["wo3"])
            act.activation(mark[:, 4:5], mark[:, 5:6], ACT.Sqrt)
            for t in range(2):
                for w in range(2):
                    wait_drained(act, f"wo{t}{w}")
                    act.activation(junk, xh[:, t, w * 512:(w + 1) * 512], ACT.Square,
                                   accum_out=stat[:, 48 + 2 * t + w:49 + 2 * t + w]).then_inc(h_ss, 1)
                    act.wait_ge(h_ss, 2 * t + w + 1)
            act.wait_ge(h_var, 1)
            act.activation(stat[:, 54:56], stat[:, 52:54], ACT.Sqrt).then_inc(h_std, 1)

            def take_hn(t):
                g = f"th{t}0"
                wait_filled(act, g)
                drains(act.copy(hnT[:, 0:4, t * P:(t + 1) * P], ps[:, BANK[g], :].rearrange("p (k t) -> p k t", k=4)), g)

            def first_part(t):
                act.wait_ge(hn_ready, t + 1)
                act.copy(parts[:, 0, t, :], hn[:, t, :]).then_inc(hi_ready, 1)

            def second_part(t):
                act.wait_ge(res_ready[t], 1)
                act.copy(parts[:, 1, t, :], resid[t]).then_inc(mid16_ready, 1)

            take_hn(0)
            first_part(0)
            take_hn(1)
            first_part(1)
            wait_filled(act, "lg")
            act.wait_ge(in_name["rb"], 16)
            drains(act.activation(lgT, ps[:, BANK["lg"], 0:T], ACT.Identity, bias=rbias[:]), "lg")
            second_part(0)
            second_part(1)
            wait_drained(act, "lt")
            act.activation(gate[:], gate[:], ACT.Exp).then_inc(r_exp, 1)

            def take_turn(dst, count, bank=7):
                act.wait_ge(t_full, count)
                act.copy(dst, ps[:, bank, :]).then_inc(t_free, 1)

            def gathered(buf, half):
                return xg[:, buf, 4 * half:4 * half + 4, :].rearrange("p k s -> p (k s)")

            gT_all = gT.rearrange("p w t -> p (w t)")
            hT_all = hT.rearrange("p f s -> p (f s)")

            def sigmoid(count):
                act.wait_ge(glu_ready, count)
                act.activation(sig, glu, ACT.Sigmoid, scale=ALPHA).then_inc(sig_ready, 1)

            take_turn(gathered(0, 0), 1)
            take_turn(gathered(0, 1), 2, 6)
            with act.Fori(0, TURNS) as it:
                n = 3
                for j, takes in enumerate(([gT_all, gathered(1, 0), hT_all], [gathered(1, 1), hT_all],
                                           [gT_all, hT_all], [gathered(0, 0), gathered(0, 1), hT_all])):
                    sigmoid(it * GROUP + (j + 1))
                    for dst in takes:
                        take_turn(dst, it * 10 + n)
                        n += 1
            act.wait_ge(list_ready, 1)
            n_over = act.value_load(olist[0:1, 2 * NLIST:2 * NLIST + 1], min_val=0, max_val=NLIST)
            with act.If(n_over > 0):
                with act.Fori(0, n_over) as i:
                    base = 2 + 10 * TURNS
                    take_turn(gathered(0, 0), i * 4 + (base + 1))
                    take_turn(gathered(0, 1), i * 4 + (base + 2))
                    sigmoid(i + (NE + 1))
                    take_turn(gT_all, i * 4 + (base + 3))
                    take_turn(hT_all, i * 4 + (base + 4))

        @block.vector
        def _(v):
            steps = [0]

            def link(ins):
                steps[0] += 1
                ins.then_inc(dve_step, 1)
                v.wait_ge(dve_step, steps[0])

            link(v.memset(h2e[FHID:FHID + 1, :], 1.0))
            link(v.memset(mark[:], 1.0))
            link(v.memset(rankm[:], 0.0))
            link(v.memset(rbias[:], 0.0))
            v.memset(zlhs[:], 0.0).then_inc(pads_ready, 1)

            def filter_arg(g, b, count):
                wait_filled(v, g)
                if count == 2:
                    v.wait_ge(f_out, 1)
                v.tensor_scalar(farg, ps[0:FHID, BANK[g], 0:T], fvec[:, b:b + 1], fvec[:, b + 1:b + 2], ALU.add, ALU.mult)\
                    .then_inc(drained[BANK[g]], 1)
                wait_drained(v, g)
                magic = 12582912.0
                link(v.tensor_scalar(frnd, farg, 0.15915494309, magic, ALU.mult, ALU.add))
                link(v.tensor_scalar(frnd, frnd, -magic, None, ALU.add))
                for part in (PI2_A, PI2_B, PI2_C):
                    link(v.scalar_tensor_tensor(farg, frnd, -part, farg, ALU.mult, ALU.add))
                v.tensor_scalar(farg, farg, PI_IN, -PI_IN, ALU.min, ALU.max).then_inc(f_arg, 1)

            v.wait_ge(x_ss, 2)
            v.tensor_scalar(stat[:, 2:4], stat[:, 0:2], 1.0 / D, EPS, ALU.mult, ALU.add).then_inc(x_var, 1)
            v.wait_ge(x_std, 1)
            link(v.reciprocal(stat[:, 6:8], stat[:, 4:6]))
            v.wait_ge(in_name["g1b"], 16)
            for t in range(2):
                v.scalar_tensor_tensor(u[:, t, :], xh[:, t, :], stat[:, 6 + t:7 + t], g1b, ALU.mult, ALU.mult).then_inc(u_ready, 1)
            v.wait_ge(u_ready, 2)
            v.wait_ge(tile_hi, 1)
            rounded, rest = unit_parts(0)
            v.tensor_tensor(tile_of(rest, 0), tile_of(unit_raw(0), 0), tile_of(rounded.bitcast(F32), 0), ALU.subtract)\
                .then_inc(tile_lo, 1)
            for i in range(4):
                v.wait_ge(uhi_ready, i + 1)
                part = (slice(None), slice(2 * i, 2 * i + 2), slice(None))
                drains(v.tensor_tensor(ulo[part].rearrange("p k t -> p (k t)"), ps[:, BANK[f"uT{i}"], :],
                                       uhi[part].rearrange("p k t -> p (k t)").bitcast(F32), ALU.subtract), f"uT{i}")

            v.wait_ge(unit_hi, 1)
            v.tensor_tensor(tile_of(rest, 1), tile_of(unit_raw(0), 1), tile_of(rounded.bitcast(F32), 1), ALU.subtract)\
                .then_inc(unit_lo[0], 1)
            wait_filled(v, "vec")
            drains(v.tensor_copy(vecT, ps[:, BANK["vec"], 0:48]), "vec")
            wait_filled(v, "fv")
            drains(v.tensor_copy(fvec, ps[0:FHID, BANK["fv"], 0:4]), "fv")
            wait_drained(v, "fv")
            filter_arg("f1", 0, 1)
            rest_of_unit(v, 1)

            def outer_taps(i):
                v.wait_ge(z_scaled, i + 1)
                zp = ps[:, BANK[f"z{i}"], 0:T]
                link(v.scalar_tensor_tensor(zz[i][:, 1:T], zp[:, 0:T - 1], vecT[:, i:i + 1], zz[i][:, 1:T], ALU.mult, ALU.add))
                drains(v.scalar_tensor_tensor(zz[i][:, 0:T - 1], zp[:, 1:T], vecT[:, 24 + i:25 + i], zz[i][:, 0:T - 1],
                                              ALU.mult, ALU.add), f"z{i}")

            wait_drained(v, "vec")
            outer_taps(0)
            outer_taps(1)
            filter_arg("f2", 2, 2)
            rest_of_unit(v, 2)
            for i in range(2, 4):
                outer_taps(i)
            v.wait_ge(in_name["decay"], 16)
            for t in range(2):
                if t == 1:
                    rest_of_unit(v, 3)
                for c in range(4):
                    g = f"h{t}{c}"
                    wait_filled(v, g)
                    drains(v.tensor_tensor(hk[:, t, c // 2, c % 2, :], ps[:, BANK[g], :], decay[:, t, :], ALU.mult), g)
                    if t == 0 and c % 2:
                        wait_drained(v, g)
                        v.memset(hk[0:1, 0, c // 2, 1, :], 0.0).then_inc(hk_ready, 1)
            rest_of_unit(v, 4)
            v.wait_ge(abs_ready, 2)
            link(v.tensor_tensor(habs, absf[:, 0, :, 0, :], absf[:, 0, :, 1, :], ALU.add))
            link(v.tensor_tensor(habs, habs, absf[:, 1, :, 0, :], ALU.add))
            v.tensor_tensor(habs, habs, absf[:, 1, :, 1, :], ALU.add).then_inc(habs_ready, 1)
            v.wait_ge(in_name["qkg"], 32)
            v.wait_ge(in_tab, 16)
            link(v.tensor_copy(tri16, tri))
            link(v.memset(ones16, 1.0))
            link(v.tensor_copy(eb16, tab[:, C_E:C_E + 2]))
            for t in range(2):
                for a in range(2):
                    g = qkg[:, 64 * a:64 * a + 64].rearrange("p (i two) -> p two i", two=2)
                    scale = HD ** -0.5 if a == 0 else 1.0
                    for n, (eo, trig) in enumerate(((0, cs), (1, sn), (0, sn), (1, cs))):
                        ins = v.scalar_tensor_tensor(rope[:, t, 4 * a + n, :], g[:, eo, :], scale, trig[t], ALU.mult, ALU.mult)
            link(ins)
            v.wait_ge(qk_sq, 4)
            for t in range(2):
                link(v.tensor_reduce(stat[:, 8 + 10 * t:18 + 10 * t], sq[t].rearrange("p (h c) -> p h c", c=HD), AX.X, ALU.add))
            v.tensor_scalar(stat[:, 8:28], stat[:, 8:28], 1.0 / HD, EPS, ALU.mult, ALU.add).then_inc(qk_var, 1)
            v.wait_ge(qk_std, 1)
            link(v.reciprocal(stat[:, 8:28], stat[:, 28:48]))
            for t in range(2):
                rs = stat[:, 8 + 10 * t:18 + 10 * t].unsqueeze(2)
                drains(v.tensor_tensor(qn[t][:, 0:NH, :], ps[:, BANK[f"q{t}"], :].rearrange("p (h c) -> p h c", c=HD),
                                       rs[:, 0:NH, :].to_broadcast([P, NH, HD]), ALU.mult), f"q{t}")
                link(v.tensor_tensor(qn[t][:, NH:NH + NKV, :], ps[:, BANK[f"kv{t}"], 0:128].rearrange("p (h c) -> p h c", c=HD),
                                     rs[:, NH:NH + NKV, :].to_broadcast([P, NKV, HD]), ALU.mult))
                drains(v.tensor_copy(vtok[:, t, :], ps[:, BANK[f"kv{t}"], 128:256]), f"kv{t}")

            def rotate(src, heads, tables, dst):
                x0, x1 = src[:, :, 0::2], src[:, :, 1::2]
                m = [a[:, 0:heads, :] for a in mm4]
                for n, x in enumerate((x0, x1, x0, x1)):
                    ins = v.tensor_tensor(m[n], x, tables[:, n:n + 1, :].to_broadcast([P, heads, 32]), ALU.mult)
                link(ins)
                per = heads // NKV
                view = [a.rearrange("p (g j) i -> p g j i", g=NKV) for a in m]
                out_ = dst.rearrange("p (j g c) -> p g j c", g=NKV, j=per)
                link(v.tensor_tensor(out_[:, :, :, 0::2], view[0], view[1], ALU.subtract))
                v.tensor_tensor(out_[:, :, :, 1::2], view[2], view[3], ALU.add).then_inc(qk_ready, 1)
                done[0] += 1
                v.wait_ge(qk_ready, done[0])

            done = [0]
            v.wait_ge(in_name["dbc"], 32)

            def take_spectrum(o):
                wait_filled(v, f"nrm{o}")
                drains(v.reciprocal(rinv[:, o, :], ps[:, BANK[f"nrm{o}"], :]), f"nrm{o}")
                wait_drained(v, f"nrm{o}")
                for k in range(2):
                    for r in range(2):
                        g = f"kf{o}{r}{k}"
                        wait_filled(v, g)
                        drains(v.scalar_tensor_tensor(kf[:, o, r, k, :], ps[:, BANK[g], :], wk[k], rinv[:, o, :],
                                                      ALU.mult, ALU.mult), g)
                        if r == 0:
                            wait_drained(v, g)
                            link(v.scalar_tensor_tensor(kf[:, o, 0, k, :], dbc[:, o, :], wk[k], kf[:, o, 0, k, :],
                                                        ALU.mult, ALU.add))

            def rotate_tile(t):
                rotate(qn[t][:, 0:NH, :], NH, rope[:, t, 0:4, :], qr[t])
                rotate(qn[t][:, NH:NH + NKV, :], NKV, rope[:, t, 4:8, :], kr[t])

            take_spectrum(0)
            v.memset(qz, 0.0).then_inc(qz_zero, 1)
            rotate_tile(0)
            for i in range(4, 8):
                outer_taps(i)
            take_spectrum(1)
            rotate_tile(1)

            def filter_product(prefix, o):
                for k in range(2):
                    yr, ys = (ps[:, BANK[f"{prefix}{r}{k}"], :] for r in range(2))
                    kr_, ks = kf[:, o, 0, k, :], kf[:, o, 1, k, :]
                    wait_filled(v, f"{prefix}0{k}")
                    v.tensor_tensor(prod[:, 0, :], yr, kr_, ALU.mult).then_inc(dve_step, 1)
                    steps[0] += 1
                    drains(v.tensor_tensor(prod[:, 2, :], yr, ks, ALU.mult), f"{prefix}0{k}")
                    wait_filled(v, f"{prefix}1{k}")
                    link(v.tensor_tensor(prod[:, 1, :], ys, ks, ALU.mult))
                    drains(v.tensor_tensor(prod[:, 3, :], ys, kr_, ALU.mult), f"{prefix}1{k}")
                    v.tensor_tensor(spec[:, 0, k, :], prod[:, 0, :], prod[:, 1, :], ALU.subtract).then_inc(spec_ready, 1)
                    wait_drained(v, f"{prefix}1{k}")
                    v.tensor_tensor(spec[:, 1, k, :], prod[:, 2, :], prod[:, 3, :], ALU.add).then_inc(spec_ready, 1)
                    v.wait_ge(spec_ready, 4 * o + 2 * k + 2)

            wait_drained(v, "kf111")
            filter_product("fa", 0)
            for i in range(8, 12):
                outer_taps(i)
                if i % 2:
                    rest_of_unit(v, 9 + (i - 9) // 2)
            for t in range(2):
                wait_drained(v, f"tx{t}")
                wait_filled(v, f"ia{t}")
                drains(v.tensor_tensor(vT[:, t, :], ps[:, BANK[f"ia{t}"], :], x1T[:, t, :], ALU.mult), f"ia{t}")

            def normalise(n):
                t, j = n // 4, n % 4
                wait_drained(v, f"sc{t}{j}")
                link(v.reciprocal(smax[:, 32 + 2 * (n % 4):34 + 2 * (n % 4)], smax[:, 16 + 2 * n:18 + 2 * n]))
                pr = probs[:, t, j::QPK, :]
                rs = smax[:, 32 + 2 * (n % 4):34 + 2 * (n % 4)].unsqueeze(2).to_broadcast([P, 2, T])
                v.tensor_tensor(pr, pr, rs, ALU.mult).then_inc(p_ready, 1)
                v.wait_ge(p_ready, n + 1)

            for n in range(8):
                g = f"sc{n // 4}{n % 4}"
                wait_filled(v, g)
                v.tensor_reduce(smax[:, 2 * n:2 * n + 2], ps[:, BANK[g], :].rearrange("p (h s) -> p h s", h=2), AX.X,
                                ALU.max, negate=True).then_inc(mx_ready, 1)
                if n >= 1:
                    normalise(n - 1)
            normalise(7)
            for n in range(11, 15):
                rest_of_unit(v, n)
            filter_product("fb", 1)
            for j in range(4):
                v.wait_ge(y_hi, j + 1)
                drains(v.tensor_tensor(ylo[:, j, :], ps[:, BANK[f"pv{j}"], 0:T], yhi[:, j, :].bitcast(F32), ALU.subtract), f"pv{j}")
            for n in range(15, 18):
                rest_of_unit(v, n)
            def rest_of_hyena(i):
                v.wait_ge(x2_hi, i + 1)
                v.tensor_tensor(x2lo[:, i, :], x2z[i], x2hi[:, i, :].bitcast(F32), ALU.subtract).then_inc(x2_lo, 1)

            for i in range(4):
                g = f"ib{i}"
                wait_filled(v, g)
                drains(v.tensor_tensor(x2z[i], ps[:, BANK[g], 0:T], x2z[i], ALU.mult), g)
                if i:
                    rest_of_hyena(i - 1)
            rest_of_hyena(3)
            rest_of_unit(v, 18)
            for i in range(4):
                g = f"uh{i}"
                wait_filled(v, g)
                wait_drained(v, f"gh{i}")
                drains(v.tensor_tensor(mT[:, 2 * i:2 * i + 2, :], ps[:, BANK[g], :].rearrange("p (m t) -> p m t", m=2),
                                       ghy[:, 2 * i:2 * i + 2, :], ALU.mult), g)
                if i % 2:
                    rest_of_unit(v, 19 + i // 2)
            def rest_of_merged(i):
                v.wait_ge(m_hi, i + 1)
                sl = slice(2 * i, 2 * i + 2)
                v.tensor_tensor(mlo[:, sl, :], mT[:, sl, :], mhi[:, sl, :].bitcast(F32), ALU.subtract).then_inc(m_lo, 1)

            for i in range(4):
                g = f"ua{i}"
                sl = slice(2 * i, 2 * i + 2)
                wait_filled(v, g)
                wait_drained(v, f"ga{i}")
                wait_drained(v, f"uh{i}")
                link(v.tensor_tensor(gat[:, sl, :], ps[:, BANK[g], :].rearrange("p (m t) -> p m t", m=2), gat[:, sl, :], ALU.mult))
                drains(v.tensor_tensor(mT[:, sl, :], mT[:, sl, :], gat[:, sl, :], ALU.add), g)
                if i == 1:
                    rest_of_merged(0)
                    rest_of_unit(v, UNIT["wo0"])
            rest_of_merged(1)
            rest_of_unit(v, UNIT["wo1"])
            rest_of_merged(2)
            rest_of_merged(3)
            rest_of_unit(v, UNIT["wo2"])
            rest_of_unit(v, UNIT["wo3"])
            for t in range(2):
                for w in range(2):
                    g = f"wo{t}{w}"
                    part = xh[:, t, w * 512:(w + 1) * 512]
                    wait_filled(v, g)
                    drains(v.tensor_tensor(part, ps[:, BANK[g], :], part, ALU.add), g)
            v.wait_ge(h_ss, 4)
            link(v.tensor_tensor(stat[:, 52:54], stat[:, 48:52:2], stat[:, 49:53:2], ALU.add))
            v.tensor_scalar(stat[:, 52:54], stat[:, 52:54], 1.0 / D, EPS, ALU.mult, ALU.add).then_inc(h_var, 1)
            v.wait_ge(h_std, 1)
            link(v.reciprocal(stat[:, 56:58], stat[:, 54:56]))
            v.wait_ge(in_name["g2b"], 16)
            for t in range(2):
                v.scalar_tensor_tensor(hn[:, t, :], xh[:, t, :], stat[:, 56 + t:57 + t], g2b, ALU.mult, ALU.mult).then_inc(hn_ready, 1)
            for t in range(2):
                wait_filled(v, f"th{t}1")
                drains(v.tensor_copy(hnT[:, 4:8, t * P:(t + 1) * P], ps[:, BANK[f"th{t}1"], :].rearrange("p (k t) -> p k t", k=4)), f"th{t}1")
            for t in range(2):
                take_parts(v, t)
            wait_filled(v, "lt")
            logit = ps[:, BANK["lt"], 0:2 * NE].rearrange("p (t e) -> p t e", t=2)
            for t in range(2):
                ins = v.max(top8[:, t, :], logit[:, t, :])
            link(ins)
            for t in range(2):
                ins = v.max_index(idx8[:, t, :], top8[:, t, :], logit[:, t, :])
            link(ins)
            drains(v.tensor_tensor(gate[:], logit, top8[:, :, 0:1].to_broadcast([P, TT, NE]), ALU.subtract), "lt")
            link(v.tensor_copy(idxf[:], idx8[:]))
            for t in range(2):
                ins = v.tensor_tensor(hot[:, t], tab[:, C_IOE:C_IOE + NE].unsqueeze(1).to_broadcast([P, TOPK, NE]),
                                      idxf[:, t, 0:TOPK].unsqueeze(2).to_broadcast([P, TOPK, NE]), ALU.is_equal)
            link(ins)
            link(v.tensor_reduce(maskf, hot.rearrange("p t r e -> p t e r"), AX.X, ALU.add))
            v.tensor_copy(mask3[:].rearrange("p t (c e) -> p t c e", c=3), maskf.unsqueeze(2).to_broadcast([P, TT, 3, NE]))\
                .then_inc(mask_ready, 1)
            wait_filled(v, "rk")
            rk = ps[:, BANK["rk"], :]
            link(v.scalar_tensor_tensor(rankm[:, :, 0:NE], rk[:, 0:2 * NE].rearrange("p (t e) -> p t e", t=2), 1.0, maskf, ALU.add, ALU.mult))

            def overflow_list():
                v.tensor_scalar(overf[0:96, :], rk[0:96, 64:65], tab[0:96, C_BASE:C_BASE + 1], None, ALU.is_gt)\
                    .then_inc(drained[BANK["rk"]], 1)
                wait_drained(v, "rk")
                v.tensor_copy(over[0:96, :], overf[0:96, :]).then_inc(over_ready, 1)
                wait_filled(v, "lp")
                drains(v.tensor_copy(pos[0:96, :], ps[0:96, BANK["lp"], 0:1]), "lp")
                wait_drained(v, "lp")
                v.tensor_scalar(onehot[0:96, :], tab[0:96, C_IOL:C_IOL + NLIST], pos[0:96, :], overf[0:96, :],
                                ALU.is_equal, ALU.mult).then_inc(pos_ready, 1)
                wait_filled(v, "ls")
                drains(v.tensor_copy(olist[0:1, 0:2 * NLIST + 1], ps[0:1, BANK["ls"], 0:2 * NLIST + 1]), "ls")
                wait_drained(v, "ls")
                v.memset(mark[:, 3:4], 0.0).then_inc(list_ready, 1)

            iota = tab[:, C_IOTA:C_IOTA + T]
            iota0 = iota[:, 0:SLOTS]

            def select(e, block, first=iota0):
                for t in range(2):
                    ins = v.tensor_scalar(sel[:, t, block * SLOTS:(block + 1) * SLOTS], first, rankm[:, t, ds(e, 1)], None, ALU.is_equal)
                return ins

            def select_gates(e, block, first=iota0):
                for t in range(2):
                    ins = v.tensor_scalar(selG[:, t, block * SLOTS:(block + 1) * SLOTS], first, rankm[:, t, ds(e, 1)],
                                          gate[:, t, ds(e, 1)], ALU.is_equal, ALU.mult)
                return ins

            def select_bias(pos_, e):
                v.tensor_scalar(selB[:, pos_, :], ones[:, 0:SLOTS], tab[:, ds(e + C_ID4, 1)], None, ALU.mult).then_inc(selb_ready, 1)

            def swiglu(count):
                v.wait_ge(h_full, count)
                hid = ps[:, 4:6, :]
                v.tensor_scalar(glu, hid[:, :, 0::2], LIMIT, None, ALU.min).then_inc(glu_ready, 1)
                v.tensor_scalar(lin, hid[:, :, 1::2], LIMIT, -LIMIT, ALU.min, ALU.max).then_inc(h_used, 1)
                v.wait_ge(glu_ready, count)
                v.wait_ge(h_used, count + 1)
                v.scalar_tensor_tensor(lin, lin, 1.0, glu, ALU.add, ALU.mult).then_inc(mid_ready, 1)
                v.wait_ge(mid_ready, count)
                v.wait_ge(sig_ready, count)
                v.tensor_tensor(hact, lin, sig, ALU.mult).then_inc(hact_ready, 1)

            def take_y(odd, count, combined):
                v.wait_ge(comb, combined)
                v.wait_ge(y_full, count)
                v.tensor_copy(yab[0:64, odd, :], ps[0:64, 6, :])
                v.tensor_copy(yab[64:P, 1 - odd, :], ps[64:P, 6, :]).then_inc(y_used, 1)

            select(0, 0)
            select(1, 1).then_inc(sel_ready, 1)
            v.memset(mark[:, 0:1], 0.0).then_inc(t_free, 1)
            v.memset(mark[:, 1:2], 0.0).then_inc(h_used, 1)
            v.memset(mark[:, 2:3], 0.0).then_inc(y_used, 1)
            select_bias(0, 0)
            overflow_list()
            v.wait_ge(r_exp, 1)
            link(v.tensor_tensor(gate[:], gate[:], maskf, ALU.mult))
            link(v.tensor_reduce(smax[:, 50:52], gate[:], AX.X, ALU.add))
            link(v.reciprocal(smax[:, 52:54], smax[:, 50:52]))
            v.tensor_tensor(gate[:], gate[:], smax[:, 52:54].unsqueeze(2).to_broadcast([P, TT, NE]), ALU.mult).then_inc(gate_ready, 1)
            v.wait_ge(gate_ready, 1)
            with v.Fori(0, TURNS) as it:
                e = it * GROUP
                v.wait_ge(t_full, it * 10 + 2)
                select(e + 2, 0)
                select(e + 3, 1).then_inc(sel_ready, 1)
                select_gates(e, 0)
                select_gates(e + 1, 1)
                select_gates(e, 2).then_inc(selg_ready, 1)
                for j in range(GROUP):
                    select_bias((j + 1) % 2, e + (j + 1))
                    swiglu(e + (j + 1))
                    take_y(j % 2, e + (j + 1), it * 2 + (j // 2 + 1))
                    if j == 1:
                        select(e + 4, 0)
                        select(e + 5, 1).then_inc(sel_ready, 1)
                        select_gates(e + 2, 0)
                        select_gates(e + 3, 1)
                        select_gates(e + 2, 2).then_inc(selg_ready, 1)
            n_over = v.value_load(olist[0:1, 2 * NLIST:2 * NLIST + 1], min_val=0, max_val=NLIST)
            with v.If(n_over > 0):
                with v.Fori(0, n_over) as i:
                    e = v.value_load(olist[0:1, ds(i, 1)], min_val=0, max_val=NE - 1)
                    base = v.value_load(olist[0:1, ds(i + NLIST, 1)], min_val=0, max_val=T - SLOTS)
                    v.wait_ge(comb, i + (NE // 2 + 1))
                    window = iota[:, ds(base, SLOTS)]
                    select(e, 0, window).then_inc(sel_ready, 1)
                    select_gates(e, 0, window)
                    select_gates(e, 2, window).then_inc(selg_ready, 1)
                    select_bias(0, e)
                    swiglu(i + (NE + 1))
                    take_y(0, i + (NE + 1), i + (NE // 2 + 1))
            for t in range(2):
                for w in range(2):
                    if t and w:
                        v.wait_ge(comb, n_over + (NE // 2 + 1))
                    else:
                        v.wait_ge(added, n_over * 3 + (3 * (NE // 2 - 1) + 2 * t + w + 1))
                    part = xh[:, t, w * 512:(w + 1) * 512]
                    v.tensor_tensor(part, ps[:, 2 * t + w, :], part, ALU.add).then_inc(out_ready, 1)

        @block.gpsimd
        def _(pool):
            def link(ins, n):
                ins.then_inc(pool_step, 1)
                pool.wait_ge(pool_step, n)

            count = [0]

            def step(ins):
                count[0] += 1
                link(ins, count[0])

            def split(out_, raw, done):
                step(pool.memset(out_[96:P, :], 0.0))
                step(pool.tensor_copy(out_[0:96, :], raw))
                step(pool.tensor_tensor(raw, raw, out_[0:96, :], ALU.subtract))
                step(pool.tensor_copy(out_[32:64, :], raw[32:64, :]))
                step(pool.tensor_copy(out_[64:96, :], raw[64:96, :]))
                pool.tensor_tensor(out_[64:96, :], raw[64:96, :], out_[64:96, :], ALU.subtract).then_inc(done, 1)
                pool.wait_ge(done, 1)

            for t in range(2):
                pool.wait_ge(abs_ready, t + 1)
                for o in range(2):
                    f, b = hk[:, t, o, 0, :], hk[:, t, o, 1, :]
                    pool.tensor_tensor(fsum[:, t, o, :], f, b, ALU.add).then_inc(pm_ready, 1)
                    pool.wait_ge(pm_ready, 4 * t + 2 * o + 1)
                    pool.tensor_tensor(b, f, b, ALU.subtract).then_inc(pm_ready, 1)
                    pool.wait_ge(pm_ready, 4 * t + 2 * o + 2)
            for n in (5, 6, 7, 8):
                rest_of_unit(pool, n)
                pool.wait_ge(unit_lo[n % 2], n // 2 + 1)
            pool.wait_ge(in_name["b1"], 48)
            split(b1p, b1raw, b1_ready)
            pool.wait_ge(in_name["b2"], 48)
            split(b2p, b2raw, b2_ready)
            third_part(pool, 0)
            third_part(pool, 1)


_INS = ["x", "norm1_g", "w_in", "conv_w", "conv_b", "filt_w1", "filt_b1", "filt_freq1", "filt_w2",
        "filt_b2", "filt_freq2", "filt_w3", "filt_b3", "hyena_d", "q_norm_g", "k_norm_g",
        "w_hyena_up", "w_attn_up", "w_out", "norm2_g", "router_w", "router_b", "expert_w1",
        "expert_b1", "expert_w2", "expert_b2"]


def kernel(**inputs):
    import numpy as _np
    import concourse.bacc as _bacc
    from concourse import mybir as _mybir
    from concourse.bass_utils import run_bass_kernel_spmd as _run

    nc = _bacc.Bacc("TRN2", target_bir_lowering=False, num_devices=1)
    arrays, args = {}, []
    named = [(n, inputs[n]) for n in _INS]
    named += list(zip(("c_tab", "c_dft", "c_decay"), tables()))
    for name, value in named:
        a = _np.ascontiguousarray(value)
        arrays[f"in_{name}"] = a
        args.append(nc.dram_tensor(f"in_{name}", a.shape, _mybir.dt.from_np(a.dtype), kind="ExternalInput").ap())
    out = nc.dram_tensor("out_0", (1, T, D), F32, kind="ExternalOutput").ap()
    hybrid_block(nc, *args, out)
    r = _run(nc, [arrays], core_ids=[0])
    return r.results[0]["out_0"]
```
